# Optimizing a Trainium2 kernel written in Bass

```python
import math
import jax, jax.numpy as jnp
from jax import lax
import numpy as np

D_MODEL = 1024
BATCH = 1
SEQ = 256
DEPTH = 1

MEM_LEN = 256
D_MIX = D_MODEL
D_RWKV = D_MIX // 2
D_CONV = D_MIX - D_RWKV
RWKV_HEAD = 64
RWKV_HEADS = D_RWKV // RWKV_HEAD
CONV_WIDTH = 31
DECAY_LORA = 64
AAA_LORA = 64
MV_LORA = 32
GATE_LORA = 128
XA_HEADS = 4
XA_HEAD_DIM = D_MODEL // XA_HEADS
D_FF = -(-8 * D_MODEL // (3 * 256)) * 256
RMS_EPS = 1e-6
LN_EPS = 1e-5
GN_EPS = 64e-5
DECAY_SCALE = math.exp(-0.5)

N_RWKV_COLS = 3 * D_RWKV + DECAY_LORA + AAA_LORA + GATE_LORA
N_IN_FIRST = 2 * D_CONV + N_RWKV_COLS
N_IN_REST = N_IN_FIRST + MV_LORA


def rms_norm(x, g):
    xf = x.astype(jnp.float32)
    y = xf * lax.rsqrt(jnp.mean(xf * xf, axis=-1, keepdims=True) + RMS_EPS)
    return (y * g.astype(jnp.float32)).astype(x.dtype)

def layer_norm(x, g, b):
    xf = x.astype(jnp.float32)
    mean = jnp.mean(xf, axis=-1, keepdims=True)
    var = jnp.mean(jnp.square(xf - mean), axis=-1, keepdims=True)
    y = (xf - mean) * lax.rsqrt(var + LN_EPS)
    return (y * g.astype(jnp.float32) + b.astype(jnp.float32)).astype(x.dtype)

def token_shift_mix(p, mu):
    prev = jnp.pad(p, ((0, 0), (1, 0), (0, 0)))[:, :-1]
    return p + mu * (prev - p)

def conformer_conv(u, conv_w, conv_b, ln_g, ln_b):
    h = u[..., :D_CONV] * jax.nn.sigmoid(u[..., D_CONV:])
    h = lax.conv_general_dilated(
        h, conv_w[:, None, :], window_strides=(1,), padding=[(CONV_WIDTH - 1, 0)],
        dimension_numbers=("NWC", "WIO", "NWC"), feature_group_count=D_CONV) + conv_b
    h = layer_norm(h, ln_g, ln_b)
    return jax.nn.silu(h)

def rwkv7_recurrence(r, w, k, v, kk, a):
    B = r.shape[0]
    tm = lambda z: jnp.moveaxis(z.astype(jnp.float32), 1, 0)

    def step(S, inp):
        r_t, w_t, k_t, v_t, kk_t, a_t = inp
        s_kk = jnp.einsum("bhvk,bhk->bhv", S, kk_t)
        S = (S * w_t[:, :, None, :]
             - s_kk[..., None] * (kk_t * a_t)[:, :, None, :]
             + v_t[..., None] * k_t[:, :, None, :])
        return S, jnp.einsum("bhvk,bhk->bhv", S, r_t)

    S0 = jnp.zeros((B, RWKV_HEADS, RWKV_HEAD, RWKV_HEAD), jnp.float32)
    _, y = lax.scan(step, S0, (tm(r), tm(w), tm(k), tm(v), tm(kk), tm(a)))
    return jnp.moveaxis(y, 0, 1)

def rwkv7_mix(p, mu, w0, w_up, a0, a_up, g_up, k_k, k_a, r_k, lnx_g, lnx_b, v_first, v0, v_up):
    B, T = p.shape[:2]
    p = token_shift_mix(p, mu)
    o = 0
    r = p[..., o:o + D_RWKV]; o += D_RWKV
    k = p[..., o:o + D_RWKV]; o += D_RWKV
    v = p[..., o:o + D_RWKV]; o += D_RWKV
    w_lo = p[..., o:o + DECAY_LORA]; o += DECAY_LORA
    a_lo = p[..., o:o + AAA_LORA]; o += AAA_LORA
    g_lo = p[..., o:o + GATE_LORA]; o += GATE_LORA

    log_w = -DECAY_SCALE * jax.nn.sigmoid((w0 + jnp.tanh(w_lo) @ w_up).astype(jnp.float32))
    w = jnp.exp(log_w)
    a = jax.nn.sigmoid(a0 + a_lo @ a_up)
    g = jax.nn.sigmoid(g_lo) @ g_up
    if v_first is None:
        v_first = v
    else:
        vres_lo = p[..., o:o + MV_LORA]
        v = v + (v_first - v) * jax.nn.sigmoid(v0 + vres_lo @ v_up)

    hd = lambda z: z.reshape(B, T, RWKV_HEADS, RWKV_HEAD)
    kk = hd(k * k_k).astype(jnp.float32)
    kk = kk * lax.rsqrt(jnp.maximum(jnp.sum(kk * kk, axis=-1, keepdims=True), 1e-24))
    k = k * (1.0 + (a - 1.0) * k_a)
    rh, kh, vh = hd(r), hd(k), hd(v)

    y = rwkv7_recurrence(rh, hd(w), kh, vh, kk, hd(a))
    mean = jnp.mean(y, axis=-1, keepdims=True)
    var = jnp.mean(jnp.square(y - mean), axis=-1, keepdims=True)
    y = (y - mean) * lax.rsqrt(var + GN_EPS)
    gn_g = lnx_g.reshape(RWKV_HEADS, RWKV_HEAD).astype(jnp.float32)
    gn_b = lnx_b.reshape(RWKV_HEADS, RWKV_HEAD).astype(jnp.float32)
    y = y * gn_g + gn_b
    bonus = jnp.sum((rh * kh * r_k).astype(jnp.float32), axis=-1, keepdims=True) * vh.astype(jnp.float32)
    y = (y + bonus).astype(p.dtype).reshape(B, T, D_RWKV) * g
    return y, v_first

def memory_cross_attention(h, mem_n, wq, wkv, wo):
    B, T, _ = h.shape
    M = mem_n.shape[1]
    q = (h @ wq).reshape(B, T, XA_HEADS, XA_HEAD_DIM)
    kv = mem_n @ wkv
    km = kv[..., :D_MODEL].reshape(B, M, XA_HEADS, XA_HEAD_DIM)
    vm = kv[..., D_MODEL:].reshape(B, M, XA_HEADS, XA_HEAD_DIM)
    s = jnp.einsum("bthd,bmhd->bhtm", q, km).astype(jnp.float32) * (XA_HEAD_DIM ** -0.5)
    pr = jax.nn.softmax(s, axis=-1).astype(vm.dtype)
    o = jnp.einsum("bhtm,bmhd->bthd", pr, vm).reshape(B, T, D_MODEL)
    return o @ wo

def swiglu(h, w_gu, w_down):
    gu = h @ w_gu
    return (jax.nn.silu(gu[..., :D_FF]) * gu[..., D_FF:]) @ w_down

def first_inputs(seed: int = 0) -> dict:
    key = jax.random.key(seed)
    ks = iter(jax.random.split(key, 40))
    nrm = lambda shape, s: jax.random.normal(next(ks), shape, jnp.float32) * s
    uni = lambda shape: jax.random.uniform(next(ks), shape, jnp.float32)
    L, Lr = DEPTH, DEPTH - 1
    return {
        "x": nrm((BATCH, SEQ, D_MODEL), 1.0),
        "mem": nrm((BATCH, MEM_LEN, D_MODEL), 1.0),
        "mem_norm_g": 1.0 + nrm((D_MODEL,), 0.05),
        "norm_gains": 1.0 + nrm((L, 6, D_MODEL), 0.05),
        "w_in_first": nrm((D_MODEL, N_IN_FIRST), D_MODEL ** -0.5),
        "w_in_rest": nrm((Lr, D_MODEL, N_IN_REST), D_MODEL ** -0.5),
        "mu_first": uni((N_RWKV_COLS,)),
        "mu_rest": uni((Lr, N_RWKV_COLS + MV_LORA)),
        "conv_w": nrm((L, CONV_WIDTH, D_CONV), CONV_WIDTH ** -0.5),
        "conv_b": nrm((L, D_CONV), 0.02),
        "conv_ln_g": 1.0 + nrm((L, D_CONV), 0.05),
        "conv_ln_b": nrm((L, D_CONV), 0.02),
        "w0": nrm((L, D_RWKV), 1.0),
        "w_up": nrm((L, DECAY_LORA, D_RWKV), DECAY_LORA ** -0.5),
        "a0": nrm((L, D_RWKV), 0.1),
        "a_up": nrm((L, AAA_LORA, D_RWKV), AAA_LORA ** -0.5),
        "g_up": nrm((L, GATE_LORA, D_RWKV), GATE_LORA ** -0.5),
        "v0": nrm((Lr, D_RWKV), 0.1),
        "v_up": nrm((Lr, MV_LORA, D_RWKV), MV_LORA ** -0.5),
        "k_k": 0.85 + nrm((L, D_RWKV), 0.05),
        "k_a": 1.0 + nrm((L, D_RWKV), 0.05),
        "r_k": nrm((L, RWKV_HEADS, RWKV_HEAD), 0.1),
        "lnx_g": 1.0 + nrm((L, D_RWKV), 0.05),
        "lnx_b": nrm((L, D_RWKV), 0.02),
        "w_out": nrm((L, D_MIX, D_MODEL), D_MIX ** -0.5),
        "wq": nrm((L, D_MODEL, D_MODEL), D_MODEL ** -0.5),
        "wkv": nrm((L, D_MODEL, 2 * D_MODEL), D_MODEL ** -0.5),
        "wo": nrm((L, D_MODEL, D_MODEL), D_MODEL ** -0.5),
        "w_gu": nrm((L, D_MODEL, 2 * D_FF), D_MODEL ** -0.5),
        "w_down": nrm((L, D_FF, D_MODEL), D_FF ** -0.5),
    }

def first_block(x, mem, mem_norm_g, norm_gains, w_in_first, w_in_rest, mu_first, mu_rest,
              conv_w, conv_b, conv_ln_g, conv_ln_b, w0, w_up, a0, a_up, g_up, v0, v_up,
              k_k, k_a, r_k, lnx_g, lnx_b, w_out, wq, wkv, wo, w_gu, w_down):
    mem_n = rms_norm(mem, mem_norm_g)
    v_first = None
    for i in range(DEPTH):
        g = norm_gains[i]
        h = rms_norm(x, g[0])
        if i == 0:
            p = h @ w_in_first
            mu, vr0, vr_up = mu_first, None, None
        else:
            p = h @ w_in_rest[i - 1]
            mu, vr0, vr_up = mu_rest[i - 1], v0[i - 1], v_up[i - 1]
        y_conv = conformer_conv(p[..., :2 * D_CONV], conv_w[i], conv_b[i], conv_ln_g[i], conv_ln_b[i])
        y_rwkv, v_first = rwkv7_mix(p[..., 2 * D_CONV:], mu, w0[i], w_up[i], a0[i], a_up[i], g_up[i],
                                    k_k[i], k_a[i], r_k[i], lnx_g[i], lnx_b[i], v_first, vr0, vr_up)
        y = jnp.concatenate([y_conv, y_rwkv], axis=-1) @ w_out[i]
        x = x + rms_norm(y, g[1])
        y = memory_cross_attention(rms_norm(x, g[2]), mem_n, wq[i], wkv[i], wo[i])
        x = x + rms_norm(y, g[3])
        y = swiglu(rms_norm(x, g[4]), w_gu[i], w_down[i])
        x = x + rms_norm(y, g[5])
    return x


DEPTH_2 = 2

N_MIXERS = 2
N_A_LAYERS = (DEPTH_2 + N_MIXERS - 1) // N_MIXERS
N_B_LAYERS = DEPTH_2 // N_MIXERS

ATTN_HEAD_DIM = 128
ATTN_HEADS = D_MODEL // ATTN_HEAD_DIM
MOBA_BLOCK = 256
MOBA_TOPK = 3
Q_CHUNK = 128
ROPE_THETA = 10000.0

SSM_EXPAND = 2
SSM_D_INNER = SSM_EXPAND * D_MODEL
SSM_HEAD_DIM = 64
SSM_HEADS = SSM_D_INNER // SSM_HEAD_DIM
SSM_GROUPS = 8
SSM_HEADS_PER_GROUP = SSM_HEADS // SSM_GROUPS
SSM_STATE = 128
SSM_CONV = 4
SSM_CHUNK = 128
SSM_CONV_DIM = SSM_D_INNER + 2 * SSM_GROUPS * SSM_STATE
SSM_IN_DIM = SSM_D_INNER + SSM_CONV_DIM + SSM_HEADS

D_FF_2 = 2816
EPS = 1e-6


def rms_norm_2(x, g):
    xf = x.astype(jnp.float32)
    y = xf * lax.rsqrt(jnp.mean(xf * xf, axis=-1, keepdims=True) + EPS)
    return (y * g.astype(jnp.float32)).astype(x.dtype)

def swiglu_2(x, w_gate, w_up, w_down):
    return (jax.nn.silu(x @ w_gate) * (x @ w_up)) @ w_down

def rope(x, positions):
    half = x.shape[-1] // 2
    inv_freq = ROPE_THETA ** (-jnp.arange(half, dtype=jnp.float32) / half)
    ang = positions.astype(jnp.float32)[..., None] * inv_freq
    cos = jnp.cos(ang)[:, :, None, :]
    sin = jnp.sin(ang)[:, :, None, :]
    xf = x.astype(jnp.float32)
    x1, x2 = xf[..., :half], xf[..., half:]
    out = jnp.concatenate([x1 * cos - x2 * sin, x2 * cos + x1 * sin], axis=-1)
    return out.astype(x.dtype)

def moba_mixer(h, positions, w_qkv, q_gain, k_gain, w_o):
    bsz, seq, _ = h.shape
    H, Dh, BS = ATTN_HEADS, ATTN_HEAD_DIM, MOBA_BLOCK
    qkv = (h @ w_qkv).reshape(bsz, seq, 3, H, Dh)
    q = rope(rms_norm_2(qkv[:, :, 0], q_gain), positions)
    k = rope(rms_norm_2(qkv[:, :, 1], k_gain), positions)
    v = qkv[:, :, 2]
    q = jnp.swapaxes(q, 1, 2)
    k = jnp.swapaxes(k, 1, 2)
    v = jnp.swapaxes(v, 1, 2)
    n_blk = -(-seq // BS)
    pad = n_blk * BS - seq
    k = jnp.pad(k, ((0, 0), (0, 0), (0, pad), (0, 0)))
    v = jnp.pad(v, ((0, 0), (0, 0), (0, pad), (0, 0)))
    kb = k.reshape(bsz, H, n_blk, BS, Dh)
    vb = v.reshape(bsz, H, n_blk, BS, Dh)
    n_sel = min(MOBA_TOPK, n_blk - 1)
    q_blk = jnp.arange(seq) // BS
    scale = Dh ** -0.5

    if n_sel > 0:
        k_mean = jnp.mean(kb.astype(jnp.float32), axis=3)
        gate = jnp.einsum('bhtd,bhnd->bhtn', q.astype(jnp.float32), k_mean)
        past = jnp.arange(n_blk)[None, :] < q_blk[:, None]
        gate = jnp.where(past, gate, -jnp.inf)
        _, sel_idx = lax.top_k(gate, n_sel)
        sel_valid = sel_idx < q_blk[:, None]

    n_qc = seq // Q_CHUNK
    head_ix = jnp.arange(H)[:, None, None]

    def one_chunk(s):
        b = s // n_qc
        t0 = (s % n_qc) * Q_CHUNK
        qc = lax.dynamic_slice_in_dim(lax.dynamic_index_in_dim(q, b, 0, False), t0, Q_CHUNK, 1)
        kb_b = lax.dynamic_index_in_dim(kb, b, 0, False)
        vb_b = lax.dynamic_index_in_dim(vb, b, 0, False)
        own = t0 // BS
        k_own = lax.dynamic_index_in_dim(kb_b, own, 1, False)
        v_own = lax.dynamic_index_in_dim(vb_b, own, 1, False)
        q_pos = t0 + jnp.arange(Q_CHUNK)
        k_pos = own * BS + jnp.arange(BS)
        s_own = jnp.einsum('hqd,hkd->hqk', qc, k_own).astype(jnp.float32) * scale
        s_own = jnp.where(k_pos[None, :] <= q_pos[:, None], s_own, -jnp.inf)
        if n_sel == 0:
            p = jax.nn.softmax(s_own, axis=-1).astype(v_own.dtype)
            return jnp.einsum('hqk,hkd->hqd', p, v_own)
        idx = lax.dynamic_slice_in_dim(lax.dynamic_index_in_dim(sel_idx, b, 0, False), t0, Q_CHUNK, 1)
        valid = lax.dynamic_slice_in_dim(lax.dynamic_index_in_dim(sel_valid, b, 0, False), t0, Q_CHUNK, 1)
        k_sel = kb_b[head_ix, idx]
        v_sel = vb_b[head_ix, idx]
        s_sel = jnp.einsum('hqd,hqjkd->hqjk', qc, k_sel).astype(jnp.float32) * scale
        s_sel = jnp.where(valid[..., None], s_sel, -jnp.inf).reshape(H, Q_CHUNK, n_sel * BS)
        p = jax.nn.softmax(jnp.concatenate([s_sel, s_own], axis=-1), axis=-1).astype(v_own.dtype)
        p_sel = p[..., :n_sel * BS].reshape(H, Q_CHUNK, n_sel, BS)
        p_own = p[..., n_sel * BS:]
        return (jnp.einsum('hqjk,hqjkd->hqd', p_sel, v_sel)
                + jnp.einsum('hqk,hkd->hqd', p_own, v_own))

    o = lax.map(one_chunk, jnp.arange(bsz * n_qc))
    o = o.reshape(bsz, n_qc, H, Q_CHUNK, Dh).transpose(0, 1, 3, 2, 4).reshape(bsz, seq, H * Dh)
    return o @ w_o

def ssd_chunked(xdt, a_dt, bm, cm):
    bsz, seq = xdt.shape[:2]
    G, R, P, N, CH = SSM_GROUPS, SSM_HEADS_PER_GROUP, SSM_HEAD_DIM, SSM_STATE, SSM_CHUNK
    nc = seq // CH
    x = xdt.reshape(bsz, nc, CH, G, R, P)
    a = a_dt.reshape(bsz, nc, CH, G, R).transpose(0, 3, 4, 1, 2)
    bc = bm.reshape(bsz, nc, CH, G, N)
    cc = cm.reshape(bsz, nc, CH, G, N)
    a_cs = jnp.cumsum(a, axis=-1)
    tril = jnp.tril(jnp.ones((CH, CH), dtype=bool))
    seg = a_cs[..., :, None] - a_cs[..., None, :]
    L = jnp.exp(jnp.where(tril, seg, -jnp.inf))
    cb = jnp.einsum('bclgn,bcsgn->bgcls', cc, bc)
    y_diag = jnp.einsum('bgrcls,bcsgrp->bclgrp', cb[:, :, None] * L, x)
    decay = jnp.exp(a_cs[..., -1:] - a_cs)
    states = jnp.einsum('bclgn,bgrcl,bclgrp->bcgrpn', bc, decay, x)
    chunk_decay = jnp.exp(a_cs[..., -1])

    def step(hs, inp):
        st, dec = inp
        return hs * dec[..., None, None] + st, hs

    h0 = jnp.zeros((bsz, G, R, P, N), dtype=jnp.float32)
    _, prev = lax.scan(step, h0, (jnp.moveaxis(states, 1, 0), jnp.moveaxis(chunk_decay, -1, 0)))
    prev = jnp.moveaxis(prev, 0, 1)
    y_off = jnp.einsum('bclgn,bcgrpn,bgrcl->bclgrp', cc, prev, jnp.exp(a_cs))
    return (y_diag + y_off).reshape(bsz, seq, G * R, P)

def mamba2_mixer(h, w_in, conv_w, conv_b, dt_bias, a_log, d_skip, norm_g, w_out):
    bsz, seq, _ = h.shape
    DI, G, N, H, P = SSM_D_INNER, SSM_GROUPS, SSM_STATE, SSM_HEADS, SSM_HEAD_DIM
    proj = h @ w_in
    z = proj[..., :DI]
    xbc = proj[..., DI:DI + SSM_CONV_DIM]
    dt = proj[..., DI + SSM_CONV_DIM:]
    xbc = lax.conv_general_dilated(xbc, conv_w[:, None, :], window_strides=(1,),
                                   padding=[(SSM_CONV - 1, 0)],
                                   dimension_numbers=('NWC', 'WIO', 'NWC'),
                                   feature_group_count=SSM_CONV_DIM)
    xbc = jax.nn.silu(xbc + conv_b)
    xs = xbc[..., :DI].reshape(bsz, seq, H, P).astype(jnp.float32)
    bm = xbc[..., DI:DI + G * N].reshape(bsz, seq, G, N).astype(jnp.float32)
    cm = xbc[..., DI + G * N:].reshape(bsz, seq, G, N).astype(jnp.float32)
    dt = jax.nn.softplus(dt.astype(jnp.float32) + dt_bias.astype(jnp.float32))
    a = -jnp.exp(a_log.astype(jnp.float32))
    y = ssd_chunked(xs * dt[..., None], dt * a, bm, cm)
    y = y + d_skip.astype(jnp.float32)[:, None] * xs
    y = y.reshape(bsz, seq, DI) * jax.nn.silu(z.astype(jnp.float32))
    yg = y.reshape(bsz, seq, G, DI // G)
    yg = yg * lax.rsqrt(jnp.mean(yg * yg, axis=-1, keepdims=True) + EPS)
    y = yg.reshape(bsz, seq, DI) * norm_g.astype(jnp.float32)
    return y.astype(h.dtype) @ w_out

def second_inputs(seed: int = 0) -> dict:
    key = jax.random.key(seed)
    ks = jax.random.split(key, 26)
    f32 = jnp.float32

    def nrm(k, shape, fan_in):
        return jax.random.normal(k, shape, f32) * (fan_in ** -0.5)

    def gain(k, shape):
        return 1.0 + 0.05 * jax.random.normal(k, shape, f32)

    dt_init = jnp.exp(jax.random.uniform(ks[20], (N_B_LAYERS, SSM_HEADS), f32)
                      * (math.log(0.1) - math.log(0.001)) + math.log(0.001))
    dt_init = jnp.maximum(dt_init, 1e-4)
    return {
        "x": jax.random.normal(ks[0], (BATCH, SEQ, D_MODEL), f32),
        "positions": jnp.broadcast_to(jnp.arange(SEQ, dtype=jnp.int32), (BATCH, SEQ)),
        "ffn1_norm": gain(ks[1], (DEPTH_2, D_MODEL)),
        "ffn1_w_gate": nrm(ks[2], (DEPTH_2, D_MODEL, D_FF_2), D_MODEL),
        "ffn1_w_up": nrm(ks[3], (DEPTH_2, D_MODEL, D_FF_2), D_MODEL),
        "ffn1_w_down": nrm(ks[4], (DEPTH_2, D_FF_2, D_MODEL), D_FF_2),
        "mix_norm": gain(ks[5], (DEPTH_2, D_MODEL)),
        "ffn2_norm": gain(ks[6], (DEPTH_2, D_MODEL)),
        "ffn2_w_gate": nrm(ks[7], (DEPTH_2, D_MODEL, D_FF_2), D_MODEL),
        "ffn2_w_up": nrm(ks[8], (DEPTH_2, D_MODEL, D_FF_2), D_MODEL),
        "ffn2_w_down": nrm(ks[9], (DEPTH_2, D_FF_2, D_MODEL), D_FF_2),
        "attn_w_qkv": nrm(ks[10], (N_A_LAYERS, D_MODEL, 3 * D_MODEL), D_MODEL),
        "attn_q_norm": gain(ks[11], (N_A_LAYERS, ATTN_HEAD_DIM)),
        "attn_k_norm": gain(ks[12], (N_A_LAYERS, ATTN_HEAD_DIM)),
        "attn_w_o": nrm(ks[13], (N_A_LAYERS, D_MODEL, D_MODEL), D_MODEL),
        "ssm_w_in": nrm(ks[14], (N_B_LAYERS, D_MODEL, SSM_IN_DIM), D_MODEL),
        "ssm_conv_w": nrm(ks[15], (N_B_LAYERS, SSM_CONV, SSM_CONV_DIM), SSM_CONV),
        "ssm_conv_b": 0.02 * jax.random.normal(ks[16], (N_B_LAYERS, SSM_CONV_DIM), f32),
        "ssm_dt_bias": dt_init + jnp.log(-jnp.expm1(-dt_init)),
        "ssm_a_log": jnp.log(jax.random.uniform(ks[17], (N_B_LAYERS, SSM_HEADS), f32, 1.0, 16.0)),
        "ssm_d": 1.0 + 0.1 * jax.random.normal(ks[18], (N_B_LAYERS, SSM_HEADS), f32),
        "ssm_norm": gain(ks[19], (N_B_LAYERS, SSM_D_INNER)),
        "ssm_w_out": nrm(ks[21], (N_B_LAYERS, SSM_D_INNER, D_MODEL), SSM_D_INNER),
    }

def second_block(x, positions, ffn1_norm, ffn1_w_gate, ffn1_w_up, ffn1_w_down, mix_norm,
              ffn2_norm, ffn2_w_gate, ffn2_w_up, ffn2_w_down,
              attn_w_qkv, attn_q_norm, attn_k_norm, attn_w_o,
              ssm_w_in, ssm_conv_w, ssm_conv_b, ssm_dt_bias, ssm_a_log, ssm_d, ssm_norm, ssm_w_out):
    for i in range(DEPTH_2):
        x = x + 0.5 * swiglu_2(rms_norm_2(x, ffn1_norm[i]), ffn1_w_gate[i], ffn1_w_up[i], ffn1_w_down[i])
        h = rms_norm_2(x, mix_norm[i])
        j = i // N_MIXERS
        if i % N_MIXERS == 0:
            x = x + moba_mixer(h, positions, attn_w_qkv[j], attn_q_norm[j], attn_k_norm[j], attn_w_o[j])
        else:
            x = x + mamba2_mixer(h, ssm_w_in[j], ssm_conv_w[j], ssm_conv_b[j], ssm_dt_bias[j],
                                 ssm_a_log[j], ssm_d[j], ssm_norm[j], ssm_w_out[j])
        x = x + 0.5 * swiglu_2(rms_norm_2(x, ffn2_norm[i]), ffn2_w_gate[i], ffn2_w_up[i], ffn2_w_down[i])
    return x


def setup_inputs(seed=0):
    out = dict(first_inputs(seed))
    for name, value in second_inputs(seed + 1).items():
        if name != "x":
            out[name + "_2"] = value
    return out


def reference(
    x, mem, mem_norm_g, norm_gains, w_in_first, w_in_rest, mu_first, mu_rest, conv_w, conv_b,
    conv_ln_g, conv_ln_b, w0, w_up, a0, a_up, g_up, v0, v_up, k_k, k_a, r_k, lnx_g, lnx_b,
    w_out, wq, wkv, wo, w_gu, w_down, positions_2, ffn1_norm_2, ffn1_w_gate_2, ffn1_w_up_2,
    ffn1_w_down_2, mix_norm_2, ffn2_norm_2, ffn2_w_gate_2, ffn2_w_up_2, ffn2_w_down_2,
    attn_w_qkv_2, attn_q_norm_2, attn_k_norm_2, attn_w_o_2, ssm_w_in_2, ssm_conv_w_2,
    ssm_conv_b_2, ssm_dt_bias_2, ssm_a_log_2, ssm_d_2, ssm_norm_2, ssm_w_out_2,
):
    x = first_block(
        x, mem, mem_norm_g, norm_gains, w_in_first, w_in_rest, mu_first, mu_rest, conv_w,
        conv_b, conv_ln_g, conv_ln_b, w0, w_up, a0, a_up, g_up, v0, v_up, k_k, k_a, r_k, lnx_g,
        lnx_b, w_out, wq, wkv, wo, w_gu, w_down,
    )
    return second_block(
        x, positions_2, ffn1_norm_2, ffn1_w_gate_2, ffn1_w_up_2, ffn1_w_down_2, mix_norm_2,
        ffn2_norm_2, ffn2_w_gate_2, ffn2_w_up_2, ffn2_w_down_2, attn_w_qkv_2, attn_q_norm_2,
        attn_k_norm_2, attn_w_o_2, ssm_w_in_2, ssm_conv_w_2, ssm_conv_b_2, ssm_dt_bias_2,
        ssm_a_log_2, ssm_d_2, ssm_norm_2, ssm_w_out_2,
    )


_drawn_inputs = setup_inputs


def setup_inputs(seed=0):
    import zlib

    import numpy as np

    out = dict(_drawn_inputs(seed))
    spreads = {}
    factors = {'conv_ln_b': 3.551,
     'k_k': 7.281,
     'lnx_b': 4.956,
     'ffn1_norm_2': 3.38,
     'ffn2_norm_2': 3.835,
     'attn_q_norm_2': 8.0,
     'attn_k_norm_2': 8.0,
     'ssm_conv_b_2': 4.496,
     'ssm_norm_2': 8.103}
    for name, (base, spread) in spreads.items():
        noise = np.random.default_rng([zlib.crc32(name.encode()), seed]).standard_normal(out[name].shape)
        drawn = base * np.exp(spread * noise) if base else spread * noise
        out[name] = __import__('jax').numpy.asarray(drawn.astype(out[name].dtype))
    for name, factor in factors.items():
        out[name] = (out[name] * factor).astype(out[name].dtype)
    return out
```

```python
import math
from collections import namedtuple
from contextlib import ExitStack

import concourse.bass as bass
from concourse import mybir

F32 = mybir.dt.float32
I32 = mybir.dt.int32
ALU = mybir.AluOpType
ACT = mybir.ActivationFunctionType
AX = mybir.AxisListType

P = 128
T = 256
TT = T // P
D = 1024
KC = D // P
FF = 2816
NB = FF // 256
HD = 64
CK = 64
NCK = T // CK
G = 8
R = 6
DECAY = math.exp(-0.5)

STREAM = [("w_in", 11), ("km", 4), ("vm", 4), ("w_out", 4), ("wq", 4), ("wo", 4), ("ffn0", 33), ("ffn1", 33),
          ("q", 4), ("k", 4), ("v", 4), ("attn_o", 4), ("ffn2", 33), ("ffn3", 33),
          ("z", 8), ("xbc", 16), ("ssm_out", 8), ("ffn4", 33)]
FIRST = {}
_n = 0
for _name, _count in STREAM:
    FIRST[_name] = _n
    _n += _count
NSLOTS = _n

PCOLS = [("gain", 80), ("ssm_norm", 16), ("mu", 14), ("w0", 4), ("a0", 4), ("k_k", 4), ("k_a", 4), ("r_k", 4),
         ("lnx_g", 4), ("lnx_b", 4), ("conv_w", 124), ("conv_b", 4), ("ln_g", 4), ("ln_b", 4),
         ("sconv_w", 128), ("sconv_b", 32), ("wa_up", 512), ("g_up", 512), ("w_dt", 256)]
PROWS = [("g1", D), ("g3", D), ("g5", D), ("q_gain", 128), ("k_gain", 128), ("dt_bias", 32), ("a_log", 32),
         ("d_skip", 32)]
CCOLS = [("ident", 128), ("pair", 128), ("ones", 128), ("upper", 128), ("future", 128), ("causal", 512),
         ("s_lt_t", 64), ("s_le_t", 64), ("eye64", 64), ("off1T", 64), ("off", 384), ("inv_freq", 64), ("zeros", 64)]


def offsets(table):
    at, out = 0, {}
    for name, width in table:
        out[name] = (at, width)
        at += width
    return out, at


PAT, NP_ = offsets(PCOLS)
RAT, NR_ = offsets(PROWS)
CAT, NC_ = offsets(CCOLS)


def build_program(nc, W, cols, rows, consts, x_in, mem_in, pos_in, out):
    with ExitStack() as ctx:
        def sb(name, words, dt=F32):
            return ctx.enter_context(nc.sbuf_tensor(name, [P, words], dt))

        def sem(name):
            return ctx.enter_context(nc.semaphore(name))

        ring_t = sb("ring", R * 2048)
        X = sb("x_resid", TT * D)[:].rearrange("p (t d) -> p t d", t=TT)
        xn_t = sb("x_normed", TT * D)
        xn = xn_t[:].rearrange("p (t d) -> p t d", t=TT)
        hT = sb("hT", KC * T)[:].rearrange("p (c t) -> p c t", c=KC)
        act_t = sb("ffn_act", 2048)
        sg = act_t[:, 0:1024].rearrange("p (q n) -> p q n", q=2)
        gact = act_t[:, 1024:2048].rearrange("p (q j t) -> p q j t", q=2, j=2)
        ptab = sb("ptab", NP_)
        rtab = sb("rtab", NR_)
        ctab = sb("ctab", NC_)
        small = sb("small", 1400)
        pos_i = sb("pos_i", TT, I32)
        ARENA = 23600
        arena = sb("arena", ARENA)
        PS = ctx.enter_context(nc.psum_tensor("PS", [P, 8, 512], F32))

        def pc(name, i=0, n=1):
            at = PAT[name][0] + i
            return ptab[:, at:at + n]

        def row(name):
            at, w = RAT[name]
            return rtab[:, at:at + w]

        def cn(name, i=0, n=None):
            at, w = CAT[name]
            n = w if n is None else n
            return ctab[:, at + i:at + i + n]

        ident = cn("ident")

        used_small = [0]

        def sm(n):
            used_small[0] += n
            assert used_small[0] <= 1400
            return small[:, used_small[0] - n:used_small[0]]

        ssq, ms, std, rstd = sm(2), sm(2), sm(2), sm(2)
        yssq, yms, ystd, yrstd = sm(4), sm(2), sm(2), sm(2)

        def region(at, words):
            assert at + words <= ARENA, (at, words)
            return arena[:, at:at + words]

        o = 0
        pin_r = region(o, 3598); o += 3598
        pin = pin_r.rearrange("p (c t) -> p c t", c=14)
        Pc = pin_r[:, 0:1040].rearrange("p (s t) -> p s t", s=16)
        tmp = pin_r[:, 1040:2064]
        bonus = pin_r[:, 2064:3088]
        Q_r = region(o, 3584); o += 3584
        Q = Q_r.rearrange("p (c t) -> p c t", c=14)
        r_f, k_f, v_f = Q_r[:, 0:1024], Q_r[:, 1024:2048], Q_r[:, 2048:3072]
        kmT = region(o, 2048).rearrange("p (c t) -> p c t", c=KC); o += 2048
        vm_r = region(o, 2048); o += 2048
        vm = vm_r.rearrange("p (t d) -> p t d", t=TT)
        MEM = vm
        memT = act_t[:].rearrange("p (c t) -> p c t", c=KC)
        glu = region(o, 1024); o += 1024
        conv = region(o, 1024); o += 1024
        usig = conv
        decay = region(o, 1024); o += 1024
        invP = decay
        a_f = region(o, 1024); o += 1024
        g_f = region(o, 1024); o += 1024
        kk = region(o, 1024); o += 1024
        V_t = region(o, 1024).rearrange("p (t d) -> p t d", t=TT); o += 1024
        K_t = xn_t[:, 0:1024].rearrange("p (t d) -> p t d", t=TT)
        B_t = xn_t[:, 1024:2048].rearrange("p (t d) -> p t d", t=TT)
        kept = [region(o + 512 * i, 512) for i in range(8)]; o += 8 * 512
        MTs, RKTs, RBTs, XiTs = kept[0:2], kept[2:4], kept[4:6], kept[6:8]
        NL, Xi = decay[:, 0:512], decay[:, 512:1024]
        Loff, Qi = act_t[:, 0:512], act_t[:, 512:1024]
        Zn = act_t[:, 1024:2048].rearrange("p (q c v) -> p q c v", q=2, c=4)
        RU, U = v_f[:, 0:512], v_f[:, 512:1024]
        Y = k_f.rearrange("p (t d) -> p t d", t=TT)
        sqr = a_f
        tshift = conv[:, 0:512]
        RW_END = o
        YT = hT
        o = 7182 + 4096
        prob = region(o, 2048).rearrange("p (s m) -> p s m", s=8); o += 2048
        probT = region(o, 2048).rearrange("p (h k t) -> p h k t", h=4, k=2); o += 2048
        qT = region(0, 2048).rearrange("p (c t) -> p c t", c=KC)
        o2 = 7182 + 4096 + 4096
        kT2 = region(2048, 2048).rearrange("p (c t) -> p c t", c=KC)
        v2 = region(4096, 2048).rearrange("p (t d) -> p t d", t=TT)
        q_r = region(7182, 2048)
        k_r = region(7182 + 2048, 2048)
        rt1 = region(o2, 2048)
        rt2 = region(o2 + 2048, 2048)
        o = 0
        xsT_r = region(o, 4096); o += 4096
        xsT = xsT_r.rearrange("p (c t) -> p c t", c=16)
        y_s = xsT_r.rearrange("p (t d) -> p t d", t=TT)
        bcT = region(o, 4096).rearrange("p (c t) -> p c t", c=16); o += 4096
        xtok_r = region(o, 4096); o += 4096
        xtok = xtok_r.rearrange("p (t d) -> p t d", t=TT)
        ysT = xtok_r.rearrange("p (c t) -> p c t", c=16)
        z_r = region(o, 4096); o += 4096
        z_s = z_r.rearrange("p (t d) -> p t d", t=TT)
        Btok = region(o, 1024).rearrange("p (g n) -> p g n", g=G); o += 1024
        ctmp = region(o, 2048).rearrange("p (q n) -> p q n", q=4); o += 2048
        LT = region(o, 1024).rearrange("p (q r l) -> p q r l", q=2, r=4); o += 1024
        Wd = region(o, 1024).rearrange("p (q r l) -> p q r l", q=2, r=4); o += 1024
        xdt = region(o, 512).rearrange("p (q n) -> p q n", q=2); o += 512
        xdec = region(o, 512).rearrange("p (q n) -> p q n", q=2); o += 512
        stT = region(o, 512).rearrange("p (q n) -> p q n", q=2); o += 512
        ytmp = region(o, 256); o += 256
        SQ = region(4096, 4096)
        posf, trig, turns = sm(TT), sm(256), sm(256)
        nmax, psum_, rsum = sm(8), sm(8), sm(8)
        qkms, qkstd, qkr = sm(32), sm(32), sm(32)
        dta_r, dt_, dte, aexp = sm(64), sm(64), sm(64), sm(32)
        dta = dta_r.rearrange("p (t h) -> p t h", t=TT)
        nacs, dec0, eacs = sm(64), sm(32), sm(32)
        cvar, cstd, crstd, bst, bag = sm(2), sm(2), sm(2), sm(12), sm(4)
        ymean, ynvar, ynstd, ynrstd = sm(16), sm(16), sm(16), sm(16)
        ysms, ysstd, ysr = sm(16), sm(16), sm(16)

        NAMES = ("params_loaded x_loaded mem_loaded pos_loaded out_stored dve_step act_step "
                 "ssq_ready ms_ready std_ready xn_ready xT_ready hT_ready x_ready silu_ready act_ready "
                 "yssq_ready yms_ready ystd_ready pad_ready pin_ready usig_ready glu_ready q_mixed lora_ready "
                 "wa_done g_done decay_ready a_ready g_ready kmT_ready vm_ready "
                 "kkraw_ready kksq_ready kksum_done kkmax_ready kknorm_ready bonus_in bonus_sum_done "
                 "ab_ready tok_done tok_ready gram_done gram_ready invq_done invq_ready invx_done inv_ready "
                 "ru_done ru_ready u_done u_ready z_done z_ready yc_done yc_ready yn_sq ynvar_ready ynstd_ready "
                 "yn_ready ynT_done yT_ready conv_ready convT_done cvar_ready cstd_ready cn_ready cnT_done "
                 "convY_ready kk_std "
                 "score_done nmax_ready exp_ready prob_ready probT_done probT_ready o_done qT_ready "
                 "qk_evac qk_sq qk_ms qk_std qk_roped qkT_done qkT_ready v_ready ang_ready trig_ready "
                 "dt_done dt_abs dt_exp dt_ln aneg dta_ready acs_done acs_ready decay2_done "
                 "conv4_ready xbc_ready z_ready2 sT_done sT_ready g_cb g_lt g_w g_y g_st g_stready g_xdt g_xdec g_yev "
                 "ys_ready ys_sq ys_ms ys_std ysn_ready ysT_done ysT_ready").split()
        S = namedtuple("Signals", NAMES)(*[sem(n) for n in NAMES])
        loaded = [sem(f"loaded{r}") for r in range(R)]
        used = [sem(f"used{r}") for r in range(R)]

        class Slot:

            def __init__(self, n, i=0):
                self.r, self.u, self.i = n % R, n // R, i
                flat = ring_t[:, self.r * 2048:(self.r + 1) * 2048]
                self.feat = flat.rearrange("p (c n) -> p c n", c=KC)
                self.rows = flat.rearrange("p (c n) -> p c n", c=2)

            def wait_loaded(self, eng):
                eng.wait_ge(loaded[self.r], self.i * 16 + 16 * (self.u + 1))

            def wait_used(self, eng):
                eng.wait_ge(used[self.r], self.i + (self.u + 1))

        NORM_SRC = {1: MEM}
        NORM_DST = {1: memT}

        def ffn_slot(f, kind, b, i=0):
            at = {"G": 3 * b - 1 if b else 0, "U": 3 * b if b else 1, "D": 3 * b + 4 if b < NB - 1 else 32}[kind]
            return Slot(FIRST[f"ffn{f}"] + at, i)

        block = ctx.enter_context(nc.Block())

        @block.sync
        def _(sp):
            sp.dma_start(X, x_in.rearrange("(t p) d -> p t d", p=P)).then_inc(S.x_loaded, 16)
            sp.dma_start(MEM, mem_in.rearrange("(t p) d -> p t d", p=P)).then_inc(S.mem_loaded, 16)
            for r in range(R):
                sp.dma_start(ring_t[:, r * 2048:(r + 1) * 2048], W[r]).then_inc(loaded[r], 16)
            with sp.Fori(1, NSLOTS // R) as i:
                for r in range(R):
                    sp.wait_ge(used[r], i)
                    sp.dma_start(ring_t[:, r * 2048:(r + 1) * 2048], W[i * R + r]).then_inc(loaded[r], 16)
            for n in range(NSLOTS // R * R, NSLOTS):
                sp.wait_ge(used[n % R], n // R)
                sp.dma_start(ring_t[:, n % R * 2048:(n % R + 1) * 2048], W[n]).then_inc(loaded[n % R], 16)
            sp.wait_ge(S.x_ready, 9)
            sp.dma_start(out.rearrange("(t p) d -> p t d", p=P), X).then_inc(S.out_stored, 16)
            sp.wait_ge(S.out_stored, 16)

        @block.tensor
        def _(pe):
            mm = nc.tensor.matmul

            def norm(k):
                pe.wait_ge(S.xn_ready, 2 * (k + 1))
                if k == 1:
                    pe.wait_ge(S.hT_ready, 8)
                for c in range(KC):
                    for t in range(TT):
                        at = c % 2 * 256 + t * P
                        last = nc.tensor.transpose(PS[:, 4 + c // 2, at:at + P], xn[:, t, c * P:(c + 1) * P], ident)
                    if c % 2:
                        last.then_inc(S.xT_ready, 1)

            def feat_slot(slot, src, bank):
                slot.wait_loaded(pe)
                for j in range(2):
                    for c in range(KC):
                        last = mm(PS[:, bank, j * T:(j + 1) * T], slot.feat[:, c, j * P:(j + 1) * P], src[:, c, :],
                                  start=c == 0, stop=c == KC - 1)
                last.then_inc(used[slot.r], 1)

            def rows_slot(slot, tiles, bank, start, stop):
                slot.wait_loaded(pe)
                for j in range(2):
                    for t in range(TT):
                        for h in range(2):
                            last = mm(PS[:, bank + 2 * t + h, :], tiles(j)[:, t * P:(t + 1) * P],
                                      slot.rows[:, j, h * 512:(h + 1) * 512], start=start and j == 0,
                                      stop=stop and j == 1)
                last.then_inc(used[slot.r], 1)

            def rows_matrix(name, src, bank, n=4, first=0, c0=0):
                for s in range(n):
                    rows_slot(Slot(FIRST[name] + first + s), lambda j: src[:, c0 + 2 * s + j, :], bank, s == 0,
                              s == n - 1)

            def ffn(f):
                k = [3, 4, 6, 7, 9][f]
                pe.wait_ge(S.hT_ready, 8 * (k + 1))

                def gate_up(b, i=0, ii=0):
                    if b >= 2:
                        pe.wait_ge(S.act_ready, ii * 2 + (NB * f + b - 1))
                    for kind, bank in (("G", 4), ("U", 5)):
                        feat_slot(ffn_slot(f, kind, b, i), hT, bank + 2 * (b % 2))

                def down(b, i=0, ii=0):
                    pe.wait_ge(S.act_ready, ii * 2 + (NB * f + b + 1))
                    rows_slot(ffn_slot(f, "D", b, i), lambda j: gact[:, b % 2, j, :], 0, b == 0, b == NB - 1)

                gate_up(0)
                gate_up(1)
                down(0)
                with pe.Fori(0, (NB - 3) // 2) as i:
                    for b in (1, 2):
                        gate_up(b + 1, i, i)
                        down(b, i, i)
                gate_up(NB - 1)
                down(NB - 2)
                down(NB - 1)

            def attention(a, src_q, src_k, src_v, dtiles, heads, half, hold):
                for h in range(4):
                    for t in range(TT):
                        s = 2 * h + t
                        for j in range(dtiles):
                            c = (half * 4 + h) * dtiles + j
                            last = mm(PS[:, s // 2, s % 2 * T:(s % 2 + 1) * T], src_q[:, c, t * P:(t + 1) * P],
                                      src_k[:, c, :], start=j == 0, stop=j == dtiles - 1)
                last.then_inc(S.score_done, 1)
                pe.wait_ge(S.prob_ready, a + 1)
                for h in range(4):
                    for m in range(2):
                        for t in range(TT):
                            at = m * T + t * P
                            last = nc.tensor.transpose(PS[:, 4 + h, at:at + P],
                                                       prob[:, 2 * h + t, m * P:(m + 1) * P], ident)
                last.then_inc(S.probT_done, 1)
                pe.wait_ge(S.probT_ready, 4 * (a + 1))
                for h in range(4):
                    for j in range(dtiles):
                        c = (half * 4 + h) * dtiles + j
                        o_ = h * dtiles + j
                        for m in range(2):
                            last = mm(PS[:, o_ // 2, o_ % 2 * T:(o_ % 2 + 1) * T], src_v[:, m, c * P:(c + 1) * P],
                                      probT[:, h, m, :], start=m == 0, stop=m == 1)
                last.then_inc(S.o_done, 1)

            pe.wait_ge(S.params_loaded, 48)
            norm(0)
            pe.wait_ge(S.hT_ready, 8)
            norm(1)
            for n in range(11):
                if n >= 4:
                    pe.wait_ge(S.pin_ready, n - 3)
                feat_slot(Slot(n), hT, n % 4)
            pe.wait_ge(S.hT_ready, 16)
            for n in range(4):
                if n >= 2:
                    pe.wait_ge(S.kmT_ready, n - 1)
                feat_slot(Slot(FIRST["km"] + n), memT, 4 + n % 2)
            pe.wait_ge(S.pin_ready, 11)
            pe.wait_ge(S.lora_ready, 3)
            for c in range(4):
                last = mm(PS[:, c // 2, c % 2 * T:(c % 2 + 1) * T], ptab[0:64, PAT["wa_up"][0] + c * P:PAT["wa_up"][0] + (c + 1) * P],
                          Q[0:64, 12, :], start=True, stop=True)
            for c in range(4):
                last = mm(PS[:, 2 + c // 2, c % 2 * T:(c % 2 + 1) * T],
                          ptab[64:128, PAT["wa_up"][0] + c * P:PAT["wa_up"][0] + (c + 1) * P],
                          Q[64:128, 12, :], start=True, stop=True)
            last.then_inc(S.wa_done, 1)
            for c in range(4):
                last = mm(PS[:, 6 + c // 2, c % 2 * T:(c % 2 + 1) * T], pc("g_up", c * P, P), Q[:, 13, :],
                          start=True, stop=True)
            last.then_inc(S.g_done, 1)
            pe.wait_ge(S.kmT_ready, 4)
            pe.wait_ge(S.kksq_ready, 1)
            for c in range(2):
                last = mm(PS[:, 4 + c, :], cn("pair"), tmp[:, c * 512:(c + 1) * 512], start=True, stop=True)
            last.then_inc(S.kksum_done, 1)
            pe.wait_ge(S.a_ready, 1)
            rows_matrix("vm", memT, 0)
            pe.wait_ge(S.bonus_in, 1)
            for c in range(2):
                last = mm(PS[:, 4 + c, :], cn("pair"), tmp[:, c * 512:(c + 1) * 512], start=True, stop=True)
            last.then_inc(S.bonus_sum_done, 1)
            pe.wait_ge(S.ab_ready, 1)
            pe.wait_ge(S.g_ready, 1)
            pe.wait_ge(S.vm_ready, 4)
            banks = [0, 1, 2, 3, 6, 7]
            for q, src in enumerate((v_f, k_f, a_f)):
                for t in range(TT):
                    for c in range(4):
                        last = nc.tensor.transpose(PS[:, banks[2 * q + t], c * P:(c + 1) * P],
                                                   src[:, c * T + t * P:c * T + (t + 1) * P], ident)
            last.then_inc(S.tok_done, 1)
            pe.wait_ge(S.tok_ready, 6)

            def chunks(t):
                for h in range(8):
                    for ch in range(2):
                        yield h, ch, h // 2, 64 * (h % 2), 64 * ch, t * P + 64 * ch

            def gram(bank, lhs, rhs, t, at=0):
                for h, ch, c, hp, cp, tok in chunks(t):
                    last = mm(PS[cp:cp + 64, bank + h % 2, at + c * 64:at + (c + 1) * 64],
                              lhs[hp:hp + 64, c * T + tok:c * T + tok + 64],
                              rhs[hp:hp + 64, c * T + tok:c * T + tok + 64], start=True, stop=True)
                return last

            def blockmul(bank, lhs, rhs, t):
                for h, ch, c, hp, cp, tok in chunks(t):
                    last = mm(PS[cp:cp + 64, bank, h * 64:(h + 1) * 64], lhs[cp:cp + 64, h * 64:(h + 1) * 64],
                              rhs[cp:cp + 64, h * 64:(h + 1) * 64], start=True, stop=True)
                return last

            At, Rt, Kt, Bt = kk, r_f, k_f, a_f
            for t in range(TT):
                XiT = XiTs[t]
                if t:
                    pe.wait_ge(S.inv_ready, 6)
                gram(0, At, Bt, t)
                gram(0, Bt, At, t, 256)
                gram(2, Kt, At, t)
                gram(2, Kt, Rt, t, 256)
                gram(6, Bt, Rt, t).then_inc(S.gram_done, 1)
                pe.wait_ge(S.gram_ready, t + 1)
                for lv in range(5):
                    n = 5 * t + lv
                    pe.wait_ge(S.inv_ready, 6 * t + lv + 1)
                    blockmul(0, Loff, XiT, t).then_inc(S.invq_done, 1)
                    pe.wait_ge(S.invq_ready, n + 1)
                    last = blockmul(1, Xi, Qi, t)
                    if lv < 4:
                        last = blockmul(2, Qi, Xi, t)
                    last.then_inc(S.invx_done, 1)
            pe.wait_ge(S.inv_ready, 12)
            for g in range(NCK):
                t, cp = g // 2, 64 * (g % 2)
                MT, RKT, RBT, XiT = MTs[t], RKTs[t], RBTs[t], XiTs[t]
                Z = Zn[:, (g - 1) % 2, :, :]
                tok = t * P + cp
                if g:
                    pe.wait_ge(S.z_ready, g)
                for c in range(4):
                    if g:
                        mm(PS[cp:cp + 64, 0, c * P:(c + 1) * P], At[:, c * T + tok:c * T + tok + 64], Z[:, c, :],
                           start=True, stop=False)
                    for h in (2 * c, 2 * c + 1):
                        last = mm(PS[cp:cp + 64, 0, h * 64:(h + 1) * 64], MT[cp:cp + 64, h * 64:(h + 1) * 64],
                                  V_t[cp:cp + 64, t, h * 64:(h + 1) * 64], start=g == 0, stop=g == 0 or h % 2 == 1)
                last.then_inc(S.ru_done, 1)
                pe.wait_ge(S.ru_ready, g + 1)
                for h in range(8):
                    last = mm(PS[cp:cp + 64, 1, h * 64:(h + 1) * 64], XiT[cp:cp + 64, h * 64:(h + 1) * 64],
                              RU[cp:cp + 64, h * 64:(h + 1) * 64], start=True, stop=True)
                last.then_inc(S.u_done, 1)
                pe.wait_ge(S.u_ready, g + 1)
                if g < NCK - 1:
                    for c in range(4):
                        cs = slice(c * P, (c + 1) * P)
                        mm(PS[:, 3, cs], K_t[cp:cp + 64, t, cs], V_t[cp:cp + 64, t, cs], start=True, stop=False)
                        if g:
                            mm(PS[:, 3, cs], ident, Z[:, c, :], start=False, stop=False)
                        last = mm(PS[:, 3, cs], B_t[cp:cp + 64, t, cs], U[cp:cp + 64, cs], start=False, stop=True)
                    last.then_inc(S.z_done, 1)
                if g:
                    pe.wait_ge(S.yc_ready, g)
                for c in range(4):
                    if g:
                        mm(PS[cp:cp + 64, 2, c * P:(c + 1) * P], Rt[:, c * T + tok:c * T + tok + 64], Z[:, c, :],
                           start=True, stop=False)
                    for h in (2 * c, 2 * c + 1):
                        hs = slice(h * 64, (h + 1) * 64)
                        mm(PS[cp:cp + 64, 2, hs], RKT[cp:cp + 64, hs], V_t[cp:cp + 64, t, hs], start=g == 0,
                           stop=False)
                        last = mm(PS[cp:cp + 64, 2, hs], RBT[cp:cp + 64, hs], U[cp:cp + 64, hs], start=False,
                                  stop=g == 0 or h % 2 == 1)
                last.then_inc(S.yc_done, 1)
            pe.wait_ge(S.conv_ready, 1)
            for t in range(TT):
                for c in range(4):
                    last = nc.tensor.transpose(PS[:, 4 + t, c * P:(c + 1) * P],
                                               conv[:, c * T + t * P:c * T + (t + 1) * P], ident)
            last.then_inc(S.convT_done, 1)
            pe.wait_ge(S.cn_ready, 2)
            for c in range(4):
                for t in range(TT):
                    at = c % 2 * T + t * P
                    last = nc.tensor.transpose(PS[:, 6 + c // 2, at:at + P], tmp[:, t * 512 + c * P:t * 512 + (c + 1) * P],
                                               ident)
            last.then_inc(S.cnT_done, 1)
            pe.wait_ge(S.yn_ready, 1)
            for c in range(4):
                for t in range(TT):
                    at = c % 2 * T + t * P
                    last = nc.tensor.transpose(PS[:, c // 2, at:at + P], Y[:, t, c * P:(c + 1) * P], ident)
            last.then_inc(S.ynT_done, 1)
            pe.wait_ge(S.convY_ready, 4)
            pe.wait_ge(S.yT_ready, 1)
            rows_matrix("w_out", YT, 0)

            norm(2)
            pe.wait_ge(S.hT_ready, 24)
            for n in range(4):
                feat_slot(Slot(FIRST["wq"] + n), hT, n)
            pe.wait_ge(S.qT_ready, 4)
            attention(0, qT, kmT, vm, 2, 4, 0, None)
            pe.wait_ge(S.qT_ready, 8)
            rows_matrix("wo", hT, 4)

            norm(3)
            ffn(0)
            norm(4)
            ffn(1)
            norm(5)
            pe.wait_ge(S.hT_ready, 48)
            rows_matrix("q", hT, 0)
            rows_matrix("k", hT, 4)
            pe.wait_ge(S.qk_evac, 4)
            rows_matrix("v", hT, 0)
            for q, src in enumerate((q_r, k_r)):
                pe.wait_ge(S.qk_roped, q + 1)
                if q:
                    pe.wait_ge(S.qkT_ready, 4)
                else:
                    pe.wait_ge(S.qk_evac, 8)
                s3 = src.rearrange("p (t d) -> p t d", t=TT)
                for h in range(8):
                    for t in range(TT):
                        at = h % 2 * T + t * P
                        last = nc.tensor.transpose(PS[:, 4 + h // 2, at:at + P], s3[:, t, h * P:(h + 1) * P], ident)
                last.then_inc(S.qkT_done, 1)
            pe.wait_ge(S.qkT_ready, 8)
            pe.wait_ge(S.v_ready, 4)
            attention(1, qT, kT2, v2, 1, 8, 0, None)
            pe.wait_ge(S.qT_ready, 12)
            attention(2, qT, kT2, v2, 1, 8, 1, None)
            pe.wait_ge(S.qT_ready, 16)
            rows_matrix("attn_o", hT, 4)
            norm(6)
            ffn(2)
            norm(7)
            ffn(3)

            norm(8)
            pe.wait_ge(S.hT_ready, 72)
            for t in range(TT):
                for c in range(KC):
                    last = mm(PS[:, 4 + t, 0:32], hT[:, c, t * P:(t + 1) * P], pc("w_dt", c * 32, 32),
                              start=c == 0, stop=c == KC - 1)
            last.then_inc(S.dt_done, 1)
            for half in range(2):
                if half:
                    pe.wait_ge(S.z_ready2, 4)
                rows_matrix("z", hT, 0, first=4 * half)
            pe.wait_ge(S.dta_ready, 1)
            for t in range(TT):
                mm(PS[:, 6, t * 32:(t + 1) * 32], cn("upper"), dta[:, t, :], start=True, stop=True)
            mm(PS[:, 6, 64:96], cn("ones"), dta[:, 0, :], start=True, stop=True).then_inc(S.acs_done, 1)
            pe.wait_ge(S.acs_ready, 1)
            for n in range(16):
                bank = [4, 5, 6, 7][n % 4]
                if n >= 4:
                    pe.wait_ge(S.conv4_ready, 2 * (n - 3))
                feat_slot(Slot(FIRST["xbc"] + n), hT, bank)
            pe.wait_ge(S.z_ready2, 8)
            for n in range(10):
                if n < 4:
                    pe.wait_ge(S.xbc_ready, 32)
                else:
                    pe.wait_ge(S.sT_ready, n - 3)
                for q in range(4):
                    if n < 8:
                        src = xsT[:, n % 4 * 4 + q, n // 4 * P:(n // 4 + 1) * P]
                    else:
                        src = bcT[:, (n - 8) * 4 + q, 0:P]
                    last = nc.tensor.transpose(PS[:, n % 4, q * P:(q + 1) * P], src, ident)
                last.then_inc(S.sT_done, 1)
            pe.wait_ge(S.sT_ready, 10)
            pe.wait_ge(S.conv4_ready, 32)
            for g in range(G):
                for t in range(TT):
                    n = 2 * g + t
                    b = n % 2
                    if n >= 2:
                        pe.wait_ge(S.g_lt, n - 1)
                        pe.wait_ge(S.g_w, n - 1)
                    mm(PS[:, b, :], ident, cn("future").unsqueeze(1).broadcast_to([P, 4, P]), start=True, stop=False)
                    for r in range(4):
                        h = 4 * g + r
                        mm(PS[:, b, r * P:(r + 1) * P], dta[:, t, h:h + 1].broadcast_to([P, P]), cn("upper"),
                           start=False, stop=r == 3)
                    mm(PS[:, 2 + b, 0:P], bcT[:, g, t * P:(t + 1) * P], bcT[:, 8 + g, t * P:(t + 1) * P],
                       start=True, stop=True).then_inc(S.g_cb, 1)
                    if t == 0:
                        pe.wait_ge(S.g_xdec, g + 1)
                        if g >= 1:
                            pe.wait_ge(S.g_stready, g)
                        mm(PS[:, 6, 0:256], Btok[:, g, :], xdec[:, g % 2, :], start=True, stop=True).then_inc(S.g_st, 1)
                    else:
                        pe.wait_ge(S.g_stready, g + 1)
                        if g >= 1:
                            pe.wait_ge(S.g_yev, n - 1)
                        mm(PS[:, 7, 0:256], bcT[:, 8 + g, P:T], stT[:, g % 2, :], start=True, stop=True)
                    pe.wait_ge(S.g_w, n + 1)
                    if n >= 2:
                        pe.wait_ge(S.g_yev, n - 1)
                    for r in range(4):
                        last = mm(PS[:, 4 + b, r * 64:(r + 1) * 64], Wd[:, b, r, :], xdt[:, b, r * 64:(r + 1) * 64],
                                  start=True, stop=True)
                    last.then_inc(S.g_y, 1)
            pe.wait_ge(S.ysn_ready, 1)
            for n in range(8):
                if n >= 4:
                    pe.wait_ge(S.ysT_ready, 2 * (n - 3))
                for j in range(2):
                    for t in range(TT):
                        c = 2 * n + j
                        last = nc.tensor.transpose(PS[:, n % 4, j * T + t * P:j * T + (t + 1) * P],
                                                   y_s[:, t, c * P:(c + 1) * P], ident)
                last.then_inc(S.ysT_done, 1)
            pe.wait_ge(S.ysT_ready, 16)
            rows_matrix("ssm_out", ysT, 4, n=8)
            norm(9)
            ffn(4)

        @block.scalar
        def _(act):
            A = nc.scalar.activation
            steps = [0]

            def step(ins):
                steps[0] += 1
                ins.then_inc(S.act_step, 1)
                act.wait_ge(S.act_step, steps[0])

            def norm(k):
                src = NORM_SRC.get(k, X)
                if k >= 2:
                    act.wait_ge(S.x_ready, k - 1)
                else:
                    act.wait_ge(S.mem_loaded if k else S.x_loaded, 16)
                if k == 1:
                    act.wait_ge(S.xT_ready, 4)
                for t in range(TT):
                    A(xn[:, t, :], src[:, t, :], ACT.Square, accum_out=ssq[:, t:t + 1]).then_inc(S.ssq_ready, 1)
                act.wait_ge(S.ms_ready, k + 1)
                A(std, ms, ACT.Sqrt).then_inc(S.std_ready, 1)
                dst = NORM_DST.get(k, hT)
                for c in range(4):
                    act.wait_ge(S.xT_ready, 4 * k + c // 2 + 1)
                    A(dst[:, c, :], PS[:, 4 + c // 2, c % 2 * T:(c % 2 + 1) * T], ACT.Copy, scale=pc("gain", 8 * k + c)).then_inc(S.hT_ready, 1)

            def ysquare(k, bank, last_slot):
                last_slot.wait_used(act)
                for t in range(TT):
                    for h in range(2):
                        A(xn[:, t, h * 512:(h + 1) * 512], PS[:, bank + 2 * t + h, :], ACT.Square,
                          accum_out=yssq[:, 2 * t + h:2 * t + h + 1]).then_inc(S.yssq_ready, 1)
                act.wait_ge(S.yms_ready, k + 1)
                A(ystd, yms, ACT.Sqrt).then_inc(S.ystd_ready, 1)

            def ffn(f):
                def silu(b, i=0, ii=0):
                    ffn_slot(f, "G", b, i).wait_used(act)
                    if b >= 2:
                        act.wait_ge(S.act_ready, ii * 2 + (NB * f + b - 1))
                    A(sg[:, b % 2, :], PS[:, 4 + 2 * (b % 2), :], ACT.Silu).then_inc(S.silu_ready, 1)
                silu(0)
                silu(1)
                with act.Fori(0, (NB - 3) // 2) as i:
                    for b in (2, 3):
                        silu(b, i, i)
                silu(NB - 1)

            def attention(a, scale):
                act.wait_ge(S.nmax_ready, a + 1)
                for s in range(8):
                    last = A(prob[:, s, :], PS[:, s // 2, s % 2 * T:(s % 2 + 1) * T], ACT.Exp, bias=nmax[:, s:s + 1],
                             scale=scale, accum_out=psum_[:, s:s + 1])
                last.then_inc(S.exp_ready, 1)
                act.wait_ge(S.probT_done, a + 1)
                for h in (0, 2):
                    A(probT[:, h, :, :], PS[:, 4 + h, :].rearrange("p (k t) -> p k t", k=2), ACT.Copy)\
                        .then_inc(S.probT_ready, 1)

            act.dma_start(ptab[:], cols).then_inc(S.params_loaded, 16)
            act.dma_start(ctab[:], consts).then_inc(S.params_loaded, 16)
            act.dma_start(rtab[:], rows.broadcast_to([P, NR_])).then_inc(S.params_loaded, 16)
            act.dma_start(pos_i[:], pos_in).then_inc(S.pos_loaded, 16)
            act.wait_ge(S.params_loaded, 48)
            norm(0)
            norm(1)
            act.wait_ge(S.ang_ready, 1)
            A(trig, trig, ACT.Sin).then_inc(S.trig_ready, 1)
            act.wait_ge(S.pad_ready, 1)
            for n in range(11):
                Slot(n).wait_used(act)
                if n < 2:
                    A(glu[:, n * 512:(n + 1) * 512], PS[:, n % 4, :], ACT.Copy).then_inc(S.pin_ready, 1)
                elif n < 4:
                    A(usig[:, (n - 2) * 512:(n - 1) * 512], PS[:, n % 4, :], ACT.Sigmoid).then_inc(S.pin_ready, 1)
                else:
                    c = 2 * (n - 4)
                    A(pin[:, c:c + 2, 1:T + 1], PS[:, n % 4, :].rearrange("p (c t) -> p c t", c=2), ACT.Copy)\
                        .then_inc(S.pin_ready, 1)
            for n in range(4):
                Slot(FIRST["km"] + n).wait_used(act)
                A(kmT[:, 2 * n:2 * n + 2, :], PS[:, 4 + n % 2, :].rearrange("p (c t) -> p c t", c=2), ACT.Copy)\
                    .then_inc(S.kmT_ready, 1)
            act.wait_ge(S.q_mixed, 7)
            A(Q[0:64, 12, :], Q[0:64, 12, :], ACT.Tanh).then_inc(S.lora_ready, 1)
            A(Q[:, 13, :], Q[:, 13, :], ACT.Sigmoid).then_inc(S.lora_ready, 2)
            act.wait_ge(S.wa_done, 1)
            for c in range(4):
                last = A(decay[:, c * T:(c + 1) * T], PS[:, c // 2, c % 2 * T:(c % 2 + 1) * T], ACT.Sigmoid,
                         bias=pc("w0", c))
            for c in range(4):
                last = A(a_f[:, c * T:(c + 1) * T], PS[:, 2 + c // 2, c % 2 * T:(c % 2 + 1) * T], ACT.Sigmoid,
                         bias=pc("a0", c))
            last.then_inc(S.a_ready, 1)
            act.wait_ge(S.g_done, 1)
            A(g_f, PS[:, 6:8, :].rearrange("p a b -> p (a b)"), ACT.Copy).then_inc(S.g_ready, 1)
            act.wait_ge(S.a_ready, 1)
            A(decay, decay, ACT.Exp, scale=-DECAY).then_inc(S.decay_ready, 1)
            act.wait_ge(S.kkmax_ready, 1)
            A(tmp, tmp, ACT.Sqrt).then_inc(S.kk_std, 1)
            Slot(FIRST["vm"] + 3).wait_used(act)
            for b in range(4):
                A(vm[:, b // 2, b % 2 * 512:(b % 2 + 1) * 512], PS[:, b, :], ACT.Copy).then_inc(S.vm_ready, 1)
            act.wait_ge(S.tok_done, 1)
            for i, (bank, dst, t) in enumerate(((0, V_t, 0), (1, V_t, 1), (2, K_t, 0), (3, K_t, 1), (6, B_t, 0), (7, B_t, 1))):
                if i % 2 == 0:
                    A(dst[:, t, :], PS[:, bank, :], ACT.Copy).then_inc(S.tok_ready, 1)
            for n in range(10):
                act.wait_ge(S.invq_done, n + 1)
                A(Qi, PS[:, 0, :], ACT.Copy).then_inc(S.invq_ready, 1)
            for g in range(NCK):
                t, cp = g // 2, 64 * (g % 2)
                act.wait_ge(S.ru_done, g + 1)
                A(RU[cp:cp + 64, :], PS[cp:cp + 64, 0, :], ACT.Copy).then_inc(S.ru_ready, 1)
                act.wait_ge(S.u_done, g + 1)
                A(U[cp:cp + 64, :], PS[cp:cp + 64, 1, :], ACT.Copy).then_inc(S.u_ready, 1)
                act.wait_ge(S.yc_done, g + 1)
                A(Y[cp:cp + 64, t, :], PS[cp:cp + 64, 2, :], ACT.Copy).then_inc(S.yc_ready, 1)
            act.wait_ge(S.cvar_ready, 1)
            A(cstd, cvar, ACT.Sqrt).then_inc(S.cstd_ready, 1)
            act.wait_ge(S.ynvar_ready, 1)
            A(ynstd, ynvar, ACT.Sqrt).then_inc(S.ynstd_ready, 1)
            act.wait_ge(S.cnT_done, 1)
            for c in range(4):
                A(YT[:, c, :], PS[:, 6 + c // 2, c % 2 * T:(c % 2 + 1) * T], ACT.Silu, bias=pc("ln_b", c),
                  scale=pc("ln_g", c)).then_inc(S.convY_ready, 1)
            ysquare(0, 0, Slot(FIRST["w_out"] + 3))
            norm(2)
            for n in range(4):
                Slot(FIRST["wq"] + n).wait_used(act)
                A(qT[:, 2 * n:2 * n + 2, :], PS[:, n, :].rearrange("p (c t) -> p c t", c=2), ACT.Copy)\
                    .then_inc(S.qT_ready, 1)
            attention(0, 1.0 / 16)
            act.wait_ge(S.o_done, 1)
            for n in range(4):
                A(hT[:, 2 * n:2 * n + 2, :], PS[:, n, :].rearrange("p (c t) -> p c t", c=2), ACT.Copy)\
                    .then_inc(S.qT_ready, 1)
            ysquare(1, 4, Slot(FIRST["wo"] + 3))
            norm(3)
            ffn(0)
            ysquare(2, 0, ffn_slot(0, "D", NB - 1))
            norm(4)
            ffn(1)
            norm(5)
            for q, (dst, bank) in enumerate(((q_r, 0), (k_r, 4))):
                Slot(FIRST["qk"[q]] + 3).wait_used(act)
                for b in range(4):
                    A(dst[:, b * 512:(b + 1) * 512], PS[:, bank + b, :], ACT.Copy).then_inc(S.qk_evac, 1)
                if q:
                    act.wait_ge(S.qk_ms, 1)
                act.wait_ge(S.qk_evac, 4 * (q + 1))
                A(rt1, dst, ACT.Square).then_inc(S.qk_sq, 1)
            for q in range(2):
                act.wait_ge(S.qk_ms, q + 1)
                A(qkstd[:, q * 16:(q + 1) * 16], qkms[:, q * 16:(q + 1) * 16], ACT.Sqrt).then_inc(S.qk_std, 1)
            Slot(FIRST["v"] + 3).wait_used(act)
            for b in range(4):
                A(v2[:, b // 2, b % 2 * 512:(b % 2 + 1) * 512], PS[:, b, :], ACT.Copy).then_inc(S.v_ready, 1)
            for q, dst in enumerate((qT, kT2)):
                act.wait_ge(S.qkT_done, q + 1)
                for n in range(4):
                    A(dst[:, 2 * n:2 * n + 2, :], PS[:, 4 + n, :].rearrange("p (c t) -> p c t", c=2), ACT.Copy)\
                        .then_inc(S.qkT_ready, 1)
            for half in range(2):
                attention(1 + half, 128 ** -0.5)
                act.wait_ge(S.o_done, 2 + half)
                for n in range(2):
                    A(hT[:, 4 * half + 2 * n:4 * half + 2 * n + 2, :], PS[:, n, :].rearrange("p (c t) -> p c t", c=2),
                      ACT.Copy).then_inc(S.qT_ready, 2)
            norm(6)
            ffn(2)
            norm(7)
            ffn(3)
            norm(8)
            act.wait_ge(S.dt_abs, 1)
            A(dte, dte, ACT.Exp, scale=-1.0).then_inc(S.dt_exp, 1)
            A(aexp, row("a_log"), ACT.Exp).then_inc(S.aneg, 1)
            act.wait_ge(S.dt_exp, 1)
            A(dte, dte, ACT.Ln, bias=1.0).then_inc(S.dt_ln, 1)
            for half in range(2):
                Slot(FIRST["z"] + 4 * half + 3).wait_used(act)
                for b in range(4):
                    at = half * 1024 + b % 2 * 512
                    A(z_s[:, b // 2, at:at + 512], PS[:, b, :], ACT.Silu).then_inc(S.z_ready2, 1)
            for c in range(32):
                act.wait_ge(S.conv4_ready, c + 1)
                dst = (xsT if c < 16 else bcT)[:, c % 16, :]
                A(dst, ctmp[:, c // 2 % 4, c % 2 * T:(c % 2 + 1) * T], ACT.Silu).then_inc(S.xbc_ready, 1)
            act.wait_ge(S.acs_ready, 1)
            A(dec0, dec0, ACT.Exp).then_inc(S.decay2_done, 1)
            A(eacs, nacs[:, 32:64], ACT.Exp, scale=-1.0).then_inc(S.decay2_done, 1)
            for n in range(10):
                act.wait_ge(S.sT_done, n + 1)
                if n < 8:
                    dst = xtok[:, n // 4, n % 4 * 512:(n % 4 + 1) * 512]
                else:
                    dst = Btok[:, (n - 8) * 4:(n - 7) * 4, :].rearrange("p g n -> p (g n)")
                A(dst, PS[:, n % 4, :], ACT.Copy).then_inc(S.sT_ready, 1)
            for g in range(G):
                for t in range(TT):
                    n = 2 * g + t
                    b = n % 2
                    act.wait_ge(S.g_cb, n + 1)
                    if n >= 2:
                        act.wait_ge(S.g_w, n - 1)
                    for r in range(4):
                        h = 4 * g + r
                        last = A(LT[:, b, r, :], PS[:, b, r * P:(r + 1) * P], ACT.Exp,
                                 bias=nacs[:, t * 32 + h:t * 32 + h + 1])
                    last.then_inc(S.g_lt, 1)
                    if t == 0:
                        act.wait_ge(S.g_st, g + 1)
                        if g >= 2:
                            act.wait_ge(S.g_y, n - 2)
                        A(stT[:, g % 2, :], PS[:, 6, 0:256], ACT.Copy).then_inc(S.g_stready, 1)
            act.wait_ge(S.ys_ready, 1)
            A(SQ, y_s.rearrange("p t d -> p (t d)"), ACT.Square).then_inc(S.ys_sq, 1)
            act.wait_ge(S.ys_ms, 1)
            A(ysstd, ysms, ACT.Sqrt).then_inc(S.ys_std, 1)
            for n in range(8):
                act.wait_ge(S.ysT_done, n + 1)
                for j in range(2):
                    c = 2 * n + j
                    A(ysT[:, c, :], PS[:, n % 4, j * T:(j + 1) * T], ACT.Copy, scale=pc("ssm_norm", c)).then_inc(S.ysT_ready, 1)
            norm(9)
            ffn(4)

        @block.vector
        def _(dve):
            v = nc.vector
            steps = [0]

            def step(ins):
                steps[0] += 1
                ins.then_inc(S.dve_step, 1)
                dve.wait_ge(S.dve_step, steps[0])

            def norm(k):
                src = NORM_SRC.get(k, X)
                dve.wait_ge(S.ssq_ready, 2 * (k + 1))
                v.tensor_scalar(ms, ssq, 1.0 / D, 1e-6, ALU.mult, ALU.add).then_inc(S.ms_ready, 1)
                dve.wait_ge(S.std_ready, k + 1)
                step(v.reciprocal(rstd, std))
                for t in range(TT):
                    v.tensor_scalar(xn[:, t, :], src[:, t, :], rstd[:, t:t + 1], None, ALU.mult).then_inc(S.xn_ready, 1)
                dst = NORM_DST.get(k, hT)
                for c in range(4, 8):
                    dve.wait_ge(S.xT_ready, 4 * k + c // 2 + 1)
                    v.tensor_scalar(dst[:, c, :], PS[:, 4 + c // 2, c % 2 * T:(c % 2 + 1) * T], pc("gain", 8 * k + c), None, ALU.mult)\
                        .then_inc(S.hT_ready, 1)

            def ynorm(k, bank, gain):
                dve.wait_ge(S.yssq_ready, 4 * (k + 1))
                step(v.tensor_tensor(yms, yssq[:, 0:4:2], yssq[:, 1:4:2], ALU.add))
                v.tensor_scalar(yms, yms, 1.0 / D, 1e-6, ALU.mult, ALU.add).then_inc(S.yms_ready, 1)
                dve.wait_ge(S.ystd_ready, k + 1)
                step(v.reciprocal(yrstd, ystd))
                for t in range(TT):
                    for h in range(2):
                        last = v.scalar_tensor_tensor(xn[:, t, h * 512:(h + 1) * 512], PS[:, bank + 2 * t + h, :],
                                                      yrstd[:, t:t + 1], row(gain)[:, h * 512:(h + 1) * 512],
                                                      ALU.mult, ALU.mult)
                step(last)
                for t in range(TT):
                    last = v.tensor_tensor(X[:, t, :], X[:, t, :], xn[:, t, :], ALU.add)
                last.then_inc(S.x_ready, 1)

            def residual(bank, last_slot, factor):
                last_slot.wait_used(dve)
                for t in range(TT):
                    for h in range(2):
                        hs = slice(h * 512, (h + 1) * 512)
                        last = v.scalar_tensor_tensor(X[:, t, hs], PS[:, bank + 2 * t + h, :], factor, X[:, t, hs],
                                                      ALU.mult, ALU.add)
                last.then_inc(S.x_ready, 1)

            def ffn(f):
                def hidden(b, i=0, ii=0):
                    ffn_slot(f, "U", b, i).wait_used(dve)
                    dve.wait_ge(S.silu_ready, ii * 2 + (NB * f + b + 1))
                    if b >= 2:
                        ffn_slot(f, "D", b - 2, i).wait_used(dve)
                    v.tensor_tensor(gact[:, b % 2, :, :].rearrange("p j t -> p (j t)"), sg[:, b % 2, :],
                                    PS[:, 5 + 2 * (b % 2), :], ALU.mult).then_inc(S.act_ready, 1)
                hidden(0)
                hidden(1)
                with dve.Fori(0, (NB - 3) // 2) as i:
                    for b in (2, 3):
                        hidden(b, i, i)
                hidden(NB - 1)

            def attention(a, scale, causal):
                dve.wait_ge(S.score_done, a + 1)
                allps = PS[:, 0:4, :].rearrange("p b (s m) -> p (b s) m", s=2)
                if causal:
                    m4 = cn("causal").rearrange("p (o t m) -> p o t m", o=1, t=TT).broadcast_to([P, 4, TT, T])
                    step(v.tensor_tensor(PS[:, 0:4, :].rearrange("p h (t m) -> p h t m", t=TT),
                                         PS[:, 0:4, :].rearrange("p h (t m) -> p h t m", t=TT), m4, ALU.add))
                step(v.tensor_reduce(nmax, allps, AX.X, ALU.max))
                v.tensor_scalar(nmax, nmax, -scale, None, ALU.mult).then_inc(S.nmax_ready, 1)
                dve.wait_ge(S.exp_ready, a + 1)
                step(v.reciprocal(rsum, psum_))
                v.tensor_tensor(prob, prob, rsum.unsqueeze(2).broadcast_to([P, 8, T]), ALU.mult).then_inc(S.prob_ready, 1)
                dve.wait_ge(S.probT_done, a + 1)
                for h in (1, 3):
                    v.tensor_copy(probT[:, h, :, :], PS[:, 4 + h, :].rearrange("p (k t) -> p k t", k=2))\
                        .then_inc(S.probT_ready, 1)

            dve.wait_ge(S.params_loaded, 48)
            norm(0)
            norm(1)
            v.memset(pin[:, :, 0:1], 0.0).then_inc(S.pad_ready, 1)
            dve.wait_ge(S.pos_loaded, 16)
            step(v.tensor_copy(posf, pos_i[:]))
            tr = trig.rearrange("p (s t f) -> p s t f", s=2, t=TT)
            for t in range(TT):
                for s in range(2):
                    last = v.tensor_scalar(tr[:, s, t, :], cn("inv_freq"), posf[:, t:t + 1], None, ALU.mult)
            step(last)
            magic = 12582912.0
            for s in range(2):
                last = v.tensor_scalar(turns[:, s * 128:(s + 1) * 128], trig[:, s * 128:(s + 1) * 128],
                                       1.0 / (2 * math.pi), 0.25 * s, ALU.mult, ALU.add)
            step(last)
            step(v.tensor_scalar(turns, turns, magic, None, ALU.add))
            step(v.tensor_scalar(turns, turns, magic, None, ALU.subtract))
            for part in (6.28125, 0.0019350051879882812, 3.019915981956753e-07):
                step(v.scalar_tensor_tensor(trig, turns, -part, trig, ALU.mult, ALU.add))
            step(v.tensor_scalar(trig[:, 128:256], trig[:, 128:256], math.pi / 2, None, ALU.add))
            v.tensor_scalar(trig, trig, 3.1415925, -3.1415925, ALU.min, ALU.max).then_inc(S.ang_ready, 1)

            dve.wait_ge(S.pin_ready, 4)
            step(v.tensor_tensor(glu, glu, usig, ALU.mult))

            for n in range(7):
                dve.wait_ge(S.pin_ready, 5 + n)
                c = 2 * n
                step(v.tensor_tensor(tshift.rearrange("p (c t) -> p c t", c=2), pin[:, c:c + 2, 0:T],
                                     pin[:, c:c + 2, 1:T + 1], ALU.subtract))
                for j in range(2):
                    last = v.scalar_tensor_tensor(Q[:, c + j, :], tshift[:, j * T:(j + 1) * T], pc("mu", c + j),
                                                  pin[:, c + j, 1:T + 1], ALU.mult, ALU.add)
                last.then_inc(S.q_mixed, 1)
                dve.wait_ge(S.q_mixed, n + 1)
            for c in range(4):
                last = v.tensor_scalar(kk[:, c * T:(c + 1) * T], Q[:, 4 + c, :], pc("k_k", c), None, ALU.mult)
            step(last)
            v.tensor_tensor(tmp, kk, kk, ALU.mult).then_inc(S.kksq_ready, 1)
            dve.wait_ge(S.kksum_done, 1)
            v.tensor_scalar(tmp, PS[:, 4:6, :].rearrange("p a b -> p (a b)"), 1e-24, None, ALU.max)\
                .then_inc(S.kkmax_ready, 1)
            dve.wait_ge(S.kk_std, 1)
            step(v.reciprocal(tmp, tmp))
            step(v.tensor_tensor(kk, kk, tmp, ALU.mult))
            dve.wait_ge(S.a_ready, 1)
            for c in range(4):
                last = v.tensor_scalar(tmp[:, c * T:(c + 1) * T], a_f[:, c * T:(c + 1) * T], -1.0, pc("k_a", c),
                                       ALU.add, ALU.mult)
            step(last)
            step(v.scalar_tensor_tensor(k_f, tmp, 1.0, k_f, ALU.add, ALU.mult))
            for c in range(4):
                cs = slice(c * T, (c + 1) * T)
                last = v.scalar_tensor_tensor(tmp[:, cs], r_f[:, cs], pc("r_k", c), k_f[:, cs], ALU.mult, ALU.mult)
            last.then_inc(S.bonus_in, 1)
            step(v.memset(Pc[:, :, 0:1], 1.0))
            dve.wait_ge(S.decay_ready, 1)
            for s in range(16):
                last = v.tensor_tensor_scan(Pc[:, s, 1:65], decay[:, s * 64:(s + 1) * 64], cn("zeros"), 1.0,
                                            ALU.mult, ALU.add)
            step(last)
            Pinc, Pexc = Pc[:, :, 1:65], Pc[:, :, 0:64]
            c16 = lambda ap: ap.rearrange("p (s t) -> p s t", s=16)
            v.scalar_tensor_tensor(a_f, kk, -1.0, a_f, ALU.mult, ALU.mult)
            step(v.reciprocal(c16(invP), Pinc))
            v.tensor_tensor(c16(kk), c16(kk), Pexc, ALU.mult)
            v.tensor_tensor(c16(r_f), c16(r_f), Pinc, ALU.mult)
            v.tensor_tensor(k_f, k_f, invP, ALU.mult)
            v.tensor_tensor(a_f, a_f, invP, ALU.mult).then_inc(S.ab_ready, 1)
            dve.wait_ge(S.bonus_sum_done, 1)
            v.tensor_tensor(bonus, PS[:, 4:6, :].rearrange("p a b -> p (a b)"), v_f, ALU.mult)
            dve.wait_ge(S.tok_done, 1)
            for i, (bank, dst, t) in enumerate(((0, V_t, 0), (1, V_t, 1), (2, K_t, 0), (3, K_t, 1), (6, B_t, 0), (7, B_t, 1))):
                if i % 2 == 1:
                    v.tensor_copy(dst[:, t, :], PS[:, bank, :]).then_inc(S.tok_ready, 1)

            h8 = lambda ap: ap.rearrange("p (h t) -> p h t", h=8)
            b8 = lambda m: m.unsqueeze(1).broadcast_to([P, 8, 64])
            taps = [(back, c) for back in range(31) for c in range(4)]

            def tap_steps(n):
                for _ in range(min(n, len(taps))):
                    back, c = taps.pop(0)
                    cs = slice(c * T, (c + 1) * T)
                    weight = pc("conv_w", (30 - back) * 4 + c)
                    if back == 0:
                        last_ = v.tensor_scalar(conv[:, cs], glu[:, cs], weight, pc("conv_b", c), ALU.mult, ALU.add)
                    else:
                        late = conv[:, c * T + back:(c + 1) * T]
                        last_ = v.scalar_tensor_tensor(late, glu[:, c * T:(c + 1) * T - back], weight, late,
                                                       ALU.mult, ALU.add)
                    if c == 3 and taps:
                        step(last_)
                    elif not taps:
                        last_.then_inc(S.conv_ready, 1)

            for t in range(TT):
                MT, RKT, RBT, XiT = MTs[t], RKTs[t], RBTs[t], XiTs[t]
                dve.wait_ge(S.gram_done, t + 1)
                grams = lambda bank, at: PS[:, bank:bank + 2, at:at + 256].rearrange("p e (c t) -> p e c t", c=4)
                heads = lambda ap: ap.rearrange("p (c e t) -> p e c t", c=4, e=2)
                m24 = lambda m: m.unsqueeze(1).unsqueeze(1).broadcast_to([P, 2, 4, 64])
                v.tensor_copy(heads(NL), grams(0, 0))
                v.tensor_tensor(heads(XiT), grams(0, 256), m24(cn("off1T")), ALU.mult)
                v.tensor_tensor(heads(MT), grams(2, 0), m24(cn("s_lt_t")), ALU.mult)
                v.tensor_tensor(heads(RKT), grams(2, 256), m24(cn("s_le_t")), ALU.mult)
                step(v.tensor_tensor(heads(RBT), grams(6, 0), m24(cn("s_le_t")), ALU.mult))
                v.tensor_tensor(h8(XiT), h8(XiT), b8(cn("eye64")), ALU.add)
                step(v.tensor_tensor(h8(Xi), h8(NL), b8(cn("off", 0, 64)), ALU.mult))
                v.tensor_tensor(h8(Xi), h8(Xi), b8(cn("eye64")), ALU.add).then_inc(S.gram_ready, 1)
                v.tensor_tensor(h8(Loff), h8(NL), b8(cn("off", 64, 64)), ALU.mult).then_inc(S.inv_ready, 1)
                tap_steps(4)
                for lv in range(5):
                    n = 5 * t + lv
                    dve.wait_ge(S.invx_done, n + 1)
                    last = v.tensor_tensor(XiT, XiT, PS[:, 1, :], ALU.add)
                    if lv < 4:
                        v.tensor_tensor(Xi, Xi, PS[:, 2, :], ALU.add)
                        v.tensor_tensor(h8(Loff), h8(NL), b8(cn("off", (lv + 2) * 64, 64)), ALU.mult).then_inc(S.inv_ready, 1)
                    else:
                        last.then_inc(S.inv_ready, 1)
                    tap_steps(8)
            tap_steps(len(taps))
            for g in range(NCK - 1):
                dve.wait_ge(S.z_done, g + 1)
                for c in range(4):
                    last = v.scalar_tensor_tensor(Zn[:, g % 2, c, :], PS[:, 3, c * P:(c + 1) * P], Pc[:, c * 4 + g, 64:65],
                                                  cn("pair"), ALU.mult, ALU.mult)
                last.then_inc(S.z_ready, 1)
            dve.wait_ge(S.convT_done, 1)
            for t in range(TT):
                last = v.bn_stats(bst[:, 6 * t:6 * t + 6], PS[:, 4 + t, :])
            step(last)
            for t in range(TT):
                last = v.bn_aggr(bag[:, 2 * t:2 * t + 2], bst[:, 6 * t:6 * t + 6])
            step(last)
            v.tensor_scalar(cvar, bag[:, 1:4:2], 1e-5, None, ALU.add).then_inc(S.cvar_ready, 1)
            dve.wait_ge(S.cstd_ready, 1)
            step(v.reciprocal(crstd, cstd))
            for t in range(TT):
                v.tensor_scalar(tmp[:, t * 512:(t + 1) * 512], PS[:, 4 + t, :], bag[:, 2 * t:2 * t + 1],
                                crstd[:, t:t + 1], ALU.subtract, ALU.mult).then_inc(S.cn_ready, 1)
            dve.wait_ge(S.yc_ready, 4)
            y16 = Y.rearrange("p t (h d) -> p (t h) d", h=8)
            b16 = lambda s_: s_.unsqueeze(2).broadcast_to([P, 16, 64])
            s16 = sqr.rearrange("p (s d) -> p s d", s=16)
            step(v.tensor_reduce(ymean, y16, AX.X, ALU.add))
            step(v.tensor_scalar(ymean, ymean, 1.0 / 64, None, ALU.mult))
            step(v.tensor_tensor(y16, y16, b16(ymean), ALU.subtract))
            step(v.tensor_tensor(s16, y16, y16, ALU.mult))
            step(v.tensor_reduce(ynvar, s16, AX.X, ALU.add))
            v.tensor_scalar(ynvar, ynvar, 1.0 / 64, 64e-5, ALU.mult, ALU.add).then_inc(S.ynvar_ready, 1)
            dve.wait_ge(S.ynstd_ready, 1)
            step(v.reciprocal(ynrstd, ynstd))
            v.tensor_tensor(y16, y16, b16(ynrstd), ALU.mult).then_inc(S.yn_ready, 1)
            dve.wait_ge(S.ynT_done, 1)
            for c in range(4):
                last = v.tensor_scalar(YT[:, 4 + c, :], PS[:, c // 2, c % 2 * T:(c % 2 + 1) * T], pc("lnx_g", c),
                                       pc("lnx_b", c), ALU.mult, ALU.add)
            step(last)
            yt = YT[:, 4:8, :].rearrange("p c t -> p (c t)")
            step(v.tensor_tensor(yt, yt, bonus, ALU.add))
            v.tensor_tensor(yt, yt, g_f, ALU.mult).then_inc(S.yT_ready, 1)
            ynorm(0, 0, "g1")
            norm(2)
            attention(0, 1.0 / 16, False)
            ynorm(1, 4, "g3")
            norm(3)
            ffn(0)
            ynorm(2, 0, "g5")
            norm(4)
            ffn(1)
            residual(0, ffn_slot(1, "D", NB - 1), 0.5)
            norm(5)
            hd = lambda ap: ap.rearrange("p (s d) -> p s d", s=16)
            for q in range(2):
                dve.wait_ge(S.qk_sq, q + 1)
                qs = slice(q * 16, (q + 1) * 16)
                step(v.tensor_reduce(qkms[:, qs], hd(rt1), AX.X, ALU.add))
                v.tensor_scalar(qkms[:, qs], qkms[:, qs], 1.0 / 128, 1e-6, ALU.mult, ALU.add).then_inc(S.qk_ms, 1)
            for q, (src, gain) in enumerate(((q_r, "q_gain"), (k_r, "k_gain"))):
                dve.wait_ge(S.qk_std, q + 1)
                qs = slice(q * 16, (q + 1) * 16)
                step(v.reciprocal(qkr[:, qs], qkstd[:, qs]))
                step(v.tensor_tensor(hd(src), hd(src), qkr[:, qs].unsqueeze(2).broadcast_to([P, 16, 128]), ALU.mult))
                step(v.tensor_tensor(hd(src), hd(src), row(gain).unsqueeze(1).broadcast_to([P, 16, 128]), ALU.mult))
                s4 = src.rearrange("p (t h d) -> p t h d", t=TT, h=8)
                w1 = rt1.rearrange("p (t h d) -> p t h d", t=TT, h=8)
                w2 = rt2.rearrange("p (t h d) -> p t h d", t=TT, h=8)
                for t in range(TT):
                    sin = tr[:, 0, t, :].unsqueeze(1).broadcast_to([P, 8, 64])
                    cos = tr[:, 1, t, :].unsqueeze(1).broadcast_to([P, 8, 64])
                    v.tensor_tensor(w1[:, t, :, 0:64], s4[:, t, :, 0:64], cos, ALU.mult)
                    v.tensor_tensor(w1[:, t, :, 64:128], s4[:, t, :, 64:128], cos, ALU.mult)
                    v.tensor_tensor(w2[:, t, :, 0:64], s4[:, t, :, 64:128], sin, ALU.mult)
                    last = v.tensor_tensor(w2[:, t, :, 64:128], s4[:, t, :, 0:64], sin, ALU.mult)
                step(last)
                hs_ = lambda ap, a: hd(ap)[:, :, a:a + 64]
                v.tensor_tensor(hs_(src, 0), hs_(rt1, 0), hs_(rt2, 0), ALU.subtract)
                v.tensor_tensor(hs_(src, 64), hs_(rt1, 64), hs_(rt2, 64), ALU.add).then_inc(S.qk_roped, 1)
            attention(1, 128 ** -0.5, True)
            attention(2, 128 ** -0.5, True)
            residual(4, Slot(FIRST["attn_o"] + 3), 1.0)
            norm(6)
            ffn(2)
            residual(0, ffn_slot(2, "D", NB - 1), 0.5)
            norm(7)
            ffn(3)
            residual(0, ffn_slot(3, "D", NB - 1), 0.5)
            norm(8)
            dve.wait_ge(S.dt_done, 1)
            for t in range(TT):
                last = v.tensor_tensor(dt_[:, t * 32:(t + 1) * 32], PS[:, 4 + t, 0:32], row("dt_bias"), ALU.add)
            step(last)
            step(v.tensor_scalar(dte, dt_, -1.0, None, ALU.mult))
            v.tensor_tensor(dte, dte, dt_, ALU.max).then_inc(S.dt_abs, 1)
            dve.wait_ge(S.dt_ln, 1)
            step(v.scalar_tensor_tensor(dt_, dt_, 0.0, dte, ALU.max, ALU.add))
            dve.wait_ge(S.aneg, 1)
            for t in range(TT):
                last = v.scalar_tensor_tensor(dta[:, t, :], dt_[:, t * 32:(t + 1) * 32], -1.0, aexp, ALU.mult, ALU.mult)
            last.then_inc(S.dta_ready, 1)
            dve.wait_ge(S.acs_done, 1)
            step(v.tensor_scalar(nacs, PS[:, 6, 0:64], -1.0, None, ALU.mult))
            v.tensor_tensor(dec0, nacs[:, 0:32], PS[:, 6, 64:96], ALU.add).then_inc(S.acs_ready, 1)
            for c in range(32):
                Slot(FIRST["xbc"] + c // 2).wait_used(dve)
                if c >= 8:
                    dve.wait_ge(S.xbc_ready, c - 7)
                ps = PS[:, 4 + c // 2 % 4, c % 2 * T:(c % 2 + 1) * T]
                dst = ctmp[:, c // 2 % 4, c % 2 * T:(c % 2 + 1) * T]
                step(v.tensor_scalar(dst, ps, pc("sconv_w", 3 * 32 + c), pc("sconv_b", c), ALU.mult, ALU.add))
                for back in (1, 2):
                    step(v.scalar_tensor_tensor(dst[:, back:T], ps[:, 0:T - back], pc("sconv_w", (3 - back) * 32 + c),
                                                dst[:, back:T], ALU.mult, ALU.add))
                v.scalar_tensor_tensor(dst[:, 3:T], ps[:, 0:T - 3], pc("sconv_w", c), dst[:, 3:T], ALU.mult,
                                       ALU.add).then_inc(S.conv4_ready, 1)
            dve.wait_ge(S.sT_ready, 10)
            r4 = lambda ap: ap.rearrange("p (r d) -> p r d", r=4)
            b4 = lambda ap: ap.unsqueeze(2).broadcast_to([P, 4, 64])
            dve.wait_ge(S.decay2_done, 2)
            def finish(n):
                g, t = n // 2, n % 2
                b = n % 2
                gs = slice(g * 256, (g + 1) * 256)
                dve.wait_ge(S.g_y, n + 1)
                if n:
                    dve.wait_ge(S.g_yev, n)
                step(v.tensor_tensor(r4(ytmp), r4(xtok[:, t, gs]), b4(row("d_skip")[:, 4 * g:4 * g + 4]), ALU.mult))
                if t:
                    step(v.tensor_tensor(ytmp, ytmp, PS[:, 4 + b, 0:256], ALU.add))
                    step(v.tensor_tensor(r4(y_s[:, t, gs]), r4(PS[:, 7, 0:256]), b4(eacs[:, 4 * g:4 * g + 4]), ALU.mult))
                    v.tensor_tensor(y_s[:, t, gs], y_s[:, t, gs], ytmp, ALU.add).then_inc(S.g_yev, 1)
                else:
                    v.tensor_tensor(y_s[:, t, gs], ytmp, PS[:, 4 + b, 0:256], ALU.add).then_inc(S.g_yev, 1)

            for n in range(2 * G):
                g, t = n // 2, n % 2
                b = n % 2
                gs = slice(g * 256, (g + 1) * 256)
                if n >= 2:
                    dve.wait_ge(S.g_y, n - 1)
                step(v.tensor_tensor(r4(xdt[:, b, :]), r4(xtok[:, t, gs]),
                                     b4(dt_[:, t * 32 + 4 * g:t * 32 + 4 * g + 4]), ALU.mult))
                if t == 0:
                    v.tensor_tensor(r4(xdec[:, g % 2, :]), r4(xdt[:, b, :]), b4(dec0[:, 4 * g:4 * g + 4]), ALU.mult)\
                        .then_inc(S.g_xdec, 1)
                dve.wait_ge(S.g_lt, n + 1)
                v.tensor_tensor(Wd[:, b, :, :], LT[:, b, :, :], PS[:, 2 + b, 0:P].unsqueeze(1).broadcast_to([P, 4, P]),
                                ALU.mult).then_inc(S.g_w, 1)
                if n >= 1:
                    finish(n - 1)
            finish(2 * G - 1)
            dve.wait_ge(S.g_yev, 2 * G)
            yf = y_s.rearrange("p t d -> p (t d)")
            v.tensor_tensor(yf, yf, z_r, ALU.mult).then_inc(S.ys_ready, 1)
            dve.wait_ge(S.ys_sq, 1)
            g16 = lambda ap: ap.rearrange("p (s d) -> p s d", s=16)
            step(v.tensor_reduce(ysms, g16(SQ), AX.X, ALU.add))
            v.tensor_scalar(ysms, ysms, 1.0 / 256, 1e-6, ALU.mult, ALU.add).then_inc(S.ys_ms, 1)
            dve.wait_ge(S.ys_std, 1)
            step(v.reciprocal(ysr, ysstd))
            v.tensor_tensor(g16(yf), g16(yf), ysr.unsqueeze(2).broadcast_to([P, 16, 256]), ALU.mult).then_inc(S.ysn_ready, 1)
            residual(4, Slot(FIRST["ssm_out"] + 7), 1.0)
            norm(9)
            ffn(4)
            residual(0, ffn_slot(4, "D", NB - 1), 0.5)


def constants():
    import numpy as np
    c = np.zeros((P, NC_), np.float32)

    def put(name, value):
        at, width = CAT[name]
        c[:, at:at + width] = np.asarray(value, np.float32).reshape(P, width)

    i, j = np.arange(P)[:, None], np.arange(P)[None, :]
    s, t = i % CK, np.arange(CK)[None, :]
    put("ident", i == j)
    put("pair", i // HD == j // HD)
    put("ones", np.ones((P, P)))
    put("upper", i <= j)
    put("future", np.where(j < i, -1e30, 0.0))
    q = np.arange(T)[None, :]
    put("causal", np.stack([np.where(q > i + P * tt, -1e30, 0.0) for tt in range(TT)], 1))
    put("s_lt_t", s < t)
    put("s_le_t", s <= t)
    put("eye64", s == t)

    def off(a, b, m):
        return (a > b) & (a // (2 * m) == b // (2 * m)) & (a // m != b // m)

    put("off1T", off(t, s, 1))
    put("off", np.stack([off(s, t, 2 ** lv) for lv in range(6)], 1))
    put("inv_freq", np.broadcast_to(np.float32(10000.0) ** (-np.arange(64, dtype=np.float32) / np.float32(64)), (P, 64)))
    return c


def kernel(**inputs):
    import numpy as np
    import concourse.bacc as bacc
    from concourse.bass_utils import run_bass_kernel_spmd

    a = {name: np.asarray(value) for name, value in inputs.items()}

    def feat(w):
        n = w.shape[1] // 256
        return w.reshape(KC, P, n, 256).transpose(2, 1, 0, 3).reshape(n, P, 2048)

    def rows(w):
        n = w.shape[0] // 256
        return w.reshape(n, 2, P, 1024).transpose(0, 2, 1, 3).reshape(n, P, 2048)

    def ffn(gate, up, down):
        g, u, d = feat(gate), feat(up), rows(down)
        order = [g[0], u[0]]
        for b in range(1, NB):
            order += [g[b], u[b], d[b - 1]]
        return np.stack(order + [d[NB - 1]])

    wkv, gu, qkv, win2 = a["wkv"][0], a["w_gu"][0], a["attn_w_qkv_2"][0], a["ssm_w_in_2"][0]

    def ffn2(which, i):
        return ffn(a[f"ffn{which}_w_gate_2"][i], a[f"ffn{which}_w_up_2"][i], a[f"ffn{which}_w_down_2"][i])

    parts = {"w_in": feat(a["w_in_first"]), "km": feat(wkv[:, :D]), "vm": rows(wkv[:, D:]), "w_out": rows(a["w_out"][0]),
             "wq": feat(a["wq"][0]), "wo": rows(a["wo"][0]), "ffn0": ffn(gu[:, :FF], gu[:, FF:], a["w_down"][0]),
             "ffn1": ffn2(1, 0), "q": rows(qkv[:, :D]), "k": rows(qkv[:, D:2 * D]), "v": rows(qkv[:, 2 * D:]),
             "attn_o": rows(a["attn_w_o_2"][0]), "ffn2": ffn2(2, 0), "ffn3": ffn2(1, 1),
             "z": np.concatenate([rows(win2[:, :1024]), rows(win2[:, 1024:2048])]),
             "xbc": feat(win2[:, 2048:6144]), "ssm_out": rows(a["ssm_w_out_2"][0]), "ffn4": ffn2(2, 1)}
    W = np.concatenate([parts[name] for name, _ in STREAM])
    assert W.shape == (NSLOTS, P, 2048)

    def col(w):
        return w.reshape(-1, P).T

    g = a["norm_gains"][0]
    f1, mx, f2 = a["ffn1_norm_2"], a["mix_norm_2"], a["ffn2_norm_2"]
    gains = [g[0], a["mem_norm_g"], g[2], g[4], f1[0], mx[0], f2[0], f1[1], mx[1], f2[1]]
    wa = np.concatenate([a["w_up"][0], a["a_up"][0]], 0)
    wdt = win2[:, 6144:].reshape(KC, P, 32).transpose(1, 0, 2).reshape(P, 256)
    values = {"gain": col(np.concatenate(gains)), "ssm_norm": col(a["ssm_norm_2"][0]), "mu": col(a["mu_first"]),
              "w0": col(a["w0"][0]), "a0": col(a["a0"][0]), "k_k": col(a["k_k"][0]), "k_a": col(a["k_a"][0]),
              "r_k": col(a["r_k"][0].reshape(-1)), "lnx_g": col(a["lnx_g"][0]), "lnx_b": col(a["lnx_b"][0]),
              "conv_w": col(a["conv_w"][0].reshape(-1)), "conv_b": col(a["conv_b"][0]), "ln_g": col(a["conv_ln_g"][0]),
              "ln_b": col(a["conv_ln_b"][0]), "sconv_w": col(a["ssm_conv_w_2"][0].reshape(-1)),
              "sconv_b": col(a["ssm_conv_b_2"][0]), "wa_up": wa, "g_up": a["g_up"][0], "w_dt": wdt}
    cols = np.ascontiguousarray(np.concatenate([values[n] for n, _ in PCOLS], 1))
    rvals = {"g1": g[1], "g3": g[3], "g5": g[5], "q_gain": a["attn_q_norm_2"][0], "k_gain": a["attn_k_norm_2"][0],
             "dt_bias": a["ssm_dt_bias_2"][0], "a_log": a["ssm_a_log_2"][0], "d_skip": a["ssm_d_2"][0]}
    rws = np.concatenate([rvals[n] for n, _ in PROWS])[None, :]
    arrays = {"W": W, "cols": cols, "rows": rws, "consts": constants(), "x": np.ascontiguousarray(a["x"][0]),
              "mem": np.ascontiguousarray(a["mem"][0]),
              "pos": np.ascontiguousarray(a["positions_2"][0].reshape(TT, P).T.astype(np.int32))}

    nc = bacc.Bacc("TRN2", target_bir_lowering=False, num_devices=1)
    ins = [nc.dram_tensor(n, v.shape, mybir.dt.from_np(v.dtype), kind="ExternalInput").ap() for n, v in arrays.items()]
    out = nc.dram_tensor("out", (T, D), F32, kind="ExternalOutput").ap()
    build_program(nc, *ins, out)
    r = run_bass_kernel_spmd(nc, [arrays], core_ids=[0])
    return r.results[0]["out"].reshape(1, T, D)
```

```python
import math
from collections import namedtuple
from contextlib import ExitStack

import concourse.bass as bass
from concourse import mybir

F32 = mybir.dt.float32
F32R = mybir.dt.float32r
I32 = mybir.dt.int32
ALU = mybir.AluOpType
ACT = mybir.ActivationFunctionType
AX = mybir.AxisListType

P = 128
T = 256
TT = T // P
D = 1024
KC = D // P
FF = 2816
NB = FF // 256
HD = 64
CK = 64
NCK = T // CK
G = 8
R = 3
H = 4
LOOP = 12
DECAY = math.exp(-0.5)

STREAM = [("w_in", 11), ("w_out", 4), ("km", 4), ("vm", 4), ("wq", 4), ("wo", 4), ("ffn0", 33), ("ffn1", 33),
          ("q", 4), ("k", 4), ("v", 4), ("attn_o", 4), ("ffn2", 33), ("ffn3", 33),
          ("z", 8), ("xbc", 16), ("ssm_out", 8), ("ffn4", 33)]
FIRST = {}
_n = 0
for _name, _count in STREAM:
    FIRST[_name] = _n
    _n += _count
NSLOTS = _n

PCOLS = [("gain", 80), ("ssm_norm", 16), ("mu", 14), ("w0", 4), ("a0", 4), ("k_k", 4), ("k_a", 4), ("r_k", 4),
         ("lnx_g", 4), ("lnx_b", 4), ("conv_w", 124), ("conv_b", 4), ("ln_g", 4), ("ln_b", 4),
         ("sconv_w", 128), ("sconv_b", 32), ("wa_up", 512), ("g_up", 512), ("w_dt", 256)]
PROWS = [("q_gain", 128), ("k_gain", 128), ("dt_bias", 32), ("a_log", 32),
         ("d_skip", 32)]
CCOLS = [("ident", 128), ("pair", 128), ("ones", 128), ("upper", 128), ("future", 128), ("causal", 512),
         ("s_lt_t", 64), ("s_le_t", 64), ("eye64", 64), ("off1T", 64), ("off", 384), ("inv_freq", 64), ("zeros", 64)]


def offsets(table):
    at, out = 0, {}
    for name, width in table:
        out[name] = (at, width)
        at += width
    return out, at


PAT, NP_ = offsets(PCOLS)
RAT, NR_ = offsets(PROWS)
CAT, NC_ = offsets(CCOLS)


def build_program(nc, W, cols, rows, post_gains, consts, x_in, mem_in, pos_in, out):
    with ExitStack() as ctx:
        def sb(name, words, dt=F32):
            return ctx.enter_context(nc.sbuf_tensor(name, [P, words], dt))

        def sem(name):
            return ctx.enter_context(nc.semaphore(name))

        raw = sb("raw_weights", R * 2048)[:].rearrange("p (h n) -> p h n", n=1024)
        w_hi = sb("w_hi", H * 1024, F32R)[:].rearrange("p (h n) -> p h n", n=1024)
        w_lo = sb("w_lo", H * 1024, F32R)[:].rearrange("p (h n) -> p h n", n=1024)
        h_hi = sb("h_hi", KC * T, F32R)[:].rearrange("p (c t) -> p c t", c=KC)
        h_lo = sb("h_lo", KC * T, F32R)[:].rearrange("p (c t) -> p c t", c=KC)
        g_hi = sb("g_hi", 1024, F32R)[:].rearrange("p (q j t) -> p q j t", q=2, j=2)
        g_lo = sb("g_lo", 1024, F32R)[:].rearrange("p (q j t) -> p q j t", q=2, j=2)
        X = sb("x_resid", TT * D)[:].rearrange("p (t d) -> p t d", t=TT)
        xn_t = sb("x_normed", TT * D)
        xn = xn_t[:].rearrange("p (t d) -> p t d", t=TT)
        sg_t = sb("silu_gate", 1024)
        sg = sg_t[:].rearrange("p (q n) -> p q n", q=2)
        post_gain = sb("post_gain", D)
        ptab = sb("ptab", NP_)
        rtab = sb("rtab", NR_)
        ctab = sb("ctab", NC_)
        small = sb("small", 1400)
        pos_i = sb("pos_i", TT, I32)
        ARENA = 21000
        arena = sb("arena", ARENA)
        PS = ctx.enter_context(nc.psum_tensor("PS", [P, 8, 512], F32))

        def pc(name, i=0, n=1):
            at = PAT[name][0] + i
            return ptab[:, at:at + n]

        def row(name):
            at, w = RAT[name]
            return rtab[:, at:at + w]

        def cn(name, i=0, n=None):
            at, w = CAT[name]
            n = w if n is None else n
            return ctab[:, at + i:at + i + n]

        ident = cn("ident")

        used_small = [0]

        def sm(n):
            used_small[0] += n
            assert used_small[0] <= 1400
            return small[:, used_small[0] - n:used_small[0]]

        ssq, ms, std, rstd = sm(2), sm(2), sm(2), sm(2)
        yssq, yms, ystd, yrstd = sm(4), sm(2), sm(2), sm(2)

        def region(at, words):
            assert at + words <= ARENA, (at, words)
            return arena[:, at:at + words]

        o = 0
        pin_r = region(o, 3598); o += 3598
        pin = pin_r.rearrange("p (c t) -> p c t", c=14)
        Pc = pin_r[:, 0:1040].rearrange("p (s t) -> p s t", s=16)
        tmp = pin_r[:, 1040:2064]
        bonus = pin_r[:, 2064:3088]
        Q_r = region(o, 3584); o += 3584
        Q = Q_r.rearrange("p (c t) -> p c t", c=14)
        r_f, k_f, v_f = Q_r[:, 0:1024], Q_r[:, 1024:2048], Q_r[:, 2048:3072]
        conv = region(o, 1024); o += 1024
        usig = conv
        MEM = region(o, 2048).rearrange("p (t d) -> p t d", t=TT)
        glu = region(o, 1024); o += 1024
        decay = region(o, 1024); o += 1024
        invP = decay
        a_f = region(o, 1024); o += 1024
        g_f = region(o, 1024); o += 1024
        kk = region(o, 1024); o += 1024
        V_t = region(o, 1024).rearrange("p (t d) -> p t d", t=TT); o += 1024
        K_t = xn_t[:, 0:1024].rearrange("p (t d) -> p t d", t=TT)
        B_t = xn_t[:, 1024:2048].rearrange("p (t d) -> p t d", t=TT)
        kept = [region(o + 512 * i, 512) for i in range(8)]; o += 8 * 512
        MTs, RKTs, RBTs, XiTs = kept[0:2], kept[2:4], kept[4:6], kept[6:8]
        NL, Xi = decay[:, 0:512], decay[:, 512:1024]
        Loff, Qi = sg_t[:, 0:512], sg_t[:, 512:1024]
        Zn = region(o, 1024).rearrange("p (q c v) -> p q c v", q=2, c=4); o += 1024
        RU, U = v_f[:, 0:512], v_f[:, 512:1024]
        Y = k_f.rearrange("p (t d) -> p t d", t=TT)
        sqr = a_f
        tshift = kk[:, 0:512]
        YF_r = xn_t[:]
        YF = YF_r.rearrange("p (c t) -> p c t", c=KC)
        qT = region(0, 2048).rearrange("p (c t) -> p c t", c=KC)
        kT2 = region(2048, 2048).rearrange("p (c t) -> p c t", c=KC)
        v2 = region(4096, 2048).rearrange("p (t d) -> p t d", t=TT)
        q_r = region(6144, 2048)
        k_r = region(8192, 2048)
        kmT = region(14336, 2048).rearrange("p (c t) -> p c t", c=KC)
        vm = region(16384, 2048).rearrange("p (t d) -> p t d", t=TT)
        prob = region(10240, 2048).rearrange("p (s m) -> p s m", s=8)
        probT = region(12288, 2048).rearrange("p (h k t) -> p h k t", h=4, k=2)
        rt1 = region(14336, 2048)
        rt2 = region(16384, 2048)
        o = 0
        xsT_r = region(o, 4096); o += 4096
        xsT = xsT_r.rearrange("p (c t) -> p c t", c=16)
        y_s = xsT_r.rearrange("p (t d) -> p t d", t=TT)
        bcT = region(o, 4096).rearrange("p (c t) -> p c t", c=16); o += 4096
        xtok_r = region(o, 4096); o += 4096
        xtok = xtok_r.rearrange("p (t d) -> p t d", t=TT)
        z_r = region(o, 4096); o += 4096
        z_s = z_r.rearrange("p (t d) -> p t d", t=TT)
        Btok = region(o, 1024).rearrange("p (g n) -> p g n", g=G); o += 1024
        ctmp = xn_t[:].rearrange("p (q n) -> p q n", q=4)
        LT = xn_t[:, 0:1024].rearrange("p (q r l) -> p q r l", q=2, r=4)
        Wd = xn_t[:, 1024:2048].rearrange("p (q r l) -> p q r l", q=2, r=4)
        xdt = region(o, 512).rearrange("p (q n) -> p q n", q=2); o += 512
        xdec = region(o, 512).rearrange("p (q n) -> p q n", q=2); o += 512
        stT = region(o, 512).rearrange("p (q n) -> p q n", q=2); o += 512
        ytmp = region(o, 256); o += 256
        SQ = region(4096, 4096)
        posf, trig, turns = sm(TT), sm(256), sm(256)
        nmax, psum_, rsum = sm(8), sm(8), sm(8)
        qkms, qkstd, qkr = sm(32), sm(32), sm(32)
        dta_r, dt_, dte, aexp = sm(64), sm(64), sm(64), sm(32)
        dta = dta_r.rearrange("p (t h) -> p t h", t=TT)
        nacs, dec0, eacs = sm(64), sm(32), sm(32)
        cvar, cstd, crstd, bst, bag = sm(2), sm(2), sm(2), sm(12), sm(4)
        ymean, ynvar, ynstd, ynrstd = sm(16), sm(16), sm(16), sm(16)
        ysms, ysstd, ysr = sm(16), sm(16), sm(16)

        NAMES = ("half_done hi_ready lo_ready hT_hi g_mult g_hi_ready yf_ready yf_hi o_hi o_ready ysT_hi conv1_ready gain_loaded gain_read "
                 "params_loaded x_loaded mem_loaded pos_loaded out_stored dve_step act_step "
                 "ssq_ready ms_ready std_ready xn_ready xT_ready hT_ready x_ready silu_ready act_ready "
                 "yssq_ready yms_ready ystd_ready pad_ready pin_ready usig_ready glu_ready q_mixed lora_ready "
                 "wa_done g_done decay_ready a_ready g_ready kmT_ready vm_ready "
                 "kkraw_ready kksq_ready kksum_done kkmax_ready kknorm_ready bonus_in bonus_sum_done "
                 "ab_ready tok_done tok_ready gram_done gram_ready invq_done invq_ready invx_done inv_ready "
                 "ru_done ru_ready u_done u_ready z_done z_ready yc_done yc_ready yn_sq ynvar_ready ynstd_ready "
                 "yn_ready ynT_done yT_ready conv_ready convT_done cvar_ready cstd_ready cn_ready cnT_done "
                 "convY_ready kk_std "
                 "score_done nmax_ready exp_ready prob_ready probT_done probT_ready o_done qT_ready "
                 "qk_evac qk_sq qk_ms qk_std qk_roped qkT_done qkT_ready v_ready ang_ready trig_ready "
                 "dt_done dt_abs dt_exp dt_ln aneg dta_ready acs_done acs_ready decay2_done "
                 "conv4_ready xbc_ready z_ready2 sT_done sT_ready g_cb g_lt g_w g_y g_st g_stready g_xdt g_xdec g_yev "
                 "ys_ready ys_sq ys_ms ys_std ysn_ready ysT_done ysT_ready").split()
        S = namedtuple("Signals", NAMES)(*[sem(n) for n in NAMES])
        loaded = [sem(f"loaded{r}") for r in range(R)]

        def done(eng, name, slot, i=0):
            eng.wait_ge(S.half_done, LOOP * i + 2 * (FIRST[name] + slot) + 2)

        def ffn_half(f, kind, b):
            at = {"G": 3 * b - 1 if b else 0, "U": 3 * b if b else 1, "D": 3 * b + 4 if b < NB - 1 else 32}[kind]
            return 2 * (FIRST[f"ffn{f}"] + at)

        block = ctx.enter_context(nc.Block())

        W3 = W.rearrange("s p (h n) -> s p h n", h=2)

        @block.gpsimd
        def _(pool):
            for k in range(3):
                if k:
                    pool.wait_ge(S.gain_read, k)
                pool.dma_start(post_gain[:], post_gains[k:k + 1, :].broadcast_to([P, D])).then_inc(S.gain_loaded, 16)
                if k == 0:
                    pool.wait_ge(S.conv_ready, 1)
                    pool.wait_ge(S.inv_ready, 12)
                    pool.dma_start(MEM, mem_in.rearrange("(t p) d -> p t d", p=P)).then_inc(S.mem_loaded, 16)

        @block.sync
        def _(sp):
            sp.dma_start(X, x_in.rearrange("(t p) d -> p t d", p=P)).then_inc(S.x_loaded, 16)
            for n in range(R):
                sp.dma_start(raw[:, 2 * n:2 * n + 2, :], W3[n]).then_inc(loaded[n], 16)
            with sp.Fori(1, NSLOTS // R) as i:
                for r in range(R):
                    sp.wait_ge(S.lo_ready, i * (2 * R) + (2 * r + 2 - 2 * R))
                    sp.dma_start(raw[:, 2 * r:2 * r + 2, :], W3[i * R + r]).then_inc(loaded[r], 16)
            for n in range(NSLOTS // R * R, NSLOTS):
                sp.wait_ge(S.lo_ready, 2 * (n - R) + 2)
                sp.dma_start(raw[:, 2 * (n % R):2 * (n % R) + 2, :], W3[n]).then_inc(loaded[n % R], 16)
            sp.wait_ge(S.x_ready, 9)
            sp.dma_start(out.rearrange("(t p) d -> p t d", p=P), X).then_inc(S.out_stored, 16)
            sp.wait_ge(S.out_stored, 16)

        @block.tensor
        def _(pe):
            mm = nc.tensor.matmul

            def norm(k, src=xn):
                pe.wait_ge(S.xn_ready, 2 * (k + 1))
                for c in range(KC):
                    for t in range(TT):
                        at = c % 2 * 256 + t * P
                        last = nc.tensor.transpose(PS[:, 4 + c // 2, at:at + P], src[:, t, c * P:(c + 1) * P], ident)
                    if c % 2:
                        last.then_inc(S.xT_ready, 1)

            def products(out, lhs, rhs, start, stop):
                mm(out, lhs[0], rhs[0], start=start, stop=False)
                mm(out, lhs[0], rhs[1], start=False, stop=False)
                return mm(out, lhs[1], rhs[0], start=False, stop=stop)

            def feat_half(n, bank, j, i=0, normed=None):
                pe.wait_ge(S.lo_ready, LOOP * i + n + 1)
                for c in range(KC):
                    if normed is not None and c % 2 == 0:
                        pe.wait_ge(S.hT_ready, 8 * normed + c + 2)
                    cs = slice(c * P, (c + 1) * P)
                    last = products(PS[:, bank, j * T:(j + 1) * T], (w_hi[:, n % H, cs], w_lo[:, n % H, cs]),
                                    (h_hi[:, c, :], h_lo[:, c, :]), c == 0, c == KC - 1)
                last.then_inc(S.half_done, 1)

            def feat_slot(n, bank, i=0, normed=None):
                feat_half(n, bank, 0, i, normed)
                feat_half(n + 1, bank, 1, i)

            def rows_half(n, hi, lo, bank, start, stop, i=0):
                pe.wait_ge(S.lo_ready, LOOP * i + n + 1)
                for t in range(TT):
                    ts = slice(t * P, (t + 1) * P)
                    for h in range(2):
                        hs = slice(h * 512, (h + 1) * 512)
                        last = products(PS[:, bank + 2 * t + h, :], (hi[:, ts], lo[:, ts]),
                                        (w_hi[:, n % H, hs], w_lo[:, n % H, hs]), start, stop)
                last.then_inc(S.half_done, 1)

            def rows_matrix(name, bank, n=4, first=0, normed=None):
                for j in range(2 * n):
                    if normed is not None:
                        pe.wait_ge(S.hT_ready, 8 * normed + j + 1)
                    rows_half(2 * (FIRST[name] + first) + j, h_hi[:, j % KC, :], h_lo[:, j % KC, :], bank, j == 0,
                              j == 2 * n - 1)

            def ffn(f):
                k = [3, 4, 6, 7, 9][f]

                def gate_up(b, i=0, ii=0):
                    if b >= 2:
                        pe.wait_ge(S.act_ready, ii * 2 + (NB * f + b - 1))
                    feat_slot(ffn_half(f, "G", b), 4 + 2 * (b % 2), i, None if b else k)
                    feat_slot(ffn_half(f, "U", b), 5 + 2 * (b % 2), i)

                def down(b, i=0, ii=0):
                    pe.wait_ge(S.act_ready, ii * 2 + (NB * f + b + 1))
                    for j in range(2):
                        rows_half(ffn_half(f, "D", b) + j, g_hi[:, b % 2, j, :], g_lo[:, b % 2, j, :], 0,
                                  b == 0 and j == 0, b == NB - 1 and j == 1, i)

                gate_up(0)
                gate_up(1)
                down(0)
                with pe.Fori(0, (NB - 3) // 2) as i:
                    for b in (1, 2):
                        gate_up(b + 1, i, i)
                        down(b, i, i)
                gate_up(NB - 1)
                down(NB - 2)
                down(NB - 1)

            def attention(a, src_q, src_k, src_v, dtiles, heads, half, hold):
                for h in range(4):
                    for t in range(TT):
                        s = 2 * h + t
                        for j in range(dtiles):
                            c = (half * 4 + h) * dtiles + j
                            last = mm(PS[:, s // 2, s % 2 * T:(s % 2 + 1) * T], src_q[:, c, t * P:(t + 1) * P],
                                      src_k[:, c, :], start=j == 0, stop=j == dtiles - 1)
                last.then_inc(S.score_done, 1)
                pe.wait_ge(S.prob_ready, a + 1)
                for h in range(4):
                    for m in range(2):
                        for t in range(TT):
                            at = m * T + t * P
                            last = nc.tensor.transpose(PS[:, 4 + h, at:at + P],
                                                       prob[:, 2 * h + t, m * P:(m + 1) * P], ident)
                last.then_inc(S.probT_done, 1)
                pe.wait_ge(S.probT_ready, 4 * (a + 1))
                for h in range(4):
                    for j in range(dtiles):
                        c = (half * 4 + h) * dtiles + j
                        o_ = h * dtiles + j
                        for m in range(2):
                            last = mm(PS[:, o_ // 2, o_ % 2 * T:(o_ % 2 + 1) * T], src_v[:, m, c * P:(c + 1) * P],
                                      probT[:, h, m, :], start=m == 0, stop=m == 1)
                last.then_inc(S.o_done, 1)

            pe.wait_ge(S.params_loaded, 48)
            norm(0)
            for n in range(11):
                if n >= 4:
                    pe.wait_ge(S.pin_ready, n - 3)
                feat_slot(2 * n, n % 4, 0, None if n else 0)
            pe.wait_ge(S.pin_ready, 11)
            pe.wait_ge(S.lora_ready, 3)
            for c in range(4):
                last = mm(PS[:, c // 2, c % 2 * T:(c % 2 + 1) * T], ptab[0:64, PAT["wa_up"][0] + c * P:PAT["wa_up"][0] + (c + 1) * P],
                          Q[0:64, 12, :], start=True, stop=True)
            for c in range(4):
                last = mm(PS[:, 2 + c // 2, c % 2 * T:(c % 2 + 1) * T],
                          ptab[64:128, PAT["wa_up"][0] + c * P:PAT["wa_up"][0] + (c + 1) * P],
                          Q[64:128, 12, :], start=True, stop=True)
            last.then_inc(S.wa_done, 1)
            for c in range(4):
                last = mm(PS[:, 6 + c // 2, c % 2 * T:(c % 2 + 1) * T], pc("g_up", c * P, P), Q[:, 13, :],
                          start=True, stop=True)
            last.then_inc(S.g_done, 1)
            pe.wait_ge(S.kksq_ready, 1)
            for c in range(2):
                last = mm(PS[:, 4 + c, :], cn("pair"), tmp[:, c * 512:(c + 1) * 512], start=True, stop=True)
            last.then_inc(S.kksum_done, 1)
            pe.wait_ge(S.bonus_in, 1)
            for c in range(2):
                last = mm(PS[:, 4 + c, :], cn("pair"), tmp[:, c * 512:(c + 1) * 512], start=True, stop=True)
            last.then_inc(S.bonus_sum_done, 1)
            pe.wait_ge(S.ab_ready, 1)
            pe.wait_ge(S.g_ready, 1)
            banks = [0, 1, 2, 3, 6, 7]
            for q, src in enumerate((v_f, k_f, a_f)):
                for t in range(TT):
                    for c in range(4):
                        last = nc.tensor.transpose(PS[:, banks[2 * q + t], c * P:(c + 1) * P],
                                                   src[:, c * T + t * P:c * T + (t + 1) * P], ident)
            last.then_inc(S.tok_done, 1)
            pe.wait_ge(S.tok_ready, 6)

            def chunks(t):
                for h in range(8):
                    for ch in range(2):
                        yield h, ch, h // 2, 64 * (h % 2), 64 * ch, t * P + 64 * ch

            def gram(bank, lhs, rhs, t, at=0):
                for h, ch, c, hp, cp, tok in chunks(t):
                    last = mm(PS[cp:cp + 64, bank + h % 2, at + c * 64:at + (c + 1) * 64],
                              lhs[hp:hp + 64, c * T + tok:c * T + tok + 64],
                              rhs[hp:hp + 64, c * T + tok:c * T + tok + 64], start=True, stop=True)
                return last

            def blockmul(bank, lhs, rhs, t):
                for h, ch, c, hp, cp, tok in chunks(t):
                    last = mm(PS[cp:cp + 64, bank, h * 64:(h + 1) * 64], lhs[cp:cp + 64, h * 64:(h + 1) * 64],
                              rhs[cp:cp + 64, h * 64:(h + 1) * 64], start=True, stop=True)
                return last

            At, Rt, Kt, Bt = kk, r_f, k_f, a_f
            for t in range(TT):
                XiT = XiTs[t]
                if t:
                    pe.wait_ge(S.inv_ready, 6)
                gram(0, At, Bt, t)
                gram(0, Bt, At, t, 256)
                gram(2, Kt, At, t)
                gram(2, Kt, Rt, t, 256)
                gram(6, Bt, Rt, t).then_inc(S.gram_done, 1)
                pe.wait_ge(S.gram_ready, t + 1)
                for lv in range(5):
                    n = 5 * t + lv
                    pe.wait_ge(S.inv_ready, 6 * t + lv + 1)
                    blockmul(0, Loff, XiT, t).then_inc(S.invq_done, 1)
                    pe.wait_ge(S.invq_ready, n + 1)
                    last = blockmul(1, Xi, Qi, t)
                    if lv < 4:
                        last = blockmul(2, Qi, Xi, t)
                    last.then_inc(S.invx_done, 1)
            pe.wait_ge(S.inv_ready, 12)
            for g in range(NCK):
                t, cp = g // 2, 64 * (g % 2)
                MT, RKT, RBT, XiT = MTs[t], RKTs[t], RBTs[t], XiTs[t]
                Z = Zn[:, (g - 1) % 2, :, :]
                tok = t * P + cp
                if g:
                    pe.wait_ge(S.z_ready, g)
                for c in range(4):
                    if g:
                        mm(PS[cp:cp + 64, 0, c * P:(c + 1) * P], At[:, c * T + tok:c * T + tok + 64], Z[:, c, :],
                           start=True, stop=False)
                    for h in (2 * c, 2 * c + 1):
                        last = mm(PS[cp:cp + 64, 0, h * 64:(h + 1) * 64], MT[cp:cp + 64, h * 64:(h + 1) * 64],
                                  V_t[cp:cp + 64, t, h * 64:(h + 1) * 64], start=g == 0, stop=g == 0 or h % 2 == 1)
                last.then_inc(S.ru_done, 1)
                pe.wait_ge(S.ru_ready, g + 1)
                for h in range(8):
                    last = mm(PS[cp:cp + 64, 1, h * 64:(h + 1) * 64], XiT[cp:cp + 64, h * 64:(h + 1) * 64],
                              RU[cp:cp + 64, h * 64:(h + 1) * 64], start=True, stop=True)
                last.then_inc(S.u_done, 1)
                pe.wait_ge(S.u_ready, g + 1)
                if g < NCK - 1:
                    for c in range(4):
                        cs = slice(c * P, (c + 1) * P)
                        mm(PS[:, 3, cs], K_t[cp:cp + 64, t, cs], V_t[cp:cp + 64, t, cs], start=True, stop=False)
                        if g:
                            mm(PS[:, 3, cs], ident, Z[:, c, :], start=False, stop=False)
                        last = mm(PS[:, 3, cs], B_t[cp:cp + 64, t, cs], U[cp:cp + 64, cs], start=False, stop=True)
                    last.then_inc(S.z_done, 1)
                if g:
                    pe.wait_ge(S.yc_ready, g)
                for c in range(4):
                    if g:
                        mm(PS[cp:cp + 64, 2, c * P:(c + 1) * P], Rt[:, c * T + tok:c * T + tok + 64], Z[:, c, :],
                           start=True, stop=False)
                    for h in (2 * c, 2 * c + 1):
                        hs = slice(h * 64, (h + 1) * 64)
                        mm(PS[cp:cp + 64, 2, hs], RKT[cp:cp + 64, hs], V_t[cp:cp + 64, t, hs], start=g == 0,
                           stop=False)
                        last = mm(PS[cp:cp + 64, 2, hs], RBT[cp:cp + 64, hs], U[cp:cp + 64, hs], start=False,
                                  stop=g == 0 or h % 2 == 1)
                last.then_inc(S.yc_done, 1)
            pe.wait_ge(S.conv_ready, 1)
            for t in range(TT):
                for c in range(4):
                    last = nc.tensor.transpose(PS[:, 4 + t, c * P:(c + 1) * P],
                                               conv[:, c * T + t * P:c * T + (t + 1) * P], ident)
            last.then_inc(S.convT_done, 1)
            pe.wait_ge(S.cn_ready, 2)
            for c in range(4):
                for t in range(TT):
                    at = c % 2 * T + t * P
                    last = nc.tensor.transpose(PS[:, 6 + c // 2, at:at + P], tmp[:, t * 512 + c * P:t * 512 + (c + 1) * P],
                                               ident)
            last.then_inc(S.cnT_done, 1)
            pe.wait_ge(S.yn_ready, 1)
            for c in range(4):
                for t in range(TT):
                    at = c % 2 * T + t * P
                    last = nc.tensor.transpose(PS[:, c // 2, at:at + P], Y[:, t, c * P:(c + 1) * P], ident)
            last.then_inc(S.ynT_done, 1)
            pe.wait_ge(S.yf_ready, 2)
            rows_matrix("w_out", 0)

            norm(1, MEM)
            for n in range(4):
                if n == 0:
                    pe.wait_ge(S.hT_ready, 16)
                if n >= 2:
                    pe.wait_ge(S.kmT_ready, n - 1)
                feat_slot(2 * (FIRST["km"] + n), 4 + n % 2)
            pe.wait_ge(S.x_ready, 1)
            rows_matrix("vm", 0)
            pe.wait_ge(S.kmT_ready, 4)
            norm(2)
            pe.wait_ge(S.vm_ready, 4)
            for n in range(4):
                feat_slot(2 * (FIRST["wq"] + n), n, 0, None if n else 2)
            pe.wait_ge(S.qT_ready, 4)
            attention(0, qT, kmT, vm, 2, 4, 0, None)
            pe.wait_ge(S.o_ready, 4)
            rows_matrix("wo", 4)

            norm(3)
            ffn(0)
            norm(4)
            ffn(1)
            norm(5)
            rows_matrix("q", 0, normed=5)
            rows_matrix("k", 4)
            pe.wait_ge(S.qk_evac, 4)
            rows_matrix("v", 0)
            for q, src in enumerate((q_r, k_r)):
                pe.wait_ge(S.qk_roped, q + 1)
                if q:
                    pe.wait_ge(S.qkT_ready, 4)
                else:
                    pe.wait_ge(S.qk_evac, 8)
                s3 = src.rearrange("p (t d) -> p t d", t=TT)
                for h in range(8):
                    for t in range(TT):
                        at = h % 2 * T + t * P
                        last = nc.tensor.transpose(PS[:, 4 + h // 2, at:at + P], s3[:, t, h * P:(h + 1) * P], ident)
                last.then_inc(S.qkT_done, 1)
            pe.wait_ge(S.qkT_ready, 8)
            pe.wait_ge(S.v_ready, 4)
            attention(1, qT, kT2, v2, 1, 8, 0, None)
            pe.wait_ge(S.o_ready, 6)
            attention(2, qT, kT2, v2, 1, 8, 1, None)
            pe.wait_ge(S.o_ready, 8)
            rows_matrix("attn_o", 4)
            norm(6)
            ffn(2)
            norm(7)
            ffn(3)

            norm(8)
            pe.wait_ge(S.hT_ready, 72)
            for t in range(TT):
                for c in range(KC):
                    ts = slice(t * P, (t + 1) * P)
                    mm(PS[:, 4 + t, 0:32], h_hi[:, c, ts].bitcast(F32), pc("w_dt", c * 32, 32), start=c == 0, stop=False)
                    last = mm(PS[:, 4 + t, 0:32], h_lo[:, c, ts].bitcast(F32), pc("w_dt", c * 32, 32), start=False,
                              stop=c == KC - 1)
            last.then_inc(S.dt_done, 1)
            for half in range(2):
                if half:
                    pe.wait_ge(S.z_ready2, 4)
                rows_matrix("z", 0, first=4 * half)
            pe.wait_ge(S.dta_ready, 1)
            for t in range(TT):
                mm(PS[:, 6, t * 32:(t + 1) * 32], cn("upper"), dta[:, t, :], start=True, stop=True)
            mm(PS[:, 6, 64:96], cn("ones"), dta[:, 0, :], start=True, stop=True).then_inc(S.acs_done, 1)
            pe.wait_ge(S.acs_ready, 1)
            for n in range(16):
                bank = [4, 5, 6, 7][n % 4]
                if n >= 4:
                    pe.wait_ge(S.conv4_ready, 2 * (n - 3))
                feat_slot(2 * (FIRST["xbc"] + n), bank)
            pe.wait_ge(S.z_ready2, 8)
            for n in range(10):
                if n < 4:
                    pe.wait_ge(S.xbc_ready, 32)
                else:
                    pe.wait_ge(S.sT_ready, n - 3)
                for q in range(4):
                    if n < 8:
                        src = xsT[:, n % 4 * 4 + q, n // 4 * P:(n // 4 + 1) * P]
                    else:
                        src = bcT[:, (n - 8) * 4 + q, 0:P]
                    last = nc.tensor.transpose(PS[:, n % 4, q * P:(q + 1) * P], src, ident)
                last.then_inc(S.sT_done, 1)
            pe.wait_ge(S.sT_ready, 10)
            pe.wait_ge(S.conv4_ready, 32)
            for g in range(G):
                for t in range(TT):
                    n = 2 * g + t
                    b = n % 2
                    if n >= 2:
                        pe.wait_ge(S.g_lt, n - 1)
                        pe.wait_ge(S.g_w, n - 1)
                    mm(PS[:, b, :], ident, cn("future").unsqueeze(1).broadcast_to([P, 4, P]), start=True, stop=False)
                    for r in range(4):
                        h = 4 * g + r
                        mm(PS[:, b, r * P:(r + 1) * P], dta[:, t, h:h + 1].broadcast_to([P, P]), cn("upper"),
                           start=False, stop=r == 3)
                    mm(PS[:, 2 + b, 0:P], bcT[:, g, t * P:(t + 1) * P], bcT[:, 8 + g, t * P:(t + 1) * P],
                       start=True, stop=True).then_inc(S.g_cb, 1)
                    if t == 0:
                        pe.wait_ge(S.g_xdec, g + 1)
                        if g >= 1:
                            pe.wait_ge(S.g_stready, g)
                        mm(PS[:, 6, 0:256], Btok[:, g, :], xdec[:, g % 2, :], start=True, stop=True).then_inc(S.g_st, 1)
                    else:
                        pe.wait_ge(S.g_stready, g + 1)
                        if g >= 1:
                            pe.wait_ge(S.g_yev, n - 1)
                        mm(PS[:, 7, 0:256], bcT[:, 8 + g, P:T], stT[:, g % 2, :], start=True, stop=True)
                    pe.wait_ge(S.g_w, n + 1)
                    if n >= 2:
                        pe.wait_ge(S.g_yev, n - 1)
                    for r in range(4):
                        last = mm(PS[:, 4 + b, r * 64:(r + 1) * 64], Wd[:, b, r, :], xdt[:, b, r * 64:(r + 1) * 64],
                                  start=True, stop=True)
                    last.then_inc(S.g_y, 1)
            pe.wait_ge(S.ysn_ready, 1)

            def out_transposes(n):
                for j in range(2):
                    for t in range(TT):
                        c = 2 * n + j
                        last = nc.tensor.transpose(PS[:, n % 4, j * T + t * P:j * T + (t + 1) * P],
                                                   y_s[:, t, c * P:(c + 1) * P], ident)
                last.then_inc(S.ysT_done, 1)

            for n in range(4):
                out_transposes(n)
            for n in range(8):
                pe.wait_ge(S.ysT_ready, 2 * n + 2)
                for j in range(2):
                    c = (2 * n + j) % KC
                    rows_half(2 * (FIRST["ssm_out"] + n) + j, h_hi[:, c, :], h_lo[:, c, :], 4, n == 0 and j == 0,
                              n == 7 and j == 1)
                if n < 4:
                    out_transposes(n + 4)
            norm(9)
            ffn(4)

        @block.scalar
        def _(act):
            A = nc.scalar.activation
            steps = [0]

            def step(ins):
                steps[0] += 1
                ins.then_inc(S.act_step, 1)
                act.wait_ge(S.act_step, steps[0])

            cursor = [0]

            def split(last, i=0):
                while cursor[0] <= min(last, 2 * NSLOTS - 1):
                    n = cursor[0]
                    if n % 2 == 0:
                        act.wait_ge(loaded[n // 2 % R], i * (16 * LOOP // 2 // R) + 16 * (n // 2 // R + 1))
                    if n >= H:
                        act.wait_ge(S.half_done, LOOP * i + n - H + 1)
                    A(w_hi[:, n % H, :], raw[:, n % (2 * R), :], ACT.Copy).then_inc(S.hi_ready, 1)
                    cursor[0] += 1

            def when_done(name, slot):
                split(2 * (FIRST[name] + slot) + 4)
                done(act, name, slot)

            def stats(k, src=X, junk=xn):
                for t in range(TT):
                    A(junk[:, t, :], src[:, t, :], ACT.Square, accum_out=ssq[:, t:t + 1]).then_inc(S.ssq_ready, 1)
                act.wait_ge(S.ms_ready, k + 1)
                A(std, ms, ACT.Sqrt).then_inc(S.std_ready, 1)

            def to_h(k):
                for c in range(KC):
                    act.wait_ge(S.xT_ready, 4 * k + c // 2 + 1)
                    A(h_hi[:, c, :], PS[:, 4 + c // 2, c % 2 * T:(c % 2 + 1) * T], ACT.Copy, scale=pc("gain", 8 * k + c))\
                        .then_inc(S.hT_hi, 1)

            def norm(k):
                act.wait_ge(S.x_ready, k - 1)
                stats(k)
                to_h(k)

            def ysquare(k, bank):
                for t in range(TT):
                    for h in range(2):
                        A(xn[:, t, h * 512:(h + 1) * 512], PS[:, bank + 2 * t + h, :], ACT.Square,
                          accum_out=yssq[:, 2 * t + h:2 * t + h + 1]).then_inc(S.yssq_ready, 1)
                act.wait_ge(S.yms_ready, k + 1)
                A(ystd, yms, ACT.Sqrt).then_inc(S.ystd_ready, 1)

            def ffn(f):
                def silu(b, i=0, ii=0):
                    n = ffn_half(f, "G", b)
                    split(n + 4, i)
                    act.wait_ge(S.half_done, LOOP * i + n + 2)
                    if b >= 2:
                        act.wait_ge(S.act_ready, ii * 2 + (NB * f + b - 1))
                    A(sg[:, b % 2, :], PS[:, 4 + 2 * (b % 2), :], ACT.Silu).then_inc(S.silu_ready, 1)
                    split(n + 7, i)
                    act.wait_ge(S.g_mult, ii * 2 + (NB * f + b + 1))
                    A(g_hi[:, b % 2, :, :].rearrange("p j t -> p (j t)"), sg[:, b % 2, :], ACT.Copy).then_inc(S.g_hi_ready, 1)

                silu(0)
                silu(1)
                with act.Fori(0, (NB - 3) // 2) as i:
                    for b in (2, 3):
                        silu(b, i, i)
                cursor[0] += LOOP * ((NB - 3) // 2 - 1)
                silu(NB - 1)
                split(ffn_half(f, "D", NB - 1) + 4)
                act.wait_ge(S.half_done, ffn_half(f, "D", NB - 1) + 2)

            def attention(a, scale):
                act.wait_ge(S.nmax_ready, a + 1)
                for s in range(8):
                    last = A(prob[:, s, :], PS[:, s // 2, s % 2 * T:(s % 2 + 1) * T], ACT.Exp, bias=nmax[:, s:s + 1],
                             scale=scale, accum_out=psum_[:, s:s + 1])
                last.then_inc(S.exp_ready, 1)
                act.wait_ge(S.probT_done, a + 1)
                for h in (0, 2):
                    A(probT[:, h, :, :], PS[:, 4 + h, :].rearrange("p (k t) -> p k t", k=2), ACT.Copy)\
                        .then_inc(S.probT_ready, 1)

            act.dma_start(ptab[:], cols).then_inc(S.params_loaded, 16)
            act.dma_start(ctab[:], consts).then_inc(S.params_loaded, 16)
            act.dma_start(rtab[:], rows.broadcast_to([P, NR_])).then_inc(S.params_loaded, 16)
            act.dma_start(pos_i[:], pos_in).then_inc(S.pos_loaded, 16)
            split(1)
            act.wait_ge(S.x_loaded, 16)
            stats(0)
            act.wait_ge(S.params_loaded, 48)
            to_h(0)
            split(3)
            act.wait_ge(S.ang_ready, 1)
            A(trig, trig, ACT.Sin).then_inc(S.trig_ready, 1)
            act.wait_ge(S.pad_ready, 1)
            for n in range(11):
                when_done("w_in", n)
                if n < 7:
                    c = 2 * n
                    A(pin[:, c:c + 2, 1:T + 1], PS[:, n % 4, :].rearrange("p (c t) -> p c t", c=2), ACT.Copy)\
                        .then_inc(S.pin_ready, 1)
                elif n < 9:
                    A(glu[:, (n - 7) * 512:(n - 6) * 512], PS[:, n % 4, :], ACT.Copy).then_inc(S.pin_ready, 1)
                else:
                    A(usig[:, (n - 9) * 512:(n - 8) * 512], PS[:, n % 4, :], ACT.Sigmoid).then_inc(S.pin_ready, 1)
            split(25)
            act.wait_ge(S.q_mixed, 7)
            A(Q[0:64, 12, :], Q[0:64, 12, :], ACT.Tanh).then_inc(S.lora_ready, 1)
            A(Q[:, 13, :], Q[:, 13, :], ACT.Sigmoid).then_inc(S.lora_ready, 2)
            act.wait_ge(S.wa_done, 1)
            for c in range(4):
                last = A(decay[:, c * T:(c + 1) * T], PS[:, c // 2, c % 2 * T:(c % 2 + 1) * T], ACT.Sigmoid,
                         bias=pc("w0", c))
            for c in range(4):
                last = A(a_f[:, c * T:(c + 1) * T], PS[:, 2 + c // 2, c % 2 * T:(c % 2 + 1) * T], ACT.Sigmoid,
                         bias=pc("a0", c))
            last.then_inc(S.a_ready, 1)
            act.wait_ge(S.g_done, 1)
            A(g_f, PS[:, 6:8, :].rearrange("p a b -> p (a b)"), ACT.Copy).then_inc(S.g_ready, 1)
            act.wait_ge(S.a_ready, 1)
            A(decay, decay, ACT.Exp, scale=-DECAY).then_inc(S.decay_ready, 1)
            act.wait_ge(S.kkmax_ready, 1)
            A(tmp, tmp, ACT.Sqrt).then_inc(S.kk_std, 1)
            act.wait_ge(S.tok_done, 1)
            for i, (bank, dst, t) in enumerate(((0, V_t, 0), (1, V_t, 1), (2, K_t, 0), (3, K_t, 1), (6, B_t, 0), (7, B_t, 1))):
                if i % 2 == 0:
                    A(dst[:, t, :], PS[:, bank, :], ACT.Copy).then_inc(S.tok_ready, 1)
            for n in range(10):
                act.wait_ge(S.invq_done, n + 1)
                A(Qi, PS[:, 0, :], ACT.Copy).then_inc(S.invq_ready, 1)
            for g in range(NCK):
                t, cp = g // 2, 64 * (g % 2)
                act.wait_ge(S.ru_done, g + 1)
                A(RU[cp:cp + 64, :], PS[cp:cp + 64, 0, :], ACT.Copy).then_inc(S.ru_ready, 1)
                act.wait_ge(S.u_done, g + 1)
                A(U[cp:cp + 64, :], PS[cp:cp + 64, 1, :], ACT.Copy).then_inc(S.u_ready, 1)
                act.wait_ge(S.yc_done, g + 1)
                A(Y[cp:cp + 64, t, :], PS[cp:cp + 64, 2, :], ACT.Copy).then_inc(S.yc_ready, 1)
            act.wait_ge(S.cvar_ready, 1)
            A(cstd, cvar, ACT.Sqrt).then_inc(S.cstd_ready, 1)
            act.wait_ge(S.ynvar_ready, 1)
            A(ynstd, ynvar, ACT.Sqrt).then_inc(S.ynstd_ready, 1)
            act.wait_ge(S.cnT_done, 1)
            for c in range(4):
                A(YF[:, c, :], PS[:, 6 + c // 2, c % 2 * T:(c % 2 + 1) * T], ACT.Silu, bias=pc("ln_b", c),
                  scale=pc("ln_g", c)).then_inc(S.convY_ready, 1)
            act.wait_ge(S.convY_ready, 4)
            A(h_hi[:, 0:4, :], YF[:, 0:4, :], ACT.Copy).then_inc(S.yf_hi, 1)
            act.wait_ge(S.yT_ready, 1)
            A(h_hi[:, 4:8, :], YF[:, 4:8, :], ACT.Copy).then_inc(S.yf_hi, 1)
            act.wait_ge(S.mem_loaded, 16)
            act.wait_ge(S.yf_ready, 2)
            stats(1, MEM)
            when_done("w_out", 3)
            to_h(1)
            ysquare(0, 0)
            for n in range(4):
                when_done("km", n)
                A(kmT[:, 2 * n:2 * n + 2, :], PS[:, 4 + n % 2, :].rearrange("p (c t) -> p c t", c=2), ACT.Copy)\
                    .then_inc(S.kmT_ready, 1)
                if n == 0:
                    act.wait_ge(S.x_ready, 1)
                    stats(2)
            when_done("vm", 3)
            for b in range(4):
                A(vm[:, b // 2, b % 2 * 512:(b % 2 + 1) * 512], PS[:, b, :], ACT.Copy).then_inc(S.vm_ready, 1)
            to_h(2)
            for n in range(4):
                when_done("wq", n)
                A(qT[:, 2 * n:2 * n + 2, :], PS[:, n, :].rearrange("p (c t) -> p c t", c=2), ACT.Copy)\
                    .then_inc(S.qT_ready, 1)
            attention(0, 1.0 / 16)

            def outputs(a, first, banks):
                act.wait_ge(S.o_done, a + 1)
                for n in range(banks):
                    A(h_hi[:, first + 2 * n:first + 2 * n + 2, :], PS[:, n, :].rearrange("p (c t) -> p c t", c=2),
                      ACT.Copy).then_inc(S.o_hi, 1)

            outputs(0, 0, 4)
            when_done("wo", 3)
            ysquare(1, 4)
            norm(3)
            ffn(0)
            ysquare(2, 0)
            norm(4)
            ffn(1)
            norm(5)
            for q, (dst, bank) in enumerate(((q_r, 0), (k_r, 4))):
                when_done("qk"[q], 3)
                for b in range(4):
                    A(dst[:, b * 512:(b + 1) * 512], PS[:, bank + b, :], ACT.Copy).then_inc(S.qk_evac, 1)
                act.wait_ge(S.qk_evac, 4 * (q + 1))
                A(rt1, dst, ACT.Square).then_inc(S.qk_sq, 1)
                act.wait_ge(S.qk_ms, q + 1)
                A(qkstd[:, q * 16:(q + 1) * 16], qkms[:, q * 16:(q + 1) * 16], ACT.Sqrt).then_inc(S.qk_std, 1)
            when_done("v", 3)
            for b in range(4):
                A(v2[:, b // 2, b % 2 * 512:(b % 2 + 1) * 512], PS[:, b, :], ACT.Copy).then_inc(S.v_ready, 1)
            split(2 * FIRST["attn_o"] + 3)
            for q, dst in enumerate((qT, kT2)):
                act.wait_ge(S.qkT_done, q + 1)
                for n in range(4):
                    A(dst[:, 2 * n:2 * n + 2, :], PS[:, 4 + n, :].rearrange("p (c t) -> p c t", c=2), ACT.Copy)\
                        .then_inc(S.qkT_ready, 1)
            for half in range(2):
                attention(1 + half, 128 ** -0.5)
                outputs(1 + half, 4 * half, 2)
            split(2 * FIRST["attn_o"] + 11)
            norm(6)
            ffn(2)
            norm(7)
            ffn(3)
            norm(8)
            act.wait_ge(S.dt_abs, 1)
            A(dte, dte, ACT.Exp, scale=-1.0).then_inc(S.dt_exp, 1)
            A(aexp, row("a_log"), ACT.Exp).then_inc(S.aneg, 1)
            act.wait_ge(S.dt_exp, 1)
            A(dte, dte, ACT.Ln, bias=1.0).then_inc(S.dt_ln, 1)
            for half in range(2):
                when_done("z", 4 * half + 3)
                for b in range(4):
                    at = half * 1024 + b % 2 * 512
                    A(z_s[:, b // 2, at:at + 512], PS[:, b, :], ACT.Silu).then_inc(S.z_ready2, 1)

            def conv_silu(c):
                act.wait_ge(S.conv4_ready, c + 1)
                dst = (xsT if c < 16 else bcT)[:, c % 16, :]
                A(dst, ctmp[:, c // 2 % 4, c % 2 * T:(c % 2 + 1) * T], ACT.Silu).then_inc(S.xbc_ready, 1)

            for n in range(16):
                when_done("xbc", n)
                if n >= 4:
                    act.wait_ge(S.xbc_ready, 2 * n - 6)
                for j in range(2):
                    c = 2 * n + j
                    A(ctmp[:, n % 4, j * T:(j + 1) * T], PS[:, 4 + n % 4, j * T:(j + 1) * T], ACT.Identity,
                      bias=pc("sconv_b", c), scale=pc("sconv_w", 3 * 32 + c)).then_inc(S.conv1_ready, 1)
                if n:
                    conv_silu(2 * n - 2)
                    conv_silu(2 * n - 1)
            conv_silu(30)
            conv_silu(31)
            act.wait_ge(S.acs_ready, 1)
            A(dec0, dec0, ACT.Exp).then_inc(S.decay2_done, 1)
            A(eacs, nacs[:, 32:64], ACT.Exp, scale=-1.0).then_inc(S.decay2_done, 1)
            for n in range(10):
                act.wait_ge(S.sT_done, n + 1)
                if n < 8:
                    dst = xtok[:, n // 4, n % 4 * 512:(n % 4 + 1) * 512]
                else:
                    dst = Btok[:, (n - 8) * 4:(n - 7) * 4, :].rearrange("p g n -> p (g n)")
                A(dst, PS[:, n % 4, :], ACT.Copy).then_inc(S.sT_ready, 1)
            for g in range(G):
                for t in range(TT):
                    n = 2 * g + t
                    b = n % 2
                    act.wait_ge(S.g_cb, n + 1)
                    if n >= 2:
                        act.wait_ge(S.g_w, n - 1)
                    for r in range(4):
                        h = 4 * g + r
                        last = A(LT[:, b, r, :], PS[:, b, r * P:(r + 1) * P], ACT.Exp,
                                 bias=nacs[:, t * 32 + h:t * 32 + h + 1])
                    last.then_inc(S.g_lt, 1)
                    if t == 0:
                        act.wait_ge(S.g_st, g + 1)
                        if g >= 2:
                            act.wait_ge(S.g_y, n - 2)
                        A(stT[:, g % 2, :], PS[:, 6, 0:256], ACT.Copy).then_inc(S.g_stready, 1)
            act.wait_ge(S.ys_ready, 1)
            A(SQ, y_s.rearrange("p t d -> p (t d)"), ACT.Square).then_inc(S.ys_sq, 1)
            act.wait_ge(S.ys_ms, 1)
            A(ysstd, ysms, ACT.Sqrt).then_inc(S.ys_std, 1)
            split(2 * FIRST["ssm_out"] + 3)
            for c in range(16):
                act.wait_ge(S.ysT_done, c // 2 + 1)
                if c >= KC:
                    split(2 * FIRST["ssm_out"] + c - KC + 4)
                    act.wait_ge(S.half_done, 2 * FIRST["ssm_out"] + c - KC + 1)
                A(h_hi[:, c % KC, :], PS[:, c // 2 % 4, c % 2 * T:(c % 2 + 1) * T], ACT.Copy,
                  scale=pc("ssm_norm", c)).then_inc(S.ysT_hi, 1)
            when_done("ssm_out", 7)
            norm(9)
            ffn(4)

        @block.vector
        def _(dve):
            v = nc.vector
            steps = [0]

            def step(ins):
                steps[0] += 1
                ins.then_inc(S.dve_step, 1)
                dve.wait_ge(S.dve_step, steps[0])

            cursor = [0]

            def split(last, i=0):
                while cursor[0] <= min(last, 2 * NSLOTS - 1):
                    n = cursor[0]
                    dve.wait_ge(S.hi_ready, LOOP * i + n + 1)
                    v.tensor_tensor(w_lo[:, n % H, :], raw[:, n % (2 * R), :], w_hi[:, n % H, :].bitcast(F32),
                                    ALU.subtract).then_inc(S.lo_ready, 1)
                    cursor[0] += 1

            def when_done(name, slot):
                split(2 * (FIRST[name] + slot) + 4)
                done(dve, name, slot)

            def stats(k, src=X, dst=xn):
                dve.wait_ge(S.ssq_ready, 2 * (k + 1))
                v.tensor_scalar(ms, ssq, 1.0 / D, 1e-6, ALU.mult, ALU.add).then_inc(S.ms_ready, 1)
                dve.wait_ge(S.std_ready, k + 1)
                step(v.reciprocal(rstd, std))
                for t in range(TT):
                    v.tensor_scalar(dst[:, t, :], src[:, t, :], rstd[:, t:t + 1], None, ALU.mult).then_inc(S.xn_ready, 1)

            def to_h(k):
                for c in range(KC):
                    dve.wait_ge(S.hT_hi, 8 * k + c // 2 * 2 + 2)
                    v.scalar_tensor_tensor(h_lo[:, c, :], PS[:, 4 + c // 2, c % 2 * T:(c % 2 + 1) * T],
                                           pc("gain", 8 * k + c), h_hi[:, c, :].bitcast(F32), ALU.mult, ALU.subtract)\
                        .then_inc(S.hT_ready, 1)

            def norm(k):
                stats(k)
                to_h(k)

            def ynorm(k, bank):
                dve.wait_ge(S.yssq_ready, 4 * (k + 1))
                step(v.tensor_tensor(yms, yssq[:, 0:4:2], yssq[:, 1:4:2], ALU.add))
                v.tensor_scalar(yms, yms, 1.0 / D, 1e-6, ALU.mult, ALU.add).then_inc(S.yms_ready, 1)
                dve.wait_ge(S.ystd_ready, k + 1)
                step(v.reciprocal(yrstd, ystd))
                dve.wait_ge(S.gain_loaded, 16 * (k + 1))
                for t in range(TT):
                    for h in range(2):
                        last = v.scalar_tensor_tensor(xn[:, t, h * 512:(h + 1) * 512], PS[:, bank + 2 * t + h, :],
                                                      yrstd[:, t:t + 1], post_gain[:, h * 512:(h + 1) * 512],
                                                      ALU.mult, ALU.mult)
                last.then_inc(S.gain_read, 1)
                dve.wait_ge(S.gain_read, k + 1)
                for t in range(TT):
                    last = v.tensor_tensor(X[:, t, :], X[:, t, :], xn[:, t, :], ALU.add)
                last.then_inc(S.x_ready, 1)

            def residual(bank, factor):
                for t in range(TT):
                    for h in range(2):
                        hs = slice(h * 512, (h + 1) * 512)
                        last = v.scalar_tensor_tensor(X[:, t, hs], PS[:, bank + 2 * t + h, :], factor, X[:, t, hs],
                                                      ALU.mult, ALU.add)
                last.then_inc(S.x_ready, 1)

            def ffn(f):
                def hidden(b, i=0, ii=0):
                    n = ffn_half(f, "G", b)
                    split(n + 6, i)
                    dve.wait_ge(S.half_done, LOOP * i + n + 4)
                    dve.wait_ge(S.silu_ready, ii * 2 + (NB * f + b + 1))
                    v.tensor_tensor(sg[:, b % 2, :], sg[:, b % 2, :], PS[:, 5 + 2 * (b % 2), :], ALU.mult)\
                        .then_inc(S.g_mult, 1)
                    split(n + 7, i)
                    dve.wait_ge(S.g_hi_ready, ii * 2 + (NB * f + b + 1))
                    v.tensor_tensor(g_lo[:, b % 2, :, :].rearrange("p j t -> p (j t)"), sg[:, b % 2, :],
                                    g_hi[:, b % 2, :, :].rearrange("p j t -> p (j t)").bitcast(F32),
                                    ALU.subtract).then_inc(S.act_ready, 1)

                hidden(0)
                hidden(1)
                with dve.Fori(0, (NB - 3) // 2) as i:
                    for b in (2, 3):
                        hidden(b, i, i)
                cursor[0] += LOOP * ((NB - 3) // 2 - 1)
                hidden(NB - 1)
                split(ffn_half(f, "D", NB - 1) + 4)
                dve.wait_ge(S.half_done, ffn_half(f, "D", NB - 1) + 2)

            def attention(a, scale, causal):
                dve.wait_ge(S.score_done, a + 1)
                allps = PS[:, 0:4, :].rearrange("p b (s m) -> p (b s) m", s=2)
                if causal:
                    m4 = cn("causal").rearrange("p (o t m) -> p o t m", o=1, t=TT).broadcast_to([P, 4, TT, T])
                    step(v.tensor_tensor(PS[:, 0:4, :].rearrange("p h (t m) -> p h t m", t=TT),
                                         PS[:, 0:4, :].rearrange("p h (t m) -> p h t m", t=TT), m4, ALU.add))
                step(v.tensor_reduce(nmax, allps, AX.X, ALU.max))
                v.tensor_scalar(nmax, nmax, -scale, None, ALU.mult).then_inc(S.nmax_ready, 1)
                dve.wait_ge(S.exp_ready, a + 1)
                step(v.reciprocal(rsum, psum_))
                v.tensor_tensor(prob, prob, rsum.unsqueeze(2).broadcast_to([P, 8, T]), ALU.mult).then_inc(S.prob_ready, 1)
                dve.wait_ge(S.probT_done, a + 1)
                for h in (1, 3):
                    v.tensor_copy(probT[:, h, :, :], PS[:, 4 + h, :].rearrange("p (k t) -> p k t", k=2))\
                        .then_inc(S.probT_ready, 1)

            split(1)
            stats(0)
            dve.wait_ge(S.params_loaded, 48)
            to_h(0)
            split(3)
            v.memset(pin[:, :, 0:1], 0.0).then_inc(S.pad_ready, 1)
            dve.wait_ge(S.pos_loaded, 16)
            step(v.tensor_copy(posf, pos_i[:]))
            tr = trig.rearrange("p (s t f) -> p s t f", s=2, t=TT)
            for t in range(TT):
                for s in range(2):
                    last = v.tensor_scalar(tr[:, s, t, :], cn("inv_freq"), posf[:, t:t + 1], None, ALU.mult)
            step(last)
            magic = 12582912.0
            for s in range(2):
                last = v.tensor_scalar(turns[:, s * 128:(s + 1) * 128], trig[:, s * 128:(s + 1) * 128],
                                       1.0 / (2 * math.pi), 0.25 * s, ALU.mult, ALU.add)
            step(last)
            step(v.tensor_scalar(turns, turns, magic, None, ALU.add))
            step(v.tensor_scalar(turns, turns, magic, None, ALU.subtract))
            for part in (6.28125, 0.0019350051879882812, 3.019915981956753e-07):
                step(v.scalar_tensor_tensor(trig, turns, -part, trig, ALU.mult, ALU.add))
            step(v.tensor_scalar(trig[:, 128:256], trig[:, 128:256], math.pi / 2, None, ALU.add))
            v.tensor_scalar(trig, trig, 3.1415925, -3.1415925, ALU.min, ALU.max).then_inc(S.ang_ready, 1)

            for n in range(7):
                split(2 * n + 4)
                dve.wait_ge(S.pin_ready, 1 + n)
                c = 2 * n
                step(v.tensor_tensor(tshift.rearrange("p (c t) -> p c t", c=2), pin[:, c:c + 2, 0:T],
                                     pin[:, c:c + 2, 1:T + 1], ALU.subtract))
                for j in range(2):
                    last = v.scalar_tensor_tensor(Q[:, c + j, :], tshift[:, j * T:(j + 1) * T], pc("mu", c + j),
                                                  pin[:, c + j, 1:T + 1], ALU.mult, ALU.add)
                last.then_inc(S.q_mixed, 1)
                dve.wait_ge(S.q_mixed, n + 1)
            for c in range(4):
                last = v.tensor_scalar(kk[:, c * T:(c + 1) * T], Q[:, 4 + c, :], pc("k_k", c), None, ALU.mult)
            step(last)
            v.tensor_tensor(tmp, kk, kk, ALU.mult).then_inc(S.kksq_ready, 1)
            split(25)
            dve.wait_ge(S.pin_ready, 11)
            step(v.tensor_tensor(glu, glu, usig, ALU.mult))
            dve.wait_ge(S.kksum_done, 1)
            v.tensor_scalar(tmp, PS[:, 4:6, :].rearrange("p a b -> p (a b)"), 1e-24, None, ALU.max)\
                .then_inc(S.kkmax_ready, 1)
            dve.wait_ge(S.kk_std, 1)
            step(v.reciprocal(tmp, tmp))
            step(v.tensor_tensor(kk, kk, tmp, ALU.mult))
            dve.wait_ge(S.a_ready, 1)
            for c in range(4):
                last = v.tensor_scalar(tmp[:, c * T:(c + 1) * T], a_f[:, c * T:(c + 1) * T], -1.0, pc("k_a", c),
                                       ALU.add, ALU.mult)
            step(last)
            step(v.scalar_tensor_tensor(k_f, tmp, 1.0, k_f, ALU.add, ALU.mult))
            for c in range(4):
                cs = slice(c * T, (c + 1) * T)
                last = v.scalar_tensor_tensor(tmp[:, cs], r_f[:, cs], pc("r_k", c), k_f[:, cs], ALU.mult, ALU.mult)
            last.then_inc(S.bonus_in, 1)
            step(v.memset(Pc[:, :, 0:1], 1.0))
            dve.wait_ge(S.decay_ready, 1)
            for s in range(16):
                last = v.tensor_tensor_scan(Pc[:, s, 1:65], decay[:, s * 64:(s + 1) * 64], cn("zeros"), 1.0,
                                            ALU.mult, ALU.add)
            step(last)
            Pinc, Pexc = Pc[:, :, 1:65], Pc[:, :, 0:64]
            c16 = lambda ap: ap.rearrange("p (s t) -> p s t", s=16)
            v.scalar_tensor_tensor(a_f, kk, -1.0, a_f, ALU.mult, ALU.mult)
            step(v.reciprocal(c16(invP), Pinc))
            v.tensor_tensor(c16(kk), c16(kk), Pexc, ALU.mult)
            v.tensor_tensor(c16(r_f), c16(r_f), Pinc, ALU.mult)
            v.tensor_tensor(k_f, k_f, invP, ALU.mult)
            v.tensor_tensor(a_f, a_f, invP, ALU.mult).then_inc(S.ab_ready, 1)
            dve.wait_ge(S.bonus_sum_done, 1)
            v.tensor_tensor(bonus, PS[:, 4:6, :].rearrange("p a b -> p (a b)"), v_f, ALU.mult)
            dve.wait_ge(S.tok_done, 1)
            for i, (bank, dst, t) in enumerate(((0, V_t, 0), (1, V_t, 1), (2, K_t, 0), (3, K_t, 1), (6, B_t, 0), (7, B_t, 1))):
                if i % 2 == 1:
                    v.tensor_copy(dst[:, t, :], PS[:, bank, :]).then_inc(S.tok_ready, 1)

            h8 = lambda ap: ap.rearrange("p (h t) -> p h t", h=8)
            b8 = lambda m: m.unsqueeze(1).broadcast_to([P, 8, 64])
            taps = [(back, c) for back in range(31) for c in range(4)]

            def tap_steps(n):
                for _ in range(min(n, len(taps))):
                    back, c = taps.pop(0)
                    cs = slice(c * T, (c + 1) * T)
                    weight = pc("conv_w", (30 - back) * 4 + c)
                    if back == 0:
                        last_ = v.tensor_scalar(conv[:, cs], glu[:, cs], weight, pc("conv_b", c), ALU.mult, ALU.add)
                    else:
                        late = conv[:, c * T + back:(c + 1) * T]
                        last_ = v.scalar_tensor_tensor(late, glu[:, c * T:(c + 1) * T - back], weight, late,
                                                       ALU.mult, ALU.add)
                    if c == 3 and taps:
                        step(last_)
                    elif not taps:
                        last_.then_inc(S.conv_ready, 1)

            for t in range(TT):
                MT, RKT, RBT, XiT = MTs[t], RKTs[t], RBTs[t], XiTs[t]
                dve.wait_ge(S.gram_done, t + 1)
                grams = lambda bank, at: PS[:, bank:bank + 2, at:at + 256].rearrange("p e (c t) -> p e c t", c=4)
                heads = lambda ap: ap.rearrange("p (c e t) -> p e c t", c=4, e=2)
                m24 = lambda m: m.unsqueeze(1).unsqueeze(1).broadcast_to([P, 2, 4, 64])
                v.tensor_copy(heads(NL), grams(0, 0))
                v.tensor_tensor(heads(XiT), grams(0, 256), m24(cn("off1T")), ALU.mult)
                v.tensor_tensor(heads(MT), grams(2, 0), m24(cn("s_lt_t")), ALU.mult)
                v.tensor_tensor(heads(RKT), grams(2, 256), m24(cn("s_le_t")), ALU.mult)
                step(v.tensor_tensor(heads(RBT), grams(6, 0), m24(cn("s_le_t")), ALU.mult))
                v.tensor_tensor(h8(XiT), h8(XiT), b8(cn("eye64")), ALU.add)
                step(v.tensor_tensor(h8(Xi), h8(NL), b8(cn("off", 0, 64)), ALU.mult))
                v.tensor_tensor(h8(Xi), h8(Xi), b8(cn("eye64")), ALU.add).then_inc(S.gram_ready, 1)
                v.tensor_tensor(h8(Loff), h8(NL), b8(cn("off", 64, 64)), ALU.mult).then_inc(S.inv_ready, 1)
                tap_steps(4)
                for lv in range(5):
                    n = 5 * t + lv
                    dve.wait_ge(S.invx_done, n + 1)
                    last = v.tensor_tensor(XiT, XiT, PS[:, 1, :], ALU.add)
                    if lv < 4:
                        v.tensor_tensor(Xi, Xi, PS[:, 2, :], ALU.add)
                        v.tensor_tensor(h8(Loff), h8(NL), b8(cn("off", (lv + 2) * 64, 64)), ALU.mult).then_inc(S.inv_ready, 1)
                    else:
                        last.then_inc(S.inv_ready, 1)
                    tap_steps(8)
            tap_steps(len(taps))
            for g in range(NCK - 1):
                dve.wait_ge(S.z_done, g + 1)
                for c in range(4):
                    last = v.scalar_tensor_tensor(Zn[:, g % 2, c, :], PS[:, 3, c * P:(c + 1) * P], Pc[:, c * 4 + g, 64:65],
                                                  cn("pair"), ALU.mult, ALU.mult)
                last.then_inc(S.z_ready, 1)
            dve.wait_ge(S.convT_done, 1)
            for t in range(TT):
                last = v.bn_stats(bst[:, 6 * t:6 * t + 6], PS[:, 4 + t, :])
            step(last)
            for t in range(TT):
                last = v.bn_aggr(bag[:, 2 * t:2 * t + 2], bst[:, 6 * t:6 * t + 6])
            step(last)
            v.tensor_scalar(cvar, bag[:, 1:4:2], 1e-5, None, ALU.add).then_inc(S.cvar_ready, 1)
            dve.wait_ge(S.cstd_ready, 1)
            step(v.reciprocal(crstd, cstd))
            for t in range(TT):
                v.tensor_scalar(tmp[:, t * 512:(t + 1) * 512], PS[:, 4 + t, :], bag[:, 2 * t:2 * t + 1],
                                crstd[:, t:t + 1], ALU.subtract, ALU.mult).then_inc(S.cn_ready, 1)
            dve.wait_ge(S.yc_ready, 4)
            y16 = Y.rearrange("p t (h d) -> p (t h) d", h=8)
            b16 = lambda s_: s_.unsqueeze(2).broadcast_to([P, 16, 64])
            s16 = sqr.rearrange("p (s d) -> p s d", s=16)
            step(v.tensor_reduce(ymean, y16, AX.X, ALU.add))
            step(v.tensor_scalar(ymean, ymean, 1.0 / 64, None, ALU.mult))
            step(v.tensor_tensor(y16, y16, b16(ymean), ALU.subtract))
            step(v.tensor_tensor(s16, y16, y16, ALU.mult))
            step(v.tensor_reduce(ynvar, s16, AX.X, ALU.add))
            v.tensor_scalar(ynvar, ynvar, 1.0 / 64, 64e-5, ALU.mult, ALU.add).then_inc(S.ynvar_ready, 1)
            dve.wait_ge(S.ynstd_ready, 1)
            step(v.reciprocal(ynrstd, ynstd))
            v.tensor_tensor(y16, y16, b16(ynrstd), ALU.mult).then_inc(S.yn_ready, 1)
            dve.wait_ge(S.ynT_done, 1)
            for c in range(4):
                last = v.tensor_scalar(YF[:, 4 + c, :], PS[:, c // 2, c % 2 * T:(c % 2 + 1) * T], pc("lnx_g", c),
                                       pc("lnx_b", c), ALU.mult, ALU.add)
            step(last)
            yt = YF[:, 4:8, :].rearrange("p c t -> p (c t)")
            step(v.tensor_tensor(yt, yt, bonus, ALU.add))
            v.tensor_tensor(yt, yt, g_f, ALU.mult).then_inc(S.yT_ready, 1)
            for n in range(2):
                dve.wait_ge(S.yf_hi, n + 1)
                v.tensor_tensor(h_lo[:, 4 * n:4 * n + 4, :], YF[:, 4 * n:4 * n + 4, :],
                                h_hi[:, 4 * n:4 * n + 4, :].bitcast(F32), ALU.subtract).then_inc(S.yf_ready, 1)
            stats(1, MEM, MEM)
            when_done("w_out", 3)
            to_h(1)
            ynorm(0, 0)
            when_done("km", 0)
            stats(2)
            when_done("vm", 3)
            to_h(2)
            when_done("wq", 3)

            def outputs(a, first, banks):
                dve.wait_ge(S.o_done, a + 1)
                for n in range(banks):
                    dve.wait_ge(S.o_hi, [0, 4, 6][a] + n + 1)
                    cs = slice(first + 2 * n, first + 2 * n + 2)
                    v.tensor_tensor(h_lo[:, cs, :], PS[:, n, :].rearrange("p (c t) -> p c t", c=2),
                                    h_hi[:, cs, :].bitcast(F32), ALU.subtract).then_inc(S.o_ready, 1)

            attention(0, 1.0 / 16, False)
            outputs(0, 0, 4)
            when_done("wo", 3)
            ynorm(1, 4)
            norm(3)
            ffn(0)
            ynorm(2, 0)
            norm(4)
            ffn(1)
            residual(0, 0.5)
            norm(5)
            hd = lambda ap: ap.rearrange("p (s d) -> p s d", s=16)
            for q in range(2):
                when_done("qk"[q], 3)
                dve.wait_ge(S.qk_sq, q + 1)
                qs = slice(q * 16, (q + 1) * 16)
                step(v.tensor_reduce(qkms[:, qs], hd(rt1), AX.X, ALU.add))
                v.tensor_scalar(qkms[:, qs], qkms[:, qs], 1.0 / 128, 1e-6, ALU.mult, ALU.add).then_inc(S.qk_ms, 1)
            for q, (src, gain) in enumerate(((q_r, "q_gain"), (k_r, "k_gain"))):
                split(2 * FIRST["v"] + 3 + q)
                dve.wait_ge(S.qk_std, q + 1)
                qs = slice(q * 16, (q + 1) * 16)
                step(v.reciprocal(qkr[:, qs], qkstd[:, qs]))
                step(v.tensor_tensor(hd(src), hd(src), qkr[:, qs].unsqueeze(2).broadcast_to([P, 16, 128]), ALU.mult))
                step(v.tensor_tensor(hd(src), hd(src), row(gain).unsqueeze(1).broadcast_to([P, 16, 128]), ALU.mult))
                s4 = src.rearrange("p (t h d) -> p t h d", t=TT, h=8)
                w1 = rt1.rearrange("p (t h d) -> p t h d", t=TT, h=8)
                w2 = rt2.rearrange("p (t h d) -> p t h d", t=TT, h=8)
                for t in range(TT):
                    sin = tr[:, 0, t, :].unsqueeze(1).broadcast_to([P, 8, 64])
                    cos = tr[:, 1, t, :].unsqueeze(1).broadcast_to([P, 8, 64])
                    split(cursor[0] if cursor[0] < 2 * FIRST["attn_o"] + 4 else 0)
                    v.tensor_tensor(w1[:, t, :, 0:64], s4[:, t, :, 0:64], cos, ALU.mult)
                    v.tensor_tensor(w1[:, t, :, 64:128], s4[:, t, :, 64:128], cos, ALU.mult)
                    v.tensor_tensor(w2[:, t, :, 0:64], s4[:, t, :, 64:128], sin, ALU.mult)
                    last = v.tensor_tensor(w2[:, t, :, 64:128], s4[:, t, :, 0:64], sin, ALU.mult)
                step(last)
                hs_ = lambda ap, a: hd(ap)[:, :, a:a + 64]
                v.tensor_tensor(hs_(src, 0), hs_(rt1, 0), hs_(rt2, 0), ALU.subtract)
                v.tensor_tensor(hs_(src, 64), hs_(rt1, 64), hs_(rt2, 64), ALU.add).then_inc(S.qk_roped, 1)
            split(2 * FIRST["attn_o"] + 3)
            attention(1, 128 ** -0.5, True)
            outputs(1, 0, 2)
            attention(2, 128 ** -0.5, True)
            outputs(2, 4, 2)
            when_done("attn_o", 3)
            residual(4, 1.0)
            norm(6)
            ffn(2)
            residual(0, 0.5)
            norm(7)
            ffn(3)
            residual(0, 0.5)
            norm(8)
            dve.wait_ge(S.dt_done, 1)
            for t in range(TT):
                last = v.tensor_tensor(dt_[:, t * 32:(t + 1) * 32], PS[:, 4 + t, 0:32], row("dt_bias"), ALU.add)
            step(last)
            step(v.tensor_scalar(dte, dt_, -1.0, None, ALU.mult))
            v.tensor_tensor(dte, dte, dt_, ALU.max).then_inc(S.dt_abs, 1)
            dve.wait_ge(S.dt_ln, 1)
            step(v.scalar_tensor_tensor(dt_, dt_, 0.0, dte, ALU.max, ALU.add))
            dve.wait_ge(S.aneg, 1)
            for t in range(TT):
                last = v.scalar_tensor_tensor(dta[:, t, :], dt_[:, t * 32:(t + 1) * 32], -1.0, aexp, ALU.mult, ALU.mult)
            last.then_inc(S.dta_ready, 1)
            when_done("z", 7)
            dve.wait_ge(S.acs_done, 1)
            step(v.tensor_scalar(nacs, PS[:, 6, 0:64], -1.0, None, ALU.mult))
            v.tensor_tensor(dec0, nacs[:, 0:32], PS[:, 6, 64:96], ALU.add).then_inc(S.acs_ready, 1)
            for c in range(32):
                if c % 2 == 0:
                    when_done("xbc", c // 2)
                dve.wait_ge(S.conv1_ready, c // 2 * 2 + 2)
                ps = PS[:, 4 + c // 2 % 4, c % 2 * T:(c % 2 + 1) * T]
                dst = ctmp[:, c // 2 % 4, c % 2 * T:(c % 2 + 1) * T]
                for back in (1, 2):
                    step(v.scalar_tensor_tensor(dst[:, back:T], ps[:, 0:T - back], pc("sconv_w", (3 - back) * 32 + c),
                                                dst[:, back:T], ALU.mult, ALU.add))
                v.scalar_tensor_tensor(dst[:, 3:T], ps[:, 0:T - 3], pc("sconv_w", c), dst[:, 3:T], ALU.mult,
                                       ALU.add).then_inc(S.conv4_ready, 1)
            dve.wait_ge(S.sT_ready, 10)
            r4 = lambda ap: ap.rearrange("p (r d) -> p r d", r=4)
            b4 = lambda ap: ap.unsqueeze(2).broadcast_to([P, 4, 64])
            dve.wait_ge(S.decay2_done, 2)
            def finish(n):
                g, t = n // 2, n % 2
                b = n % 2
                gs = slice(g * 256, (g + 1) * 256)
                dve.wait_ge(S.g_y, n + 1)
                if n:
                    dve.wait_ge(S.g_yev, n)
                step(v.tensor_tensor(r4(ytmp), r4(xtok[:, t, gs]), b4(row("d_skip")[:, 4 * g:4 * g + 4]), ALU.mult))
                if t:
                    step(v.tensor_tensor(ytmp, ytmp, PS[:, 4 + b, 0:256], ALU.add))
                    step(v.tensor_tensor(r4(y_s[:, t, gs]), r4(PS[:, 7, 0:256]), b4(eacs[:, 4 * g:4 * g + 4]), ALU.mult))
                    v.tensor_tensor(y_s[:, t, gs], y_s[:, t, gs], ytmp, ALU.add).then_inc(S.g_yev, 1)
                else:
                    v.tensor_tensor(y_s[:, t, gs], ytmp, PS[:, 4 + b, 0:256], ALU.add).then_inc(S.g_yev, 1)

            for n in range(2 * G):
                g, t = n // 2, n % 2
                b = n % 2
                gs = slice(g * 256, (g + 1) * 256)
                if n >= 2:
                    dve.wait_ge(S.g_y, n - 1)
                step(v.tensor_tensor(r4(xdt[:, b, :]), r4(xtok[:, t, gs]),
                                     b4(dt_[:, t * 32 + 4 * g:t * 32 + 4 * g + 4]), ALU.mult))
                if t == 0:
                    v.tensor_tensor(r4(xdec[:, g % 2, :]), r4(xdt[:, b, :]), b4(dec0[:, 4 * g:4 * g + 4]), ALU.mult)\
                        .then_inc(S.g_xdec, 1)
                dve.wait_ge(S.g_lt, n + 1)
                v.tensor_tensor(Wd[:, b, :, :], LT[:, b, :, :], PS[:, 2 + b, 0:P].unsqueeze(1).broadcast_to([P, 4, P]),
                                ALU.mult).then_inc(S.g_w, 1)
                if n >= 1:
                    finish(n - 1)
            finish(2 * G - 1)
            dve.wait_ge(S.g_yev, 2 * G)
            yf = y_s.rearrange("p t d -> p (t d)")
            v.tensor_tensor(yf, yf, z_r, ALU.mult).then_inc(S.ys_ready, 1)
            dve.wait_ge(S.ys_sq, 1)
            g16 = lambda ap: ap.rearrange("p (s d) -> p s d", s=16)
            step(v.tensor_reduce(ysms, g16(SQ), AX.X, ALU.add))
            v.tensor_scalar(ysms, ysms, 1.0 / 256, 1e-6, ALU.mult, ALU.add).then_inc(S.ys_ms, 1)
            dve.wait_ge(S.ys_std, 1)
            step(v.reciprocal(ysr, ysstd))
            v.tensor_tensor(g16(yf), g16(yf), ysr.unsqueeze(2).broadcast_to([P, 16, 256]), ALU.mult).then_inc(S.ysn_ready, 1)
            split(2 * FIRST["ssm_out"] + 3)
            for c in range(16):
                if c >= KC:
                    split(2 * FIRST["ssm_out"] + c - KC + 4)
                dve.wait_ge(S.ysT_hi, c // 2 * 2 + 2)
                v.scalar_tensor_tensor(h_lo[:, c % KC, :], PS[:, c // 2 % 4, c % 2 * T:(c % 2 + 1) * T],
                                       pc("ssm_norm", c), h_hi[:, c % KC, :].bitcast(F32), ALU.mult, ALU.subtract)\
                    .then_inc(S.ysT_ready, 1)
            when_done("ssm_out", 7)
            residual(4, 1.0)
            norm(9)
            ffn(4)
            residual(0, 0.5)


def constants():
    import numpy as np
    c = np.zeros((P, NC_), np.float32)

    def put(name, value):
        at, width = CAT[name]
        c[:, at:at + width] = np.asarray(value, np.float32).reshape(P, width)

    i, j = np.arange(P)[:, None], np.arange(P)[None, :]
    s, t = i % CK, np.arange(CK)[None, :]
    put("ident", i == j)
    put("pair", i // HD == j // HD)
    put("ones", np.ones((P, P)))
    put("upper", i <= j)
    put("future", np.where(j < i, -1e30, 0.0))
    q = np.arange(T)[None, :]
    put("causal", np.stack([np.where(q > i + P * tt, -1e30, 0.0) for tt in range(TT)], 1))
    put("s_lt_t", s < t)
    put("s_le_t", s <= t)
    put("eye64", s == t)

    def off(a, b, m):
        return (a > b) & (a // (2 * m) == b // (2 * m)) & (a // m != b // m)

    put("off1T", off(t, s, 1))
    put("off", np.stack([off(s, t, 2 ** lv) for lv in range(6)], 1))
    put("inv_freq", np.broadcast_to(np.float32(10000.0) ** (-np.arange(64, dtype=np.float32) / np.float32(64)), (P, 64)))
    return c


def kernel(**inputs):
    import numpy as np
    import concourse.bacc as bacc
    from concourse.bass_utils import run_bass_kernel_spmd

    a = {name: np.asarray(value) for name, value in inputs.items()}

    def feat(w):
        n = w.shape[1] // 256
        return w.reshape(KC, P, n, 2, P).transpose(2, 1, 3, 0, 4).reshape(n, P, 2048)

    def rows(w):
        n = w.shape[0] // 256
        return w.reshape(n, 2, P, 1024).transpose(0, 2, 1, 3).reshape(n, P, 2048)

    def ffn(gate, up, down):
        g, u, d = feat(gate), feat(up), rows(down)
        order = [g[0], u[0]]
        for b in range(1, NB):
            order += [g[b], u[b], d[b - 1]]
        return np.stack(order + [d[NB - 1]])

    wkv, gu, qkv, win2 = a["wkv"][0], a["w_gu"][0], a["attn_w_qkv_2"][0], a["ssm_w_in_2"][0]

    def ffn2(which, i):
        return ffn(a[f"ffn{which}_w_gate_2"][i], a[f"ffn{which}_w_up_2"][i], a[f"ffn{which}_w_down_2"][i])

    parts = {"w_in": feat(np.concatenate([a["w_in_first"][:, D:], a["w_in_first"][:, :D]], 1)), "km": feat(wkv[:, :D]), "vm": rows(wkv[:, D:]), "w_out": rows(a["w_out"][0]),
             "wq": feat(a["wq"][0]), "wo": rows(a["wo"][0]), "ffn0": ffn(gu[:, :FF], gu[:, FF:], a["w_down"][0]),
             "ffn1": ffn2(1, 0), "q": rows(qkv[:, :D]), "k": rows(qkv[:, D:2 * D]), "v": rows(qkv[:, 2 * D:]),
             "attn_o": rows(a["attn_w_o_2"][0]), "ffn2": ffn2(2, 0), "ffn3": ffn2(1, 1),
             "z": np.concatenate([rows(win2[:, :1024]), rows(win2[:, 1024:2048])]),
             "xbc": feat(win2[:, 2048:6144]), "ssm_out": rows(a["ssm_w_out_2"][0]), "ffn4": ffn2(2, 1)}
    W = np.concatenate([parts[name] for name, _ in STREAM])
    assert W.shape == (NSLOTS, P, 2048)

    def col(w):
        return w.reshape(-1, P).T

    g = a["norm_gains"][0]
    f1, mx, f2 = a["ffn1_norm_2"], a["mix_norm_2"], a["ffn2_norm_2"]
    gains = [g[0], a["mem_norm_g"], g[2], g[4], f1[0], mx[0], f2[0], f1[1], mx[1], f2[1]]
    wa = np.concatenate([a["w_up"][0], a["a_up"][0]], 0)
    wdt = win2[:, 6144:].reshape(KC, P, 32).transpose(1, 0, 2).reshape(P, 256)
    values = {"gain": col(np.concatenate(gains)), "ssm_norm": col(a["ssm_norm_2"][0]), "mu": col(a["mu_first"]),
              "w0": col(a["w0"][0]), "a0": col(a["a0"][0]), "k_k": col(a["k_k"][0]), "k_a": col(a["k_a"][0]),
              "r_k": col(a["r_k"][0].reshape(-1)), "lnx_g": col(a["lnx_g"][0]), "lnx_b": col(a["lnx_b"][0]),
              "conv_w": col(a["conv_w"][0].reshape(-1)), "conv_b": col(a["conv_b"][0]), "ln_g": col(a["conv_ln_g"][0]),
              "ln_b": col(a["conv_ln_b"][0]), "sconv_w": col(a["ssm_conv_w_2"][0].reshape(-1)),
              "sconv_b": col(a["ssm_conv_b_2"][0]), "wa_up": wa, "g_up": a["g_up"][0], "w_dt": wdt}
    cols = np.ascontiguousarray(np.concatenate([values[n] for n, _ in PCOLS], 1))
    rvals = {"q_gain": a["attn_q_norm_2"][0], "k_gain": a["attn_k_norm_2"][0],
             "dt_bias": a["ssm_dt_bias_2"][0], "a_log": a["ssm_a_log_2"][0], "d_skip": a["ssm_d_2"][0]}
    rws = np.concatenate([rvals[n] for n, _ in PROWS])[None, :]
    arrays = {"W": W, "cols": cols, "rows": rws, "post_gains": np.ascontiguousarray(g[1::2]), "consts": constants(), "x": np.ascontiguousarray(a["x"][0]),
              "mem": np.ascontiguousarray(a["mem"][0]),
              "pos": np.ascontiguousarray(a["positions_2"][0].reshape(TT, P).T.astype(np.int32))}

    nc = bacc.Bacc("TRN2", target_bir_lowering=False, num_devices=1)
    ins = [nc.dram_tensor(n, v.shape, mybir.dt.from_np(v.dtype), kind="ExternalInput").ap() for n, v in arrays.items()]
    out = nc.dram_tensor("out", (T, D), F32, kind="ExternalOutput").ap()
    build_program(nc, *ins, out)
    r = run_bass_kernel_spmd(nc, [arrays], core_ids=[0])
    return r.results[0]["out"].reshape(1, T, D)
```

```python
import math
from collections import namedtuple
from contextlib import ExitStack

import concourse.bass as bass
from concourse import mybir

F32 = mybir.dt.float32
F32R = mybir.dt.float32r
I32 = mybir.dt.int32
ALU = mybir.AluOpType
ACT = mybir.ActivationFunctionType
AX = mybir.AxisListType

P = 128
T = 256
TT = T // P
D = 1024
KC = D // P
FF = 2816
NB = FF // 256
HD = 64
CK = 64
NCK = T // CK
G = 8
R = 3
H = 4
LOOP = 12
DECAY = math.exp(-0.5)

STREAM = [("w_in", 11), ("w_out", 4), ("km", 4), ("vm", 4), ("wq", 4), ("wo", 4), ("ffn0", 33), ("ffn1", 33),
          ("q", 4), ("k", 4), ("v", 4), ("attn_o", 4), ("ffn2", 33), ("ffn3", 33),
          ("z", 8), ("xbc", 16), ("ssm_out", 8), ("ffn4", 33)]
FIRST = {}
_n = 0
for _name, _count in STREAM:
    FIRST[_name] = _n
    _n += _count
NSLOTS = _n

PCOLS = [("gain", 80), ("ssm_norm", 16), ("mu", 14), ("w0", 4), ("a0", 4), ("k_k", 4), ("k_a", 4), ("r_k", 4),
         ("lnx_g", 4), ("lnx_b", 4), ("conv_w", 124), ("conv_b", 4), ("ln_g", 4), ("ln_b", 4),
         ("sconv_w", 128), ("sconv_b", 32), ("wa_up", 512), ("g_up", 512), ("w_dt", 256)]
PROWS = [("q_gain", 128), ("k_gain", 128), ("dt_bias", 32), ("a_log", 32),
         ("d_skip", 32)]
CCOLS = [("ident", 128), ("pair", 128), ("ones", 128), ("upper", 128), ("future", 128), ("causal", 512),
         ("s_lt_t", 64), ("s_le_t", 64), ("eye64", 64), ("off1T", 64), ("off", 384), ("inv_freq", 64), ("zeros", 64)]


def offsets(table):
    at, out = 0, {}
    for name, width in table:
        out[name] = (at, width)
        at += width
    return out, at


PAT, NP_ = offsets(PCOLS)
RAT, NR_ = offsets(PROWS)
CAT, NC_ = offsets(CCOLS)


def build_program(nc, W, cols, rows, post_gains, consts, x_in, mem_in, pos_in, out):
    with ExitStack() as ctx:
        def sb(name, words, dt=F32):
            return ctx.enter_context(nc.sbuf_tensor(name, [P, words], dt))

        def sem(name):
            return ctx.enter_context(nc.semaphore(name))

        raw = sb("raw_weights", R * 2048)[:].rearrange("p (h n) -> p h n", n=1024)
        w_hi = sb("w_hi", H * 1024, F32R)[:].rearrange("p (h n) -> p h n", n=1024)
        w_lo = sb("w_lo", H * 1024, F32R)[:].rearrange("p (h n) -> p h n", n=1024)
        h_hi = sb("h_hi", KC * T, F32R)[:].rearrange("p (c t) -> p c t", c=KC)
        h_lo = sb("h_lo", KC * T, F32R)[:].rearrange("p (c t) -> p c t", c=KC)
        g_hi = sb("g_hi", 1024, F32R)[:].rearrange("p (q j t) -> p q j t", q=2, j=2)
        g_lo = sb("g_lo", 1024, F32R)[:].rearrange("p (q j t) -> p q j t", q=2, j=2)
        X = sb("x_resid", TT * D)[:].rearrange("p (t d) -> p t d", t=TT)
        xn_t = sb("x_normed", TT * D)
        xn = xn_t[:].rearrange("p (t d) -> p t d", t=TT)
        sg_t = sb("silu_gate", 1024)
        sg = sg_t[:].rearrange("p (q n) -> p q n", q=2)
        post_gain = sb("post_gain", D)
        ptab = sb("ptab", NP_)
        rtab = sb("rtab", NR_)
        ctab = sb("ctab", NC_)
        small = sb("small", 1400)
        pos_i = sb("pos_i", TT, I32)
        ARENA = 20500
        arena = sb("arena", ARENA)
        rounded = sb("rounded", 512, F32R)
        ident_r, future_r, upper_r = [rounded[:, i * P:(i + 1) * P] for i in range(3)]
        dta_hi = rounded[:, 384:448].rearrange("p (t h) -> p t h", t=TT)
        dta_lo = rounded[:, 448:512].rearrange("p (t h) -> p t h", t=TT)
        PS = ctx.enter_context(nc.psum_tensor("PS", [P, 8, 512], F32))

        def pc(name, i=0, n=1):
            at = PAT[name][0] + i
            return ptab[:, at:at + n]

        def row(name):
            at, w = RAT[name]
            return rtab[:, at:at + w]

        def cn(name, i=0, n=None):
            at, w = CAT[name]
            n = w if n is None else n
            return ctab[:, at + i:at + i + n]

        ident = cn("ident")

        used_small = [0]

        def sm(n):
            used_small[0] += n
            assert used_small[0] <= 1400
            return small[:, used_small[0] - n:used_small[0]]

        ssq, ms, std, rstd = sm(4), sm(2), sm(2), sm(2)
        warm = sm(1)
        yssq, yms, ystd, yrstd = sm(4), sm(2), sm(2), sm(2)

        def region(at, words):
            assert at + words <= ARENA, (at, words)
            return arena[:, at:at + words]

        o = 0
        pin_r = region(o, 3598); o += 3598
        pin = pin_r[:, 0:2056].rearrange("p (q c t) -> p q c t", q=4, c=2)
        Pc = pin_r[:, 2056:3096].rearrange("p (s t) -> p s t", s=16)
        bonus = pin_r[:, 0:1024]
        Q_r = region(o, 3584); o += 3584
        Q = Q_r.rearrange("p (c t) -> p c t", c=14)
        r_f, k_f, v_f = Q_r[:, 0:1024], Q_r[:, 1024:2048], Q_r[:, 2048:3072]
        conv = region(o, 1024); o += 1024
        usig = conv
        MEM = region(o, 2048).rearrange("p (t d) -> p t d", t=TT)
        glu = region(o, 1024); o += 1024
        decay = region(o, 1024); o += 1024
        a_f = region(o, 1024); o += 1024
        g_f = region(o, 1024); o += 1024
        kk = region(o, 1024); o += 1024
        V_t = region(o, 1024).rearrange("p (t d) -> p t d", t=TT); o += 1024
        K_t = xn_t[:, 0:1024].rearrange("p (t d) -> p t d", t=TT)
        B_t = xn_t[:, 1024:2048].rearrange("p (t d) -> p t d", t=TT)
        kept = [region(o + 512 * i, 512) for i in range(8)]; o += 8 * 512
        invP = arena[:, o - 4 * 512:o - 2 * 512]
        newton = arena[:, o - 6 * 512:o - 4 * 512]
        MTs, RKTs, RBTs, XiTs = kept[0:2], kept[2:4], kept[4:6], kept[6:8]
        NL, Xi = decay[:, 0:512], decay[:, 512:1024]
        Loff, Qi = sg_t[:, 0:512], sg_t[:, 512:1024]
        Zn = region(o, 1024).rearrange("p (q c v) -> p q c v", q=2, c=4); o += 1024
        RU, U = v_f[:, 0:512], v_f[:, 512:1024]
        Y = k_f.rearrange("p (t d) -> p t d", t=TT)
        sqr = a_f
        tshift = kept[0]
        tmp = region(o, 1024); o += 1024
        tmpb = V_t.rearrange("p t d -> p (t d)")
        NLs, Xis = (NL, k_f[:, 0:512]), (Xi, k_f[:, 512:1024])
        Loffs, Qis = (Loff, a_f[:, 0:512]), (Qi, a_f[:, 512:1024])
        YF_r = xn_t[:]
        YF = YF_r.rearrange("p (c t) -> p c t", c=KC)
        qT = region(0, 2048).rearrange("p (c t) -> p c t", c=KC)
        kT2 = region(2048, 2048).rearrange("p (c t) -> p c t", c=KC)
        v2 = region(4096, 2048).rearrange("p (t d) -> p t d", t=TT)
        q_r = region(6144, 2048)
        k_r = region(8192, 2048)
        kmT = region(14336, 2048).rearrange("p (c t) -> p c t", c=KC)
        vm = region(16384, 2048).rearrange("p (t d) -> p t d", t=TT)
        prob = region(10240, 2048).rearrange("p (s m) -> p s m", s=8)
        probT = region(12288, 2048).rearrange("p (h k t) -> p h k t", h=4, k=2)
        rt1 = region(14336, 2048)
        rt2 = region(16384, 2048)
        o = 0
        xsT_r = region(o, 4096); o += 4096
        xsT = xsT_r.rearrange("p (c t) -> p c t", c=16)
        y_s = xsT_r.rearrange("p (t d) -> p t d", t=TT)
        bcT = region(o, 4096).rearrange("p (c t) -> p c t", c=16); o += 4096
        xtok_r = region(o, 4096); o += 4096
        xtok = xtok_r.rearrange("p (t d) -> p t d", t=TT)
        z_r = region(o, 4096); o += 4096
        z_s = z_r.rearrange("p (t d) -> p t d", t=TT)
        Btok = region(o, 1024).rearrange("p (g n) -> p g n", g=G); o += 1024
        ctmp = xn_t[:].rearrange("p (q n) -> p q n", q=4)
        LT = xn_t[:, 0:1024].rearrange("p (q r l) -> p q r l", q=2, r=4)
        Wd = xn_t[:, 1024:2048].rearrange("p (q r l) -> p q r l", q=2, r=4)
        xdt = region(o, 512).rearrange("p (q n) -> p q n", q=2); o += 512
        xdec = region(o, 512).rearrange("p (q n) -> p q n", q=2); o += 512
        stT = region(o, 512).rearrange("p (q n) -> p q n", q=2); o += 512
        dx = region(o, 512).rearrange("p (q n) -> p q n", q=2); o += 512
        junk = region(o, 256); o += 256
        posf, trig, turns = sm(TT), sm(256), sm(256)
        nmax, psum_, rsum = sm(8), sm(8), sm(8)
        qkms, qkstd, qkr = sm(32), sm(32), sm(32)
        dta_r, dt_, dte, aexp = sm(64), sm(64), sm(64), sm(32)
        dta = dta_r.rearrange("p (t h) -> p t h", t=TT)
        nacs, dec0, eacs = sm(64), sm(32), sm(32)
        cvar, cstd, crstd, bst, bag = sm(2), sm(2), sm(2), sm(12), sm(4)
        ymean, ynvar, ynstd, ynrstd = sm(16), sm(16), sm(16), sm(16)
        ysms, ysstd, ysr = sm(16), sm(16), sm(16)

        NAMES = ("half_done hi_ready lo_ready hT_hi g_mult g_hi_ready yf_ready yf_hi o_hi o_ready ysT_hi conv1_ready rounded_ready warm_ready x_part y_first g_dx dsplit_hi ysn_done gain_loaded gain_read "
                 "params_loaded x_loaded mem_loaded pos_loaded out_stored dve_step act_step "
                 "ssq_ready ms_ready std_ready xn_ready xT_ready hT_ready x_ready silu_ready act_ready "
                 "yssq_ready yms_ready ystd_ready pad_ready pin_ready usig_ready glu_ready q_mixed lora_ready "
                 "wa_done g_done decay_ready a_ready g_ready kmT_ready vm_ready "
                 "kkraw_ready kksq_ready kksum_done kkmax_ready kknorm_ready bonus_in bonus_sum_done "
                 "ab_ready tok_done tok_ready gram_done gram_ready invq_done invq_ready invx_done inv_ready "
                 "ru_done ru_ready u_done u_ready z_done z_ready yc_done yc_ready yn_sq ynvar_ready ynstd_ready "
                 "yn_ready ynT_done yT_ready conv_ready convT_done cvar_ready cstd_ready cn_ready cnT_done "
                 "convY_ready kk_std "
                 "score_done nmax_ready exp_ready prob_ready probT_done probT_ready o_done qT_ready "
                 "consts_loaded sin_ready qk_normed kk_ln kk_rstd rows_loaded diff_ready kk_used scan_done invP_ready rk_ready g_sum qk_evac qk_sq qk_ms qk_std qk_roped qkT_done qkT_ready v_ready ang_ready trig_ready "
                 "dt_done dt_abs dt_exp dt_ln aneg dta_ready acs_done acs_ready decay2_done "
                 "conv4_ready xbc_ready z_ready2 sT_done sT_ready g_cb g_lt g_w g_y g_st g_stready g_xdt g_xdec g_yev "
                 "ys_ready ys_sq ys_ms ys_std ysn_ready ysT_done ysT_ready").split()
        S = namedtuple("Signals", NAMES)(*[sem(n) for n in NAMES])
        loaded = [sem(f"loaded{r}") for r in range(R)]

        def done(eng, name, slot, i=0):
            eng.wait_ge(S.half_done, LOOP * i + 2 * (FIRST[name] + slot) + 2)

        def ffn_half(f, kind, b):
            at = {"G": 3 * b - 1 if b else 0, "U": 3 * b if b else 1, "D": 3 * b + 4 if b < NB - 1 else 32}[kind]
            return 2 * (FIRST[f"ffn{f}"] + at)

        block = ctx.enter_context(nc.Block())

        W3 = W.rearrange("s p (h n) -> s p h n", h=2)

        @block.gpsimd
        def _(pool):
            tt = nc.gpsimd.tensor_tensor
            c16 = lambda ap: ap.rearrange("p (s t) -> p s t", s=16)
            for k in range(3):
                if k:
                    pool.wait_ge(S.gain_read, k)
                else:
                    pool.wait_ge(S.pin_ready, 1)
                pool.dma_start(post_gain[:], post_gains[k:k + 1, :].broadcast_to([P, D])).then_inc(S.gain_loaded, 16)
                if k == 0:
                    for n in range(7):
                        if n == 3:
                            pool.wait_ge(S.kkraw_ready, 1)
                            tt(tmp, kk, kk, ALU.mult).then_inc(S.kksq_ready, 1)
                        pool.wait_ge(S.pin_ready, 1 + n)
                        if n:
                            pool.wait_ge(S.q_mixed, n)
                        tt(tshift.rearrange("p (c t) -> p c t", c=2), pin[:, n % 4, :, 0:T], pin[:, n % 4, :, 1:T + 1],
                            ALU.subtract).then_inc(S.diff_ready, 1)
                    pool.wait_ge(S.bonus_in, 1)
                    pool.wait_ge(S.scan_done, 1)
                    tt(c16(r_f), c16(r_f), Pc[:, :, 1:65], ALU.mult)
                    pool.wait_ge(S.invP_ready, 1)
                    tt(k_f, k_f, invP, ALU.mult).then_inc(S.rk_ready, 1)
                    pool.wait_ge(S.kk_used, 1)
                    tt(c16(kk), c16(kk), Pc[:, :, 0:64], ALU.mult).then_inc(S.rk_ready, 1)
                    pool.wait_ge(S.pin_ready, 11)
                    tt(glu, glu, usig, ALU.mult).then_inc(S.glu_ready, 1)
                    pool.wait_ge(S.conv_ready, 1)
                    pool.wait_ge(S.inv_ready, 12)
                    pool.dma_start(MEM, mem_in.rearrange("(t p) d -> p t d", p=P)).then_inc(S.mem_loaded, 16)

            tr = trig.rearrange("p (s t f) -> p s t f", s=2, t=TT)
            pool.wait_ge(S.trig_ready, 1)
            for q, src in enumerate((q_r, k_r)):
                s4 = src.rearrange("p (t h d) -> p t h d", t=TT, h=8)
                w2 = rt2.rearrange("p (t h d) -> p t h d", t=TT, h=8)
                pool.wait_ge(S.qk_normed, q + 1)
                if q:
                    pool.wait_ge(S.qk_roped, q)
                for t in range(TT):
                    sin = tr[:, 0, t, :].unsqueeze(1).broadcast_to([P, 8, 64])
                    tt(w2[:, t, :, 0:64], s4[:, t, :, 64:128], sin, ALU.mult)
                    last = tt(w2[:, t, :, 64:128], s4[:, t, :, 0:64], sin, ALU.mult)
                last.then_inc(S.sin_ready, 1)

            pool.wait_ge(S.rows_loaded, 16)
            pool.wait_ge(S.sT_ready, 10)
            pool.wait_ge(S.decay2_done, 2)
            r4 = lambda ap: ap.rearrange("p (r d) -> p r d", r=4)
            b4 = lambda ap: ap.unsqueeze(2).broadcast_to([P, 4, 64])

            def gate(n):
                g, t = n // 2, n % 2
                y = y_s[:, t, g * 256:(g + 1) * 256]
                pool.wait_ge(S.g_sum, n + 1)
                tt(y, y, z_s[:, t, g * 256:(g + 1) * 256], ALU.mult).then_inc(S.g_yev, 1)

            for n in range(2 * G):
                g, t = n // 2, n % 2
                b = n % 2
                gs = slice(g * 256, (g + 1) * 256)
                if n >= 2:
                    pool.wait_ge(S.g_y, n - 1)
                tt(r4(xdt[:, b, :]), r4(xtok[:, t, gs]), b4(dt_[:, t * 32 + 4 * g:t * 32 + 4 * g + 4]), ALU.mult)\
                    .then_inc(S.g_xdt, 1)
                if t == 0:
                    pool.wait_ge(S.g_xdt, n + 1)
                    tt(r4(xdec[:, g % 2, :]), r4(xdt[:, b, :]), b4(dec0[:, 4 * g:4 * g + 4]), ALU.mult)\
                        .then_inc(S.g_xdec, 1)
                if n >= 2:
                    pool.wait_ge(S.g_sum, n - 1)
                tt(r4(dx[:, b, :]), r4(xtok[:, t, gs]), b4(row("d_skip")[:, 4 * g:4 * g + 4]), ALU.mult)\
                    .then_inc(S.g_dx, 1)
                if n >= 2:
                    gate(n - 2)
            gate(2 * G - 2)
            gate(2 * G - 1)

        @block.sync
        def _(sp):
            sp.dma_start(X, x_in.rearrange("(t p) d -> p t d", p=P)).then_inc(S.x_loaded, 16)
            for n in range(R):
                if n == 1:
                    sp.wait_ge(S.params_loaded, 16)
                sp.dma_start(raw[:, 2 * n:2 * n + 2, :], W3[n]).then_inc(loaded[n], 16)
            with sp.Fori(1, NSLOTS // R) as i:
                for r in range(R):
                    sp.wait_ge(S.lo_ready, i * (2 * R) + (2 * r + 2 - 2 * R))
                    sp.dma_start(raw[:, 2 * r:2 * r + 2, :], W3[i * R + r]).then_inc(loaded[r], 16)
            for n in range(NSLOTS // R * R, NSLOTS):
                sp.wait_ge(S.lo_ready, 2 * (n - R) + 2)
                sp.dma_start(raw[:, 2 * (n % R):2 * (n % R) + 2, :], W3[n]).then_inc(loaded[n % R], 16)
            sp.wait_ge(S.x_part, 36)
            sp.dma_start(out.rearrange("(t p) d -> p t d", p=P), X).then_inc(S.out_stored, 16)
            sp.wait_ge(S.out_stored, 16)

        @block.tensor
        def _(pe):
            mm = nc.tensor.matmul

            def norm(k, src=xn):
                pe.wait_ge(S.xn_ready, 2 * (k + 1))
                for c in range(KC):
                    for t in range(TT):
                        at = c % 2 * 256 + t * P
                        last = nc.tensor.transpose(PS[:, 4 + c // 2, at:at + P], src[:, t, c * P:(c + 1) * P], ident)
                    if c % 2:
                        last.then_inc(S.xT_ready, 1)

            def products(out, lhs, rhs, start, stop):
                mm(out, lhs[0], rhs[0], start=start, stop=False)
                mm(out, lhs[0], rhs[1], start=False, stop=False)
                return mm(out, lhs[1], rhs[0], start=False, stop=stop)

            def feat_half(n, bank, j, i=0, normed=None):
                pe.wait_ge(S.lo_ready, LOOP * i + n + 1)
                for c in range(KC):
                    if normed is not None and c % 2 == 0:
                        pe.wait_ge(S.hT_ready, 8 * normed + c + 2)
                    cs = slice(c * P, (c + 1) * P)
                    last = products(PS[:, bank, j * T:(j + 1) * T], (w_hi[:, n % H, cs], w_lo[:, n % H, cs]),
                                    (h_hi[:, c, :], h_lo[:, c, :]), c == 0, c == KC - 1)
                last.then_inc(S.half_done, 1)

            def feat_slot(n, bank, i=0, normed=None):
                feat_half(n, bank, 0, i, normed)
                feat_half(n + 1, bank, 1, i)

            def rows_half(n, hi, lo, bank, start, stop, i=0, last_of_x=False):
                pe.wait_ge(S.lo_ready, LOOP * i + n + 1)
                for t in range(TT):
                    ts = slice(t * P, (t + 1) * P)
                    for h in range(2):
                        hs = slice(h * 512, (h + 1) * 512)
                        last = products(PS[:, bank + 2 * t + h, :], (hi[:, ts], lo[:, ts]),
                                        (w_hi[:, n % H, hs], w_lo[:, n % H, hs]), start, stop)
                    if last_of_x and t == 0:
                        last.then_inc(S.y_first, 1)
                last.then_inc(S.half_done, 1)

            def rows_matrix(name, bank, n=4, first=0, normed=None, last_of_x=False):
                for j in range(2 * n):
                    if normed is not None:
                        pe.wait_ge(S.hT_ready, 8 * normed + j + 1)
                    rows_half(2 * (FIRST[name] + first) + j, h_hi[:, j % KC, :], h_lo[:, j % KC, :], bank, j == 0,
                              j == 2 * n - 1, 0, last_of_x and j == 2 * n - 1)

            def ffn(f):
                k = [3, 4, 6, 7, 9][f]

                def gate_up(b, i=0, ii=0):
                    if b >= 2:
                        pe.wait_ge(S.act_ready, ii * 2 + (NB * f + b - 1))
                    feat_slot(ffn_half(f, "G", b), 4 + 2 * (b % 2), i, None if b else k)
                    feat_slot(ffn_half(f, "U", b), 5 + 2 * (b % 2), i)

                def down(b, i=0, ii=0):
                    pe.wait_ge(S.act_ready, ii * 2 + (NB * f + b + 1))
                    for j in range(2):
                        rows_half(ffn_half(f, "D", b) + j, g_hi[:, b % 2, j, :], g_lo[:, b % 2, j, :], 0,
                                  b == 0 and j == 0, b == NB - 1 and j == 1, i, b == NB - 1 and j == 1)

                gate_up(0)
                gate_up(1)
                down(0)
                with pe.Fori(0, (NB - 3) // 2) as i:
                    for b in (1, 2):
                        gate_up(b + 1, i, i)
                        down(b, i, i)
                gate_up(NB - 1)
                down(NB - 2)
                down(NB - 1)

            def attention(a, src_q, src_k, src_v, dtiles, first, causal):
                for h in range(4):
                    for t in range(TT):
                        keys = P if causal and t == 0 else T
                        out_ = PS[:, h, t * T:t * T + keys]
                        if causal:
                            mm(PS[:, h, t * T + t * P:t * T + (t + 1) * P], future_r, ident_r, start=True, stop=False)
                            parts = [slice(t * P, (t + 1) * P)] + ([slice(0, P)] if t else [])
                        else:
                            parts = [slice(0, T)]
                        for q, ks in enumerate(parts):
                            for j in range(dtiles):
                                c = (first + h) * dtiles + j
                                last = mm(PS[:, h, t * T + ks.start:t * T + ks.stop], src_q[:, c, t * P:(t + 1) * P],
                                          src_k[:, c, ks], start=j == 0 and not (causal and q == 0),
                                          stop=j == dtiles - 1)
                    last.then_inc(S.score_done, 1)

                def transposed(h):
                    pe.wait_ge(S.prob_ready, 4 * a + h + 1)
                    for m in range(2):
                        for t in range(TT):
                            if causal and m > t:
                                continue
                            at = m * T + t * P
                            last = nc.tensor.transpose(PS[:, 4 + h, at:at + P],
                                                       prob[:, 2 * h + t, m * P:(m + 1) * P], ident)
                    last.then_inc(S.probT_done, 1)

                def output(h):
                    pe.wait_ge(S.probT_ready, 4 * a + h + 1)
                    for j in range(dtiles):
                        c = (first + h) * dtiles + j
                        o_ = h * dtiles + j
                        at = o_ % 2 * T
                        for m in range(2):
                            t0 = m * P if causal else 0
                            last = mm(PS[:, o_ // 2, at + t0:at + T], src_v[:, m, c * P:(c + 1) * P],
                                      probT[:, h, m, t0:T], start=m == 0, stop=m == 1)
                    if dtiles == 2 or h % 2:
                        last.then_inc(S.o_done, 1)

                transposed(0)
                for h in range(1, 4):
                    transposed(h)
                    output(h - 1)
                output(3)

            pe.wait_ge(S.consts_loaded, 16)
            norm(0)
            pe.wait_ge(S.params_loaded, 16)
            for n in range(11):
                if n >= 4:
                    pe.wait_ge(S.pin_ready, n - 3)
                feat_slot(2 * n, n % 4, 0, None if n else 0)
                if n == 2:
                    pe.wait_ge(S.lora_ready, 3)
                    for q, rows_ in enumerate((slice(0, 64), slice(64, 128))):
                        for c in range(4):
                            at = PAT["wa_up"][0] + c * P
                            last = mm(PS[:, 4 + 2 * q + c // 2, c % 2 * T:(c % 2 + 1) * T], ptab[rows_, at:at + P],
                                      Q[rows_, 12, :], start=True, stop=True)
                    last.then_inc(S.wa_done, 1)
                if n == 4:
                    pe.wait_ge(S.a_ready, 1)
                    for c in range(4):
                        last = mm(PS[:, 6 + c // 2, c % 2 * T:(c % 2 + 1) * T], pc("g_up", c * P, P), Q[:, 13, :],
                                  start=True, stop=True)
                    last.then_inc(S.g_done, 1)
                    pe.wait_ge(S.kksq_ready, 1)
                    for c in range(2):
                        last = mm(PS[:, 4 + c, :], cn("pair"), tmp[:, c * 512:(c + 1) * 512], start=True, stop=True)
                    last.then_inc(S.kksum_done, 1)
                if n == 8:
                    pe.wait_ge(S.bonus_in, 1)
                    for c in range(2):
                        last = mm(PS[:, 4 + c, :], cn("pair"), tmpb[:, c * 512:(c + 1) * 512], start=True, stop=True)
                    last.then_inc(S.bonus_sum_done, 1)
            pe.wait_ge(S.pin_ready, 11)
            pe.wait_ge(S.ab_ready, 1)
            pe.wait_ge(S.rk_ready, 2)
            pe.wait_ge(S.g_ready, 1)
            banks = [0, 1, 2, 3, 6, 7]
            for q, src in enumerate((v_f, k_f, a_f)):
                for t in range(TT):
                    for c in range(4):
                        last = nc.tensor.transpose(PS[:, banks[2 * q + t], c * P:(c + 1) * P],
                                                   src[:, c * T + t * P:c * T + (t + 1) * P], ident)
            last.then_inc(S.tok_done, 1)
            pe.wait_ge(S.tok_ready, 6)

            def chunks(t):
                for h in range(8):
                    for ch in range(2):
                        yield h, ch, h // 2, 64 * (h % 2), 64 * ch, t * P + 64 * ch

            def gram(bank, lhs, rhs, t, at=0):
                for h, ch, c, hp, cp, tok in chunks(t):
                    last = mm(PS[cp:cp + 64, bank + h % 2, at + c * 64:at + (c + 1) * 64],
                              lhs[hp:hp + 64, c * T + tok:c * T + tok + 64],
                              rhs[hp:hp + 64, c * T + tok:c * T + tok + 64], start=True, stop=True)
                return last

            def blockmul(bank, lhs, rhs, t):
                for h, ch, c, hp, cp, tok in chunks(t):
                    last = mm(PS[cp:cp + 64, bank, h * 64:(h + 1) * 64], lhs[cp:cp + 64, h * 64:(h + 1) * 64],
                              rhs[cp:cp + 64, h * 64:(h + 1) * 64], start=True, stop=True)
                return last

            At, Rt, Kt, Bt = kk, r_f, k_f, a_f
            for t in range(TT):
                if t:
                    pe.wait_ge(S.gram_ready, 1)
                gram(0, At, Bt, t)
                gram(0, Bt, At, t, 256)
                gram(2, Kt, At, t)
                gram(2, Kt, Rt, t, 256)
                gram(6, Bt, Rt, t).then_inc(S.gram_done, 1)
            pe.wait_ge(S.gram_ready, 2)
            for lv in range(5):
                for t in range(TT):
                    pe.wait_ge(S.inv_ready, 2 * lv + t + 1)
                    blockmul(3 * t, Loffs[t], XiTs[t], t).then_inc(S.invq_done, 1)
                for t in range(TT):
                    pe.wait_ge(S.invq_ready, 2 * lv + t + 1)
                    last = blockmul(3 * t + 1, Xis[t], Qis[t], t)
                    if lv < 4:
                        last = blockmul(3 * t + 2, Qis[t], Xis[t], t)
                    last.then_inc(S.invx_done, 1)
            pe.wait_ge(S.inv_ready, 12)
            for g in range(NCK):
                t, cp = g // 2, 64 * (g % 2)
                MT, RKT, RBT, XiT = MTs[t], RKTs[t], RBTs[t], XiTs[t]
                Z = Zn[:, (g - 1) % 2, :, :]
                tok = t * P + cp
                if g:
                    pe.wait_ge(S.z_ready, g)
                for c in range(4):
                    if g:
                        mm(PS[cp:cp + 64, 0, c * P:(c + 1) * P], At[:, c * T + tok:c * T + tok + 64], Z[:, c, :],
                           start=True, stop=False)
                    for h in (2 * c, 2 * c + 1):
                        last = mm(PS[cp:cp + 64, 0, h * 64:(h + 1) * 64], MT[cp:cp + 64, h * 64:(h + 1) * 64],
                                  V_t[cp:cp + 64, t, h * 64:(h + 1) * 64], start=g == 0, stop=g == 0 or h % 2 == 1)
                last.then_inc(S.ru_done, 1)
                pe.wait_ge(S.ru_ready, g + 1)
                for h in range(8):
                    last = mm(PS[cp:cp + 64, 1, h * 64:(h + 1) * 64], XiT[cp:cp + 64, h * 64:(h + 1) * 64],
                              RU[cp:cp + 64, h * 64:(h + 1) * 64], start=True, stop=True)
                last.then_inc(S.u_done, 1)
                pe.wait_ge(S.u_ready, g + 1)
                if g < NCK - 1:
                    for c in range(4):
                        cs = slice(c * P, (c + 1) * P)
                        mm(PS[:, 3, cs], K_t[cp:cp + 64, t, cs], V_t[cp:cp + 64, t, cs], start=True, stop=False)
                        if g:
                            mm(PS[:, 3, cs], ident, Z[:, c, :], start=False, stop=False)
                        last = mm(PS[:, 3, cs], B_t[cp:cp + 64, t, cs], U[cp:cp + 64, cs], start=False, stop=True)
                    last.then_inc(S.z_done, 1)
                if g:
                    pe.wait_ge(S.yc_ready, g)
                for c in range(4):
                    if g:
                        mm(PS[cp:cp + 64, 2, c * P:(c + 1) * P], Rt[:, c * T + tok:c * T + tok + 64], Z[:, c, :],
                           start=True, stop=False)
                    for h in (2 * c, 2 * c + 1):
                        hs = slice(h * 64, (h + 1) * 64)
                        mm(PS[cp:cp + 64, 2, hs], RKT[cp:cp + 64, hs], V_t[cp:cp + 64, t, hs], start=g == 0,
                           stop=False)
                        last = mm(PS[cp:cp + 64, 2, hs], RBT[cp:cp + 64, hs], U[cp:cp + 64, hs], start=False,
                                  stop=g == 0 or h % 2 == 1)
                last.then_inc(S.yc_done, 1)
            pe.wait_ge(S.conv_ready, 1)
            for t in range(TT):
                for c in range(4):
                    last = nc.tensor.transpose(PS[:, 4 + t, c * P:(c + 1) * P],
                                               conv[:, c * T + t * P:c * T + (t + 1) * P], ident)
            last.then_inc(S.convT_done, 1)
            pe.wait_ge(S.yc_ready, 4)
            pe.wait_ge(S.cn_ready, 2)
            for c in range(4):
                for t in range(TT):
                    at = c % 2 * T + t * P
                    last = nc.tensor.transpose(PS[:, 6 + c // 2, at:at + P], tmp[:, t * 512 + c * P:t * 512 + (c + 1) * P],
                                               ident)
            last.then_inc(S.cnT_done, 1)
            def mixed_rows(js):
                for j in js:
                    pe.wait_ge(S.yf_ready, [1, 1, 1, 1, 2, 2, 3, 3][j])
                    rows_half(2 * FIRST["w_out"] + j, h_hi[:, j, :], h_lo[:, j, :], 0, j == 0, j == 7, 0, j == 7)

            mixed_rows(range(4))
            pe.wait_ge(S.yn_ready, 2)
            for c in range(4):
                for t in range(TT):
                    at = c % 2 * T + t * P
                    last = nc.tensor.transpose(PS[:, 4 + c // 2, at:at + P], Y[:, t, c * P:(c + 1) * P], ident)
                if c % 2:
                    last.then_inc(S.ynT_done, 1)
            mixed_rows(range(4, 8))

            norm(1, MEM)
            for n in range(4):
                if n == 0:
                    pe.wait_ge(S.hT_ready, 16)
                if n >= 2:
                    pe.wait_ge(S.kmT_ready, n - 1)
                feat_slot(2 * (FIRST["km"] + n), 4 + n % 2)
            pe.wait_ge(S.x_part, 4)
            rows_matrix("vm", 0)
            pe.wait_ge(S.kmT_ready, 4)
            norm(2)
            pe.wait_ge(S.vm_ready, 4)
            for n in range(4):
                feat_slot(2 * (FIRST["wq"] + n), n, 0, None if n else 2)
            pe.wait_ge(S.qT_ready, 4)
            attention(0, qT, kmT, vm, 2, 0, False)
            pe.wait_ge(S.o_ready, 4)
            rows_matrix("wo", 4, last_of_x=True)

            norm(3)
            ffn(0)
            norm(4)
            ffn(1)
            norm(5)
            rows_matrix("q", 0, normed=5)
            rows_matrix("k", 4)
            pe.wait_ge(S.qk_evac, 4)
            rows_matrix("v", 0)
            for q, src in enumerate((q_r, k_r)):
                pe.wait_ge(S.qk_roped, q + 1)
                if q:
                    pe.wait_ge(S.qkT_ready, 4)
                else:
                    pe.wait_ge(S.qk_evac, 8)
                s3 = src.rearrange("p (t d) -> p t d", t=TT)
                for h in range(8):
                    for t in range(TT):
                        at = h % 2 * T + t * P
                        last = nc.tensor.transpose(PS[:, 4 + h // 2, at:at + P], s3[:, t, h * P:(h + 1) * P], ident)
                last.then_inc(S.qkT_done, 1)
            pe.wait_ge(S.qkT_ready, 8)
            pe.wait_ge(S.v_ready, 4)
            pe.wait_ge(S.rounded_ready, 1)
            attention(1, qT, kT2, v2, 1, 0, True)
            pe.wait_ge(S.o_ready, 6)
            attention(2, qT, kT2, v2, 1, 4, True)
            pe.wait_ge(S.o_ready, 8)
            rows_matrix("attn_o", 4, last_of_x=True)
            norm(6)
            ffn(2)
            norm(7)
            ffn(3)

            norm(8)
            pe.wait_ge(S.hT_ready, 72)
            for t in range(TT):
                for c in range(KC):
                    ts = slice(t * P, (t + 1) * P)
                    mm(PS[:, 4 + t, 0:32], h_hi[:, c, ts].bitcast(F32), pc("w_dt", c * 32, 32), start=c == 0, stop=False)
                    last = mm(PS[:, 4 + t, 0:32], h_lo[:, c, ts].bitcast(F32), pc("w_dt", c * 32, 32), start=False,
                              stop=c == KC - 1)
            last.then_inc(S.dt_done, 1)
            for half in range(2):
                if half:
                    pe.wait_ge(S.z_ready2, 4)
                rows_matrix("z", 0, first=4 * half)
            pe.wait_ge(S.dta_ready, 1)
            for t in range(TT):
                mm(PS[:, 6, t * 32:(t + 1) * 32], cn("upper"), dta[:, t, :], start=True, stop=True)
            mm(PS[:, 6, 64:96], cn("ones"), dta[:, 0, :], start=True, stop=True).then_inc(S.acs_done, 1)
            pe.wait_ge(S.acs_ready, 1)
            for n in range(16):
                bank = [4, 5, 6, 7][n % 4]
                if n >= 4:
                    pe.wait_ge(S.conv4_ready, 2 * (n - 3))
                feat_slot(2 * (FIRST["xbc"] + n), bank)
            pe.wait_ge(S.z_ready2, 8)
            for n in range(10):
                if n < 4:
                    pe.wait_ge(S.xbc_ready, 32)
                else:
                    pe.wait_ge(S.sT_ready, n - 3)
                for q in range(4):
                    if n < 8:
                        src = xsT[:, n % 4 * 4 + q, n // 4 * P:(n // 4 + 1) * P]
                    else:
                        src = bcT[:, (n - 8) * 4 + q, 0:P]
                    last = nc.tensor.transpose(PS[:, n % 4, q * P:(q + 1) * P], src, ident)
                last.then_inc(S.sT_done, 1)
            pe.wait_ge(S.sT_ready, 10)
            pe.wait_ge(S.conv4_ready, 32)
            pe.wait_ge(S.dsplit_hi, 2)

            def front(n):
                g, t, b = n // 2, n % 2, n % 2
                if n >= 2:
                    pe.wait_ge(S.g_lt, n - 1)
                    pe.wait_ge(S.g_w, n - 1)
                mm(PS[:, b, :], ident_r, future_r.unsqueeze(1).broadcast_to([P, 4, P]), start=True, stop=False)
                for r in range(4):
                    h = 4 * g + r
                    for part in (dta_hi, dta_lo):
                        mm(PS[:, b, r * P:(r + 1) * P], part[:, t, h:h + 1].broadcast_to([P, P]), upper_r,
                           start=False, stop=r == 3 and part is dta_lo)
                mm(PS[:, 2 + b, 0:P], bcT[:, g, t * P:(t + 1) * P], bcT[:, 8 + g, t * P:(t + 1) * P],
                   start=True, stop=True).then_inc(S.g_cb, 1)

            def back(n):
                g, t, b = n // 2, n % 2, n % 2
                if t == 0:
                    pe.wait_ge(S.g_xdec, g + 1)
                    if g >= 1:
                        pe.wait_ge(S.g_stready, g)
                    mm(PS[:, 6, 0:256], Btok[:, g, :], xdec[:, g % 2, :], start=True, stop=True).then_inc(S.g_st, 1)
                else:
                    pe.wait_ge(S.g_stready, g + 1)
                    if g >= 1:
                        pe.wait_ge(S.g_sum, n - 1)
                    mm(PS[:, 7, 0:256], bcT[:, 8 + g, P:T], stT[:, g % 2, :], start=True, stop=True)
                pe.wait_ge(S.g_w, n + 1)
                pe.wait_ge(S.g_xdt, n + 1)
                if n >= 2:
                    pe.wait_ge(S.g_sum, n - 1)
                for r in range(4):
                    last = mm(PS[:, 4 + b, r * 64:(r + 1) * 64], Wd[:, b, r, :], xdt[:, b, r * 64:(r + 1) * 64],
                              start=True, stop=True)
                last.then_inc(S.g_y, 1)

            front(0)
            for n in range(2 * G):
                if n + 1 < 2 * G:
                    front(n + 1)
                back(n)
            def out_transposes(n):
                pe.wait_ge(S.ysn_ready, 2 * n + 2)
                for j in range(2):
                    for t in range(TT):
                        c = 2 * n + j
                        last = nc.tensor.transpose(PS[:, n % 4, j * T + t * P:j * T + (t + 1) * P],
                                                   y_s[:, t, c * P:(c + 1) * P], ident)
                last.then_inc(S.ysT_done, 1)

            for n in range(4):
                out_transposes(n)
            for n in range(8):
                pe.wait_ge(S.ysT_ready, 2 * n + 2)
                for j in range(2):
                    c = (2 * n + j) % KC
                    rows_half(2 * (FIRST["ssm_out"] + n) + j, h_hi[:, c, :], h_lo[:, c, :], 4, n == 0 and j == 0,
                              n == 7 and j == 1, 0, n == 7 and j == 1)
                if n < 4:
                    out_transposes(n + 4)
            norm(9)
            ffn(4)

        @block.scalar
        def _(act):
            A = nc.scalar.activation
            steps = [0]

            def step(ins):
                steps[0] += 1
                ins.then_inc(S.act_step, 1)
                act.wait_ge(S.act_step, steps[0])

            cursor = [0]

            def split(last, i=0):
                while cursor[0] <= min(last, 2 * NSLOTS - 1):
                    n = cursor[0]
                    if n % 2 == 0:
                        act.wait_ge(loaded[n // 2 % R], i * (16 * LOOP // 2 // R) + 16 * (n // 2 // R + 1))
                    if n >= H:
                        act.wait_ge(S.half_done, LOOP * i + n - H + 1)
                    A(w_hi[:, n % H, :], raw[:, n % (2 * R), :], ACT.Copy).then_inc(S.hi_ready, 1)
                    cursor[0] += 1

            def when_done(name, slot):
                split(2 * (FIRST[name] + slot) + 4)
                done(act, name, slot)

            def warm_sqrt():
                A(warm, warm, ACT.Sqrt)

            def stats(k, src=X, parts=0):
                for t in range(TT):
                    for h in range(2):
                        hs = slice(h * 512, (h + 1) * 512)
                        if parts:
                            act.wait_ge(S.x_part, 4 * (parts - 1) + 2 * t + h + 1)
                        A(xn[:, t, hs], src[:, t, hs], ACT.Square, accum_out=ssq[:, 2 * t + h:2 * t + h + 1])\
                            .then_inc(S.ssq_ready, 1)
                act.wait_ge(S.ms_ready, k + 1)
                A(std, ms, ACT.Sqrt).then_inc(S.std_ready, 1)

            def to_h(k):
                for c in range(KC):
                    act.wait_ge(S.xT_ready, 4 * k + c // 2 + 1)
                    A(h_hi[:, c, :], PS[:, 4 + c // 2, c % 2 * T:(c % 2 + 1) * T], ACT.Copy, scale=pc("gain", 8 * k + c))\
                        .then_inc(S.hT_hi, 1)

            def norm(k):
                stats(k, X, k - 1)
                to_h(k)

            def ysquare(k, bank):
                for t in range(TT):
                    for h in range(2):
                        A(xn[:, t, h * 512:(h + 1) * 512], PS[:, bank + 2 * t + h, :], ACT.Square,
                          accum_out=yssq[:, 2 * t + h:2 * t + h + 1]).then_inc(S.yssq_ready, 1)
                act.wait_ge(S.yms_ready, k + 1)
                A(ystd, yms, ACT.Sqrt).then_inc(S.ystd_ready, 1)

            def ffn(f):
                def silu(b, i=0, ii=0):
                    n = ffn_half(f, "G", b)
                    split(n + 4, i)
                    act.wait_ge(S.half_done, LOOP * i + n + 2)
                    if b >= 2:
                        act.wait_ge(S.act_ready, ii * 2 + (NB * f + b - 1))
                    A(sg[:, b % 2, :], PS[:, 4 + 2 * (b % 2), :], ACT.Silu).then_inc(S.silu_ready, 1)
                    split(n + 7, i)
                    act.wait_ge(S.g_mult, ii * 2 + (NB * f + b + 1))
                    A(g_hi[:, b % 2, :, :].rearrange("p j t -> p (j t)"), sg[:, b % 2, :], ACT.Copy).then_inc(S.g_hi_ready, 1)

                silu(0)
                silu(1)
                with act.Fori(0, (NB - 3) // 2) as i:
                    for b in (2, 3):
                        silu(b, i, i)
                cursor[0] += LOOP * ((NB - 3) // 2 - 1)
                silu(NB - 1)
                split(ffn_half(f, "D", NB - 1) + 1)
                warm_sqrt()
                split(ffn_half(f, "D", NB - 1) + 4)
                act.wait_ge(S.half_done, ffn_half(f, "D", NB - 1) + 2)

            def attention(a, scale, causal):
                def exps(h):
                    act.wait_ge(S.nmax_ready, 4 * a + h + 1)
                    for t in range(TT):
                        keys, s = (P if causal and t == 0 else T), 2 * h + t
                        last = A(prob[:, s, 0:keys], PS[:, h, t * T:t * T + keys], ACT.Exp, bias=nmax[:, s:s + 1],
                                 scale=scale, accum_out=psum_[:, s:s + 1])
                    last.then_inc(S.exp_ready, 1)

                for h in range(4):
                    exps(h)
                    if h % 2 == 0:
                        continue
                    act.wait_ge(S.probT_done, 4 * a + h)
                    act.wait_ge(S.probT_ready, 4 * a + h - 1)
                    parts = [(0, 0), (1, P)] if causal else [(0, 0), (1, 0)]
                    for m, t0 in parts:
                        last = A(probT[:, h - 1, m, t0:T], PS[:, 3 + h, m * T + t0:(m + 1) * T], ACT.Copy)
                    last.then_inc(S.probT_ready, 1)

            act.dma_start(ctab[:], consts).then_inc(S.consts_loaded, 16)
            act.dma_start(ptab[:], cols).then_inc(S.params_loaded, 16)
            act.dma_start(rtab[:], rows.broadcast_to([P, NR_])).then_inc(S.rows_loaded, 16)
            act.dma_start(pos_i[:], pos_in).then_inc(S.pos_loaded, 16)
            act.wait_ge(S.warm_ready, 1)
            warm_sqrt()
            act.wait_ge(S.x_loaded, 16)
            stats(0)
            split(1)
            act.wait_ge(S.params_loaded, 16)
            to_h(0)
            split(3)
            act.wait_ge(S.pad_ready, 1)
            for n in range(11):
                when_done("w_in", n)
                if n < 7:
                    if n >= 4:
                        act.wait_ge(S.q_mixed, n - 3)
                    A(pin[:, n % 4, :, 1:T + 1], PS[:, n % 4, :].rearrange("p (c t) -> p c t", c=2), ACT.Copy)\
                        .then_inc(S.pin_ready, 1)
                elif n < 9:
                    A(glu[:, (n - 7) * 512:(n - 6) * 512], PS[:, n % 4, :], ACT.Copy).then_inc(S.pin_ready, 1)
                else:
                    A(usig[:, (n - 9) * 512:(n - 8) * 512], PS[:, n % 4, :], ACT.Sigmoid).then_inc(S.pin_ready, 1)
                if n == 0:
                    act.wait_ge(S.q_mixed, 1)
                    A(Q[0:64, 12, :], Q[0:64, 12, :], ACT.Tanh).then_inc(S.lora_ready, 1)
                    A(Q[:, 13, :], Q[:, 13, :], ACT.Sigmoid).then_inc(S.lora_ready, 2)
                if n == 2:
                    act.wait_ge(S.q_mixed, 3)
                    for c in range(4):
                        last = A(kk[:, c * T:(c + 1) * T], Q[:, 4 + c, :], ACT.Copy, scale=pc("k_k", c))
                    last.then_inc(S.kkraw_ready, 1)
                    act.wait_ge(S.wa_done, 1)
                    for c in range(4):
                        A(decay[:, c * T:(c + 1) * T], PS[:, 4 + c // 2, c % 2 * T:(c % 2 + 1) * T], ACT.Sigmoid,
                          bias=pc("w0", c))
                    for c in range(4):
                        last = A(a_f[:, c * T:(c + 1) * T], PS[:, 6 + c // 2, c % 2 * T:(c % 2 + 1) * T], ACT.Sigmoid,
                                 bias=pc("a0", c))
                    last.then_inc(S.a_ready, 1)
                    act.wait_ge(S.a_ready, 1)
                    A(invP, decay, ACT.Exp, scale=DECAY).then_inc(S.decay_ready, 1)
                    act.wait_ge(S.decay_ready, 1)
                    A(decay, decay, ACT.Exp, scale=-DECAY).then_inc(S.decay_ready, 1)
                if n == 4:
                    act.wait_ge(S.g_done, 1)
                    A(g_f, PS[:, 6:8, :].rearrange("p a b -> p (a b)"), ACT.Copy).then_inc(S.g_ready, 1)
                if n == 5:
                    act.wait_ge(S.kkmax_ready, 1)
                    A(tmp, tmp, ACT.Ln).then_inc(S.kk_ln, 1)
                    act.wait_ge(S.kk_ln, 1)
                    A(tmp, tmp, ACT.Exp, scale=-0.5).then_inc(S.kk_rstd, 1)
            split(25)
            act.wait_ge(S.tok_done, 1)
            for i, (bank, dst, t) in enumerate(((0, V_t, 0), (1, V_t, 1), (2, K_t, 0), (3, K_t, 1), (6, B_t, 0), (7, B_t, 1))):
                if i % 2 == 0:
                    A(dst[:, t, :], PS[:, bank, :], ACT.Copy).then_inc(S.tok_ready, 1)
            act.wait_ge(S.ang_ready, 1)
            A(trig, trig, ACT.Sin).then_inc(S.trig_ready, 1)
            for lv in range(5):
                for t in range(TT):
                    act.wait_ge(S.invq_done, 2 * lv + t + 1)
                    A(Qis[t], PS[:, 3 * t, :], ACT.Copy).then_inc(S.invq_ready, 1)
            for g in range(NCK):
                t, cp = g // 2, 64 * (g % 2)
                act.wait_ge(S.ru_done, g + 1)
                A(RU[cp:cp + 64, :], PS[cp:cp + 64, 0, :], ACT.Copy).then_inc(S.ru_ready, 1)
                act.wait_ge(S.u_done, g + 1)
                A(U[cp:cp + 64, :], PS[cp:cp + 64, 1, :], ACT.Copy).then_inc(S.u_ready, 1)
                act.wait_ge(S.yc_done, g + 1)
                A(Y[cp:cp + 64, t, :], PS[cp:cp + 64, 2, :], ACT.Copy).then_inc(S.yc_ready, 1)
            act.wait_ge(S.cvar_ready, 1)
            A(cstd, cvar, ACT.Sqrt).then_inc(S.cstd_ready, 1)
            act.wait_ge(S.cnT_done, 1)
            for c in range(4):
                A(YF[:, c, :], PS[:, 6 + c // 2, c % 2 * T:(c % 2 + 1) * T], ACT.Silu, bias=pc("ln_b", c),
                  scale=pc("ln_g", c)).then_inc(S.convY_ready, 1)
            act.wait_ge(S.convY_ready, 4)
            A(h_hi[:, 0:4, :], YF[:, 0:4, :], ACT.Copy).then_inc(S.yf_hi, 1)
            act.wait_ge(S.ynvar_ready, 1)
            A(ynstd, ynvar, ACT.Sqrt).then_inc(S.ynstd_ready, 1)
            split(2 * FIRST["w_out"] + 5)
            for n in range(2):
                cs = slice(4 + 2 * n, 6 + 2 * n)
                act.wait_ge(S.yT_ready, n + 1)
                A(h_hi[:, cs, :], YF[:, cs, :], ACT.Copy).then_inc(S.yf_hi, 1)
            split(2 * FIRST["w_out"] + 7)
            act.wait_ge(S.mem_loaded, 16)
            act.wait_ge(S.yf_ready, 3)
            stats(1, MEM)
            warm_sqrt()
            when_done("w_out", 3)
            to_h(1)
            ysquare(0, 0)
            for n in range(4):
                when_done("km", n)
                A(kmT[:, 2 * n:2 * n + 2, :], PS[:, 4 + n % 2, :].rearrange("p (c t) -> p c t", c=2), ACT.Copy)\
                    .then_inc(S.kmT_ready, 1)
                if n == 0:
                    stats(2, X, 1)
            when_done("vm", 3)
            for b in range(4):
                A(vm[:, b // 2, b % 2 * 512:(b % 2 + 1) * 512], PS[:, b, :], ACT.Copy).then_inc(S.vm_ready, 1)
            to_h(2)
            for n in range(4):
                when_done("wq", n)
                A(qT[:, 2 * n:2 * n + 2, :], PS[:, n, :].rearrange("p (c t) -> p c t", c=2), ACT.Copy)\
                    .then_inc(S.qT_ready, 1)
            attention(0, 1.0 / 16, False)

            def outputs(a, first, banks):
                for n in range(banks):
                    act.wait_ge(S.o_done, [0, 4, 6][a] + n + 1)
                    A(h_hi[:, first + 2 * n:first + 2 * n + 2, :], PS[:, n, :].rearrange("p (c t) -> p c t", c=2),
                      ACT.Copy).then_inc(S.o_hi, 1)

            outputs(0, 0, 4)
            warm_sqrt()
            when_done("wo", 3)
            ysquare(1, 4)
            norm(3)
            ffn(0)
            ysquare(2, 0)
            norm(4)
            ffn(1)
            norm(5)
            for q, (dst, bank) in enumerate(((q_r, 0), (k_r, 4))):
                when_done("qk"[q], 3)
                for b in range(4):
                    A(dst[:, b * 512:(b + 1) * 512], PS[:, bank + b, :], ACT.Copy).then_inc(S.qk_evac, 1)
                act.wait_ge(S.qk_evac, 4 * (q + 1))
                A(rt1, dst, ACT.Square).then_inc(S.qk_sq, 1)
                act.wait_ge(S.qk_ms, q + 1)
                A(qkstd[:, q * 16:(q + 1) * 16], qkms[:, q * 16:(q + 1) * 16], ACT.Sqrt).then_inc(S.qk_std, 1)
            when_done("v", 3)
            for b in range(4):
                A(v2[:, b // 2, b % 2 * 512:(b % 2 + 1) * 512], PS[:, b, :], ACT.Copy).then_inc(S.v_ready, 1)
            split(2 * FIRST["attn_o"] + 3)
            for q, dst in enumerate((qT, kT2)):
                act.wait_ge(S.qkT_done, q + 1)
                for n in range(4):
                    A(dst[:, 2 * n:2 * n + 2, :], PS[:, 4 + n, :].rearrange("p (c t) -> p c t", c=2), ACT.Copy)\
                        .then_inc(S.qkT_ready, 1)
            for half in range(2):
                attention(1 + half, 128 ** -0.5, True)
                outputs(1 + half, 4 * half, 2)
            warm_sqrt()
            split(2 * FIRST["attn_o"] + 11)
            norm(6)
            ffn(2)
            norm(7)
            ffn(3)
            norm(8)
            act.wait_ge(S.dt_abs, 1)
            A(dte, dte, ACT.Exp, scale=-1.0).then_inc(S.dt_exp, 1)
            act.wait_ge(S.rows_loaded, 16)
            A(aexp, row("a_log"), ACT.Exp).then_inc(S.aneg, 1)
            act.wait_ge(S.dt_exp, 1)
            A(dte, dte, ACT.Ln, bias=1.0).then_inc(S.dt_ln, 1)
            for half in range(2):
                when_done("z", 4 * half + 3)
                for b in range(4):
                    at = half * 1024 + b % 2 * 512
                    A(z_s[:, b // 2, at:at + 512], PS[:, b, :], ACT.Silu).then_inc(S.z_ready2, 1)

            def conv_silu(c):
                act.wait_ge(S.conv4_ready, c + 1)
                dst = (xsT if c < 16 else bcT)[:, c % 16, :]
                A(dst, ctmp[:, c // 2 % 4, c % 2 * T:(c % 2 + 1) * T], ACT.Silu).then_inc(S.xbc_ready, 1)

            for n in range(16):
                when_done("xbc", n)
                if n >= 4:
                    act.wait_ge(S.xbc_ready, 2 * n - 6)
                for j in range(2):
                    c = 2 * n + j
                    A(ctmp[:, n % 4, j * T:(j + 1) * T], PS[:, 4 + n % 4, j * T:(j + 1) * T], ACT.Identity,
                      bias=pc("sconv_b", c), scale=pc("sconv_w", 3 * 32 + c)).then_inc(S.conv1_ready, 1)
                if n:
                    conv_silu(2 * n - 2)
                    conv_silu(2 * n - 1)
            conv_silu(30)
            conv_silu(31)
            act.wait_ge(S.acs_ready, 1)
            A(dec0, dec0, ACT.Exp).then_inc(S.decay2_done, 1)
            A(eacs, nacs[:, 32:64], ACT.Exp, scale=-1.0).then_inc(S.decay2_done, 1)
            for n in range(10):
                act.wait_ge(S.sT_done, n + 1)
                if n < 8:
                    dst = xtok[:, n // 4, n % 4 * 512:(n % 4 + 1) * 512]
                else:
                    dst = Btok[:, (n - 8) * 4:(n - 7) * 4, :].rearrange("p g n -> p (g n)")
                A(dst, PS[:, n % 4, :], ACT.Copy).then_inc(S.sT_ready, 1)
            def gated_square(n):
                g, t = n // 2, n % 2
                act.wait_ge(S.g_yev, n + 1)
                if n >= 1:
                    act.wait_ge(S.ys_sq, n)
                A(junk, y_s[:, t, g * 256:(g + 1) * 256], ACT.Square, accum_out=ysms[:, t * G + g:t * G + g + 1])\
                    .then_inc(S.ys_sq, 1)

            for n in range(2 * G):
                g, t, b = n // 2, n % 2, n % 2
                act.wait_ge(S.g_cb, n + 1)
                if n >= 2:
                    act.wait_ge(S.g_w, n - 1)
                for r in range(4):
                    h = 4 * g + r
                    last = A(LT[:, b, r, :], PS[:, b, r * P:(r + 1) * P], ACT.Exp,
                             bias=nacs[:, t * 32 + h:t * 32 + h + 1])
                last.then_inc(S.g_lt, 1)
                if t == 0:
                    act.wait_ge(S.g_st, g + 1)
                    if g >= 2:
                        act.wait_ge(S.g_y, n - 2)
                    A(stT[:, g % 2, :], PS[:, 6, 0:256], ACT.Copy).then_inc(S.g_stready, 1)
                if n >= 3:
                    gated_square(n - 3)
            warm_sqrt()
            for n in range(2 * G - 3, 2 * G):
                gated_square(n)
            act.wait_ge(S.ys_ms, 1)
            A(ysstd, ysms, ACT.Sqrt).then_inc(S.ys_std, 1)
            split(2 * FIRST["ssm_out"] + 3)
            for c in range(16):
                act.wait_ge(S.ysT_done, c // 2 + 1)
                if c >= KC:
                    split(2 * FIRST["ssm_out"] + c - KC + 4)
                    act.wait_ge(S.half_done, 2 * FIRST["ssm_out"] + c - KC + 1)
                A(h_hi[:, c % KC, :], PS[:, c // 2 % 4, c % 2 * T:(c % 2 + 1) * T], ACT.Copy,
                  scale=pc("ssm_norm", c)).then_inc(S.ysT_hi, 1)
            warm_sqrt()
            split(2 * FIRST["ssm_out"] + 18)
            norm(9)
            ffn(4)

        @block.vector
        def _(dve):
            v = nc.vector
            steps = [0]

            def step(ins):
                steps[0] += 1
                ins.then_inc(S.dve_step, 1)
                dve.wait_ge(S.dve_step, steps[0])

            cursor = [0]

            def split(last, i=0):
                while cursor[0] <= min(last, 2 * NSLOTS - 1):
                    n = cursor[0]
                    dve.wait_ge(S.hi_ready, LOOP * i + n + 1)
                    v.tensor_tensor(w_lo[:, n % H, :], raw[:, n % (2 * R), :], w_hi[:, n % H, :].bitcast(F32),
                                    ALU.subtract).then_inc(S.lo_ready, 1)
                    cursor[0] += 1

            def when_done(name, slot):
                split(2 * (FIRST[name] + slot) + 4)
                done(dve, name, slot)

            def stats(k, src=X, dst=xn):
                dve.wait_ge(S.ssq_ready, 4 * (k + 1))
                step(v.tensor_tensor(ms, ssq[:, 0:4:2], ssq[:, 1:4:2], ALU.add))
                v.tensor_scalar(ms, ms, 1.0 / D, 1e-6, ALU.mult, ALU.add).then_inc(S.ms_ready, 1)
                dve.wait_ge(S.std_ready, k + 1)
                step(v.reciprocal(rstd, std))
                for t in range(TT):
                    v.tensor_scalar(dst[:, t, :], src[:, t, :], rstd[:, t:t + 1], None, ALU.mult).then_inc(S.xn_ready, 1)

            def to_h(k):
                for c in range(KC):
                    dve.wait_ge(S.hT_hi, 8 * k + c // 2 * 2 + 2)
                    v.scalar_tensor_tensor(h_lo[:, c, :], PS[:, 4 + c // 2, c % 2 * T:(c % 2 + 1) * T],
                                           pc("gain", 8 * k + c), h_hi[:, c, :].bitcast(F32), ALU.mult, ALU.subtract)\
                        .then_inc(S.hT_ready, 1)

            def norm(k):
                stats(k)
                to_h(k)

            def ynorm(k, bank):
                dve.wait_ge(S.yssq_ready, 4 * (k + 1))
                step(v.tensor_tensor(yms, yssq[:, 0:4:2], yssq[:, 1:4:2], ALU.add))
                v.tensor_scalar(yms, yms, 1.0 / D, 1e-6, ALU.mult, ALU.add).then_inc(S.yms_ready, 1)
                dve.wait_ge(S.ystd_ready, k + 1)
                step(v.reciprocal(yrstd, ystd))
                dve.wait_ge(S.gain_loaded, 16 * (k + 1))
                parts = [(t, slice(h * 512, (h + 1) * 512), bank + 2 * t + h) for t in range(TT) for h in range(2)]

                def scaled(t, hs, b):
                    return v.scalar_tensor_tensor(xn[:, t, hs], PS[:, b, :], yrstd[:, t:t + 1], post_gain[:, hs],
                                                  ALU.mult, ALU.mult)

                step(scaled(*parts[0]))
                for n, (t, hs, b) in enumerate(parts):
                    if n < 3:
                        nxt = scaled(*parts[n + 1])
                        if n == 2:
                            nxt.then_inc(S.gain_read, 1)
                    v.tensor_tensor(X[:, t, hs], X[:, t, hs], xn[:, t, hs], ALU.add).then_inc(S.x_part, 1)
                    dve.wait_ge(S.x_part, 4 * k + n + 1)

            residuals = [0]

            def residual(bank, factor, name, slot):
                n = residuals[0]
                residuals[0] += 1
                first_of_n = [3, 4, 5, 6, 7, 8][n]
                split(2 * (FIRST[name] + slot) + 2)
                dve.wait_ge(S.y_first, first_of_n + 1)
                for t in range(TT):
                    if t:
                        done(dve, name, slot)
                    for h in range(2):
                        hs = slice(h * 512, (h + 1) * 512)
                        v.scalar_tensor_tensor(X[:, t, hs], PS[:, bank + 2 * t + h, :], factor, X[:, t, hs],
                                               ALU.mult, ALU.add).then_inc(S.x_part, 1)
                split(2 * (FIRST[name] + slot) + 4)

            def ffn(f):
                def hidden(b, i=0, ii=0):
                    n = ffn_half(f, "G", b)
                    split(n + 6, i)
                    dve.wait_ge(S.half_done, LOOP * i + n + 4)
                    dve.wait_ge(S.silu_ready, ii * 2 + (NB * f + b + 1))
                    v.tensor_tensor(sg[:, b % 2, :], sg[:, b % 2, :], PS[:, 5 + 2 * (b % 2), :], ALU.mult)\
                        .then_inc(S.g_mult, 1)
                    split(n + 7, i)
                    dve.wait_ge(S.g_hi_ready, ii * 2 + (NB * f + b + 1))
                    v.tensor_tensor(g_lo[:, b % 2, :, :].rearrange("p j t -> p (j t)"), sg[:, b % 2, :],
                                    g_hi[:, b % 2, :, :].rearrange("p j t -> p (j t)").bitcast(F32),
                                    ALU.subtract).then_inc(S.act_ready, 1)

                hidden(0)
                hidden(1)
                with dve.Fori(0, (NB - 3) // 2) as i:
                    for b in (2, 3):
                        hidden(b, i, i)
                cursor[0] += LOOP * ((NB - 3) // 2 - 1)
                hidden(NB - 1)

            def attention(a, scale, causal):
                def maxima(h):
                    dve.wait_ge(S.score_done, 4 * a + h + 1)
                    if causal:
                        v.tensor_reduce(nmax[:, 2 * h:2 * h + 1], PS[:, h, 0:P], AX.X, ALU.max)
                        step(v.tensor_reduce(nmax[:, 2 * h + 1:2 * h + 2], PS[:, h, T:2 * T], AX.X, ALU.max))
                    else:
                        step(v.tensor_reduce(nmax[:, 2 * h:2 * h + 2], PS[:, h, :].rearrange("p (t m) -> p t m", t=TT),
                                             AX.X, ALU.max))
                    v.tensor_scalar(nmax[:, 2 * h:2 * h + 2], nmax[:, 2 * h:2 * h + 2], -scale, None, ALU.mult)\
                        .then_inc(S.nmax_ready, 1)

                def normed(h):
                    dve.wait_ge(S.exp_ready, 4 * a + h + 1)
                    step(v.reciprocal(rsum[:, 2 * h:2 * h + 2], psum_[:, 2 * h:2 * h + 2]))
                    for t in range(TT):
                        keys, s = (P if causal and t == 0 else T), 2 * h + t
                        last = v.tensor_scalar(prob[:, s, 0:keys], prob[:, s, 0:keys], rsum[:, s:s + 1], None, ALU.mult)
                    last.then_inc(S.prob_ready, 1)

                def odd(h):
                    dve.wait_ge(S.probT_done, 4 * a + h + 1)
                    dve.wait_ge(S.probT_ready, 4 * a + h)
                    for m, t0 in ([(0, 0), (1, P)] if causal else [(0, 0), (1, 0)]):
                        last = v.tensor_copy(probT[:, h, m, t0:T], PS[:, 4 + h, m * T + t0:(m + 1) * T])
                    last.then_inc(S.probT_ready, 1)

                maxima(0)
                maxima(1)
                normed(0)
                maxima(2)
                normed(1)
                maxima(3)
                odd(1)
                normed(2)
                normed(3)
                odd(3)

            v.memset(warm, 1.0).then_inc(S.warm_ready, 1)
            stats(0)
            split(1)
            dve.wait_ge(S.params_loaded, 16)
            to_h(0)
            split(3)
            v.tensor_copy(ident_r, ident)
            v.tensor_copy(future_r, cn("future"))
            v.tensor_copy(upper_r, cn("upper")).then_inc(S.rounded_ready, 1)
            v.memset(pin_r[:, 0:2056].rearrange("p (c t) -> p c t", c=8)[:, :, 0:1], 0.0).then_inc(S.pad_ready, 1)
            def shift(n):
                split(2 * n + 4)
                dve.wait_ge(S.diff_ready, 1 + n)
                c = [12, 4, 6, 0, 2, 8, 10][n]
                for j in range(2):
                    last = v.scalar_tensor_tensor(Q[:, c + j, :], tshift[:, j * T:(j + 1) * T], pc("mu", c + j),
                                                  pin[:, n % 4, j, 1:T + 1], ALU.mult, ALU.add)
                last.then_inc(S.q_mixed, 1)
                dve.wait_ge(S.q_mixed, n + 1)

            def more():
                split(min(cursor[0], 21))

            c16 = lambda ap: ap.rearrange("p (s t) -> p s t", s=16)
            Pinc = Pc[:, :, 1:65]
            shift(0)
            step(v.memset(Pc[:, :, 0:1], 1.0))
            shift(1)
            shift(2)
            shift(3)
            dve.wait_ge(S.a_ready, 1)
            for c in range(4):
                last = v.tensor_scalar(tmpb[:, c * T:(c + 1) * T], a_f[:, c * T:(c + 1) * T], -1.0, pc("k_a", c),
                                       ALU.add, ALU.mult)
            step(last)
            step(v.scalar_tensor_tensor(k_f, tmpb, 1.0, k_f, ALU.add, ALU.mult))
            shift(4)
            for c in range(4):
                cs = slice(c * T, (c + 1) * T)
                last = v.scalar_tensor_tensor(tmpb[:, cs], r_f[:, cs], pc("r_k", c), k_f[:, cs], ALU.mult, ALU.mult)
            last.then_inc(S.bonus_in, 1)
            dve.wait_ge(S.decay_ready, 2)
            for q in range(16):
                last = v.tensor_tensor_scan(Pc[:, q, 1:65], decay[:, q * 64:(q + 1) * 64], cn("zeros"), 1.0,
                                            ALU.mult, ALU.add)
            last.then_inc(S.scan_done, 1)
            for q in range(16):
                qs = slice(q * 64, (q + 1) * 64)
                last = v.tensor_tensor_scan(invP[:, qs], invP[:, qs], cn("zeros"), 1.0, ALU.mult, ALU.add)
            step(last)
            dve.wait_ge(S.scan_done, 1)
            step(v.scalar_tensor_tensor(c16(newton), Pinc, -1.0, c16(invP), ALU.mult, ALU.mult))
            v.scalar_tensor_tensor(invP, newton, 2.0, invP, ALU.add, ALU.mult).then_inc(S.invP_ready, 1)
            dve.wait_ge(S.kksum_done, 1)
            v.tensor_scalar(tmp, PS[:, 4:6, :].rearrange("p a b -> p (a b)"), 1e-24, None, ALU.max)\
                .then_inc(S.kkmax_ready, 1)
            shift(5)
            dve.wait_ge(S.invP_ready, 1)
            dve.wait_ge(S.kkraw_ready, 1)
            dve.wait_ge(S.kk_rstd, 1)
            step(v.tensor_tensor(kk, kk, tmp, ALU.mult))
            shift(6)
            v.scalar_tensor_tensor(a_f, kk, -1.0, a_f, ALU.mult, ALU.mult).then_inc(S.kk_used, 1)
            dve.wait_ge(S.kk_used, 1)
            more()
            v.tensor_tensor(a_f, a_f, invP, ALU.mult).then_inc(S.ab_ready, 1)
            split(25)
            dve.wait_ge(S.bonus_sum_done, 1)
            v.tensor_tensor(bonus, PS[:, 4:6, :].rearrange("p a b -> p (a b)"), v_f, ALU.mult)
            dve.wait_ge(S.tok_done, 1)
            for i, (bank, dst, t) in enumerate(((0, V_t, 0), (1, V_t, 1), (2, K_t, 0), (3, K_t, 1), (6, B_t, 0), (7, B_t, 1))):
                if i % 2 == 1:
                    v.tensor_copy(dst[:, t, :], PS[:, bank, :]).then_inc(S.tok_ready, 1)

            dve.wait_ge(S.pos_loaded, 16)
            step(v.tensor_copy(posf, pos_i[:]))
            tr = trig.rearrange("p (s t f) -> p s t f", s=2, t=TT)
            for t in range(TT):
                for s in range(2):
                    last = v.tensor_scalar(tr[:, s, t, :], cn("inv_freq"), posf[:, t:t + 1], None, ALU.mult)
            step(last)
            magic = 12582912.0
            for s in range(2):
                last = v.tensor_scalar(turns[:, s * 128:(s + 1) * 128], trig[:, s * 128:(s + 1) * 128],
                                       1.0 / (2 * math.pi), 0.25 * s, ALU.mult, ALU.add)
            step(last)
            step(v.tensor_scalar(turns, turns, magic, None, ALU.add))
            step(v.tensor_scalar(turns, turns, magic, None, ALU.subtract))
            for part in (6.28125, 0.0019350051879882812, 3.019915981956753e-07):
                step(v.scalar_tensor_tensor(trig, turns, -part, trig, ALU.mult, ALU.add))
            step(v.tensor_scalar(trig[:, 128:256], trig[:, 128:256], math.pi / 2, None, ALU.add))
            v.tensor_scalar(trig, trig, 3.1415925, -3.1415925, ALU.min, ALU.max).then_inc(S.ang_ready, 1)

            h8 = lambda ap: ap.rearrange("p (h t) -> p h t", h=8)
            b8 = lambda m: m.unsqueeze(1).broadcast_to([P, 8, 64])
            taps = [(back, c) for back in range(31) for c in range(4)]

            def tap_steps(n):
                if len(taps) == 124:
                    dve.wait_ge(S.glu_ready, 1)
                for _ in range(min(n, len(taps))):
                    back, c = taps.pop(0)
                    cs = slice(c * T, (c + 1) * T)
                    weight = pc("conv_w", (30 - back) * 4 + c)
                    if back == 0:
                        last_ = v.tensor_scalar(conv[:, cs], glu[:, cs], weight, pc("conv_b", c), ALU.mult, ALU.add)
                    else:
                        late = conv[:, c * T + back:(c + 1) * T]
                        last_ = v.scalar_tensor_tensor(late, glu[:, c * T:(c + 1) * T - back], weight, late,
                                                       ALU.mult, ALU.add)
                    if c == 3 and taps:
                        step(last_)
                    elif not taps:
                        last_.then_inc(S.conv_ready, 1)

            for t in range(TT):
                MT, RKT, RBT, XiT, NL, Xi, Loff = MTs[t], RKTs[t], RBTs[t], XiTs[t], NLs[t], Xis[t], Loffs[t]
                dve.wait_ge(S.gram_done, t + 1)
                grams = lambda bank, at: PS[:, bank:bank + 2, at:at + 256].rearrange("p e (c t) -> p e c t", c=4)
                heads = lambda ap: ap.rearrange("p (c e t) -> p e c t", c=4, e=2)
                m24 = lambda m: m.unsqueeze(1).unsqueeze(1).broadcast_to([P, 2, 4, 64])
                v.tensor_copy(heads(NL), grams(0, 0))
                v.tensor_tensor(heads(XiT), grams(0, 256), m24(cn("off1T")), ALU.mult)
                v.tensor_tensor(heads(MT), grams(2, 0), m24(cn("s_lt_t")), ALU.mult)
                v.tensor_tensor(heads(RKT), grams(2, 256), m24(cn("s_le_t")), ALU.mult)
                v.tensor_tensor(heads(RBT), grams(6, 0), m24(cn("s_le_t")), ALU.mult).then_inc(S.gram_ready, 1)
                dve.wait_ge(S.gram_ready, t + 1)
                v.tensor_tensor(h8(XiT), h8(XiT), b8(cn("eye64")), ALU.add)
                step(v.tensor_tensor(h8(Xi), h8(NL), b8(cn("off", 0, 64)), ALU.mult))
                v.tensor_tensor(h8(Xi), h8(Xi), b8(cn("eye64")), ALU.add)
                v.tensor_tensor(h8(Loff), h8(NL), b8(cn("off", 64, 64)), ALU.mult).then_inc(S.inv_ready, 1)
            for lv in range(5):
                for t in range(TT):
                    XiT, NL, Xi, Loff = XiTs[t], NLs[t], Xis[t], Loffs[t]
                    b = 3 * t
                    dve.wait_ge(S.invx_done, 2 * lv + t + 1)
                    last = v.tensor_tensor(XiT, XiT, PS[:, b + 1, :], ALU.add)
                    if lv < 4:
                        v.tensor_tensor(Xi, Xi, PS[:, b + 2, :], ALU.add)
                        last = v.tensor_tensor(h8(Loff), h8(NL), b8(cn("off", (lv + 2) * 64, 64)), ALU.mult)
                    last.then_inc(S.inv_ready, 1)
                    tap_steps(8)
                    if lv == 0 and t == 0:
                        for c in range(4):
                            cs = slice(c * T, (c + 1) * T)
                            v.tensor_scalar(bonus[:, cs], bonus[:, cs], pc("lnx_b", c), None, ALU.add)
            for g in range(NCK - 1):
                dve.wait_ge(S.z_done, g + 1)
                for c in range(4):
                    last = v.scalar_tensor_tensor(Zn[:, g % 2, c, :], PS[:, 3, c * P:(c + 1) * P], Pc[:, c * 4 + g, 64:65],
                                                  cn("pair"), ALU.mult, ALU.mult)
                last.then_inc(S.z_ready, 1)
                tap_steps(12 if g < NCK - 2 else len(taps))
            y8 = lambda t: Y[:, t, :].rearrange("p (h d) -> p h d", h=8)
            b8h = lambda s_, t: s_[:, 8 * t:8 * t + 8].unsqueeze(2).broadcast_to([P, 8, 64])

            def head_stats(t):
                ts, sq = slice(8 * t, 8 * t + 8), sqr[:, t * 512:(t + 1) * 512].rearrange("p (h d) -> p h d", h=8)
                dve.wait_ge(S.yc_ready, 2 * t + 2)
                step(v.tensor_reduce(ymean[:, ts], y8(t), AX.X, ALU.add))
                step(v.tensor_scalar(ymean[:, ts], ymean[:, ts], 1.0 / 64, None, ALU.mult))
                step(v.tensor_tensor(y8(t), y8(t), b8h(ymean, t), ALU.subtract))
                step(v.tensor_tensor(sq, y8(t), y8(t), ALU.mult))
                step(v.tensor_reduce(ynvar[:, ts], sq, AX.X, ALU.add))

            head_stats(0)
            dve.wait_ge(S.convT_done, 1)
            for t in range(TT):
                last = v.bn_stats(bst[:, 6 * t:6 * t + 6], PS[:, 4 + t, :])
            step(last)
            for t in range(TT):
                last = v.bn_aggr(bag[:, 2 * t:2 * t + 2], bst[:, 6 * t:6 * t + 6])
            step(last)
            v.tensor_scalar(cvar, bag[:, 1:4:2], 1e-5, None, ALU.add).then_inc(S.cvar_ready, 1)
            dve.wait_ge(S.cstd_ready, 1)
            step(v.reciprocal(crstd, cstd))
            for t in range(TT):
                v.tensor_scalar(tmp[:, t * 512:(t + 1) * 512], PS[:, 4 + t, :], bag[:, 2 * t:2 * t + 1],
                                crstd[:, t:t + 1], ALU.subtract, ALU.mult).then_inc(S.cn_ready, 1)
            def yf_low(n):
                cs = [slice(0, 4), slice(4, 6), slice(6, 8)][n]
                dve.wait_ge(S.yf_hi, n + 1)
                v.tensor_tensor(h_lo[:, cs, :], YF[:, cs, :], h_hi[:, cs, :].bitcast(F32), ALU.subtract)\
                    .then_inc(S.yf_ready, 1)

            head_stats(1)
            v.tensor_scalar(ynvar, ynvar, 1.0 / 64, 64e-5, ALU.mult, ALU.add).then_inc(S.ynvar_ready, 1)
            yf_low(0)
            dve.wait_ge(S.ynstd_ready, 1)
            step(v.reciprocal(ynrstd, ynstd))
            for t in range(TT):
                v.tensor_tensor(y8(t), y8(t), b8h(ynrstd, t), ALU.mult).then_inc(S.yn_ready, 1)
            split(2 * FIRST["w_out"] + 5)
            for n in range(2):
                dve.wait_ge(S.ynT_done, n + 1)
                for c in (2 * n, 2 * n + 1):
                    last = v.scalar_tensor_tensor(YF[:, 4 + c, :], PS[:, 4 + n, c % 2 * T:(c % 2 + 1) * T], pc("lnx_g", c),
                                                  bonus[:, c * T:(c + 1) * T], ALU.mult, ALU.add)
                step(last)
                yt = YF[:, 4 + 2 * n:6 + 2 * n, :].rearrange("p c t -> p (c t)")
                v.tensor_tensor(yt, yt, g_f[:, n * 512:(n + 1) * 512], ALU.mult).then_inc(S.yT_ready, 1)
                dve.wait_ge(S.yT_ready, n + 1)
            yf_low(1)
            yf_low(2)
            split(2 * FIRST["w_out"] + 7)
            stats(1, MEM, MEM)
            when_done("w_out", 3)
            to_h(1)
            ynorm(0, 0)
            when_done("km", 0)
            stats(2)
            when_done("vm", 3)
            to_h(2)
            when_done("wq", 3)

            def outputs(a, first, banks):
                for n in range(banks):
                    dve.wait_ge(S.o_hi, [0, 4, 6][a] + n + 1)
                    cs = slice(first + 2 * n, first + 2 * n + 2)
                    v.tensor_tensor(h_lo[:, cs, :], PS[:, n, :].rearrange("p (c t) -> p c t", c=2),
                                    h_hi[:, cs, :].bitcast(F32), ALU.subtract).then_inc(S.o_ready, 1)

            attention(0, 1.0 / 16, False)
            outputs(0, 0, 4)
            when_done("wo", 3)
            ynorm(1, 4)
            norm(3)
            ffn(0)
            when_done("ffn0", 32)
            ynorm(2, 0)
            norm(4)
            ffn(1)
            residual(0, 0.5, "ffn1", 32)
            dve.wait_ge(S.rows_loaded, 16)
            norm(5)
            hd = lambda ap: ap.rearrange("p (s d) -> p s d", s=16)
            for q in range(2):
                when_done("qk"[q], 3)
                dve.wait_ge(S.qk_sq, q + 1)
                qs = slice(q * 16, (q + 1) * 16)
                step(v.tensor_reduce(qkms[:, qs], hd(rt1), AX.X, ALU.add))
                v.tensor_scalar(qkms[:, qs], qkms[:, qs], 1.0 / 128, 1e-6, ALU.mult, ALU.add).then_inc(S.qk_ms, 1)
            for q, (src, gain) in enumerate(((q_r, "q_gain"), (k_r, "k_gain"))):
                split(2 * FIRST["v"] + 3 + q)
                dve.wait_ge(S.qk_std, q + 1)
                qs = slice(q * 16, (q + 1) * 16)
                step(v.reciprocal(qkr[:, qs], qkstd[:, qs]))
                step(v.tensor_tensor(hd(src), hd(src), qkr[:, qs].unsqueeze(2).broadcast_to([P, 16, 128]), ALU.mult))
                v.tensor_tensor(hd(src), hd(src), row(gain).unsqueeze(1).broadcast_to([P, 16, 128]), ALU.mult)\
                    .then_inc(S.qk_normed, 1)
                dve.wait_ge(S.qk_normed, q + 1)
                s4 = src.rearrange("p (t h d) -> p t h d", t=TT, h=8)
                w1 = rt1.rearrange("p (t h d) -> p t h d", t=TT, h=8)
                for t in range(TT):
                    cos = tr[:, 1, t, :].unsqueeze(1).broadcast_to([P, 8, 64])
                    split(cursor[0] if cursor[0] < 2 * FIRST["attn_o"] + 4 else 0)
                    v.tensor_tensor(w1[:, t, :, 0:64], s4[:, t, :, 0:64], cos, ALU.mult)
                    last = v.tensor_tensor(w1[:, t, :, 64:128], s4[:, t, :, 64:128], cos, ALU.mult)
                step(last)
                dve.wait_ge(S.sin_ready, q + 1)
                hs_ = lambda ap, a: hd(ap)[:, :, a:a + 64]
                v.tensor_tensor(hs_(src, 0), hs_(rt1, 0), hs_(rt2, 0), ALU.subtract)
                v.tensor_tensor(hs_(src, 64), hs_(rt1, 64), hs_(rt2, 64), ALU.add).then_inc(S.qk_roped, 1)
            split(2 * FIRST["attn_o"] + 3)
            attention(1, 128 ** -0.5, True)
            outputs(1, 0, 2)
            attention(2, 128 ** -0.5, True)
            outputs(2, 4, 2)
            residual(4, 1.0, "attn_o", 3)
            norm(6)
            ffn(2)
            residual(0, 0.5, "ffn2", 32)
            norm(7)
            ffn(3)
            residual(0, 0.5, "ffn3", 32)
            norm(8)
            dve.wait_ge(S.dt_done, 1)
            for t in range(TT):
                last = v.tensor_tensor(dt_[:, t * 32:(t + 1) * 32], PS[:, 4 + t, 0:32], row("dt_bias"), ALU.add)
            step(last)
            step(v.tensor_scalar(dte, dt_, -1.0, None, ALU.mult))
            v.tensor_tensor(dte, dte, dt_, ALU.max).then_inc(S.dt_abs, 1)
            dve.wait_ge(S.dt_ln, 1)
            step(v.scalar_tensor_tensor(dt_, dt_, 0.0, dte, ALU.max, ALU.add))
            dve.wait_ge(S.aneg, 1)
            for t in range(TT):
                last = v.scalar_tensor_tensor(dta[:, t, :], dt_[:, t * 32:(t + 1) * 32], -1.0, aexp, ALU.mult, ALU.mult)
            last.then_inc(S.dta_ready, 1)
            when_done("z", 7)
            dve.wait_ge(S.acs_done, 1)
            step(v.tensor_scalar(nacs, PS[:, 6, 0:64], -1.0, None, ALU.mult))
            v.tensor_tensor(dec0, nacs[:, 0:32], PS[:, 6, 64:96], ALU.add).then_inc(S.acs_ready, 1)
            for c in range(32):
                if c % 2 == 0:
                    when_done("xbc", c // 2)
                dve.wait_ge(S.conv1_ready, c // 2 * 2 + 2)
                ps = PS[:, 4 + c // 2 % 4, c % 2 * T:(c % 2 + 1) * T]
                dst = ctmp[:, c // 2 % 4, c % 2 * T:(c % 2 + 1) * T]
                for back in (1, 2):
                    step(v.scalar_tensor_tensor(dst[:, back:T], ps[:, 0:T - back], pc("sconv_w", (3 - back) * 32 + c),
                                                dst[:, back:T], ALU.mult, ALU.add))
                v.scalar_tensor_tensor(dst[:, 3:T], ps[:, 0:T - 3], pc("sconv_w", c), dst[:, 3:T], ALU.mult,
                                       ALU.add).then_inc(S.conv4_ready, 1)
            dve.wait_ge(S.dta_ready, 1)
            v.tensor_copy(dta_hi, dta).then_inc(S.dsplit_hi, 1)
            dve.wait_ge(S.dsplit_hi, 1)
            v.tensor_tensor(dta_lo, dta, dta_hi.bitcast(F32), ALU.subtract).then_inc(S.dsplit_hi, 1)
            dve.wait_ge(S.sT_ready, 10)
            dve.wait_ge(S.decay2_done, 2)
            r4 = lambda ap: ap.rearrange("p (r d) -> p r d", r=4)
            b4 = lambda ap: ap.unsqueeze(2).broadcast_to([P, 4, 64])

            def finish(n):
                g, t, b = n // 2, n % 2, n % 2
                gs = slice(g * 256, (g + 1) * 256)
                y = y_s[:, t, gs]
                dve.wait_ge(S.g_y, n + 1)
                dve.wait_ge(S.g_dx, n + 1)
                last = v.tensor_tensor(y, dx[:, b, :], PS[:, 4 + b, 0:256], ALU.add)
                if t:
                    step(last)
                    step(v.tensor_tensor(r4(dx[:, b, :]), r4(PS[:, 7, 0:256]), b4(eacs[:, 4 * g:4 * g + 4]), ALU.mult))
                    last = v.tensor_tensor(y, y, dx[:, b, :], ALU.add)
                last.then_inc(S.g_sum, 1)

            for n in range(2 * G):
                b = n % 2
                if n >= 2:
                    dve.wait_ge(S.g_y, n - 1)
                dve.wait_ge(S.g_lt, n + 1)
                v.tensor_tensor(Wd[:, b, :, :], LT[:, b, :, :], PS[:, 2 + b, 0:P].unsqueeze(1).broadcast_to([P, 4, P]),
                                ALU.mult).then_inc(S.g_w, 1)
                if n >= 1:
                    finish(n - 1)
            finish(2 * G - 1)
            dve.wait_ge(S.ys_sq, 2 * G)
            v.tensor_scalar(ysms, ysms, 1.0 / 256, 1e-6, ALU.mult, ALU.add).then_inc(S.ys_ms, 1)
            dve.wait_ge(S.ys_std, 1)
            step(v.reciprocal(ysr, ysstd))
            for g in range(G):
                for t in range(TT):
                    y = y_s[:, t, g * 256:(g + 1) * 256]
                    v.tensor_scalar(y, y, ysr[:, t * G + g:t * G + g + 1], None, ALU.mult).then_inc(S.ysn_ready, 1)
            split(2 * FIRST["ssm_out"] + 3)
            for c in range(16):
                if c >= KC:
                    split(2 * FIRST["ssm_out"] + c - KC + 4)
                dve.wait_ge(S.ysT_hi, c // 2 * 2 + 2)
                v.scalar_tensor_tensor(h_lo[:, c % KC, :], PS[:, c // 2 % 4, c % 2 * T:(c % 2 + 1) * T],
                                       pc("ssm_norm", c), h_hi[:, c % KC, :].bitcast(F32), ALU.mult, ALU.subtract)\
                    .then_inc(S.ysT_ready, 1)
            residual(4, 1.0, "ssm_out", 7)
            norm(9)
            ffn(4)
            residual(0, 0.5, "ffn4", 32)


def constants():
    import numpy as np
    c = np.zeros((P, NC_), np.float32)

    def put(name, value):
        at, width = CAT[name]
        c[:, at:at + width] = np.asarray(value, np.float32).reshape(P, width)

    i, j = np.arange(P)[:, None], np.arange(P)[None, :]
    s, t = i % CK, np.arange(CK)[None, :]
    put("ident", i == j)
    put("pair", i // HD == j // HD)
    put("ones", np.ones((P, P)))
    put("upper", i <= j)
    put("future", np.where(j < i, -1e30, 0.0))
    q = np.arange(T)[None, :]
    put("causal", np.stack([np.where(q > i + P * tt, -1e30, 0.0) for tt in range(TT)], 1))
    put("s_lt_t", s < t)
    put("s_le_t", s <= t)
    put("eye64", s == t)

    def off(a, b, m):
        return (a > b) & (a // (2 * m) == b // (2 * m)) & (a // m != b // m)

    put("off1T", off(t, s, 1))
    put("off", np.stack([off(s, t, 2 ** lv) for lv in range(6)], 1))
    put("inv_freq", np.broadcast_to(np.float32(10000.0) ** (-np.arange(64, dtype=np.float32) / np.float32(64)), (P, 64)))
    return c


def kernel(**inputs):
    import numpy as np
    import concourse.bacc as bacc
    from concourse.bass_utils import run_bass_kernel_spmd

    a = {name: np.asarray(value) for name, value in inputs.items()}

    def feat(w):
        n = w.shape[1] // 256
        return w.reshape(KC, P, n, 2, P).transpose(2, 1, 3, 0, 4).reshape(n, P, 2048)

    def rows(w):
        n = w.shape[0] // 256
        return w.reshape(n, 2, P, 1024).transpose(0, 2, 1, 3).reshape(n, P, 2048)

    def ffn(gate, up, down):
        g, u, d = feat(gate), feat(up), rows(down)
        order = [g[0], u[0]]
        for b in range(1, NB):
            order += [g[b], u[b], d[b - 1]]
        return np.stack(order + [d[NB - 1]])

    wi = a["w_in_first"]
    w_in = np.concatenate([wi[:, D + 1536:], wi[:, D + 512:D + 1024], wi[:, D:D + 512], wi[:, D + 1024:D + 1536],
                           wi[:, :D]], 1)
    wkv, gu, qkv, win2 = a["wkv"][0], a["w_gu"][0], a["attn_w_qkv_2"][0], a["ssm_w_in_2"][0]

    def ffn2(which, i):
        return ffn(a[f"ffn{which}_w_gate_2"][i], a[f"ffn{which}_w_up_2"][i], a[f"ffn{which}_w_down_2"][i])

    parts = {"w_in": feat(w_in), "km": feat(wkv[:, :D]), "vm": rows(wkv[:, D:]), "w_out": rows(a["w_out"][0]),
             "wq": feat(a["wq"][0]), "wo": rows(a["wo"][0]), "ffn0": ffn(gu[:, :FF], gu[:, FF:], a["w_down"][0]),
             "ffn1": ffn2(1, 0), "q": rows(qkv[:, :D]), "k": rows(qkv[:, D:2 * D]), "v": rows(qkv[:, 2 * D:]),
             "attn_o": rows(a["attn_w_o_2"][0]), "ffn2": ffn2(2, 0), "ffn3": ffn2(1, 1),
             "z": np.concatenate([rows(win2[:, :1024]), rows(win2[:, 1024:2048])]),
             "xbc": feat(win2[:, 2048:6144]), "ssm_out": rows(a["ssm_w_out_2"][0]), "ffn4": ffn2(2, 1)}
    W = np.concatenate([parts[name] for name, _ in STREAM])
    assert W.shape == (NSLOTS, P, 2048)

    def col(w):
        return w.reshape(-1, P).T

    g = a["norm_gains"][0]
    f1, mx, f2 = a["ffn1_norm_2"], a["mix_norm_2"], a["ffn2_norm_2"]
    gains = [g[0], a["mem_norm_g"], g[2], g[4], f1[0], mx[0], f2[0], f1[1], mx[1], f2[1]]
    wa = np.concatenate([a["w_up"][0], a["a_up"][0]], 0)
    wdt = win2[:, 6144:].reshape(KC, P, 32).transpose(1, 0, 2).reshape(P, 256)
    values = {"gain": col(np.concatenate(gains)), "ssm_norm": col(a["ssm_norm_2"][0]), "mu": col(a["mu_first"]),
              "w0": col(a["w0"][0]), "a0": col(a["a0"][0]), "k_k": col(a["k_k"][0]), "k_a": col(a["k_a"][0]),
              "r_k": col(a["r_k"][0].reshape(-1)), "lnx_g": col(a["lnx_g"][0]), "lnx_b": col(a["lnx_b"][0]),
              "conv_w": col(a["conv_w"][0].reshape(-1)), "conv_b": col(a["conv_b"][0]), "ln_g": col(a["conv_ln_g"][0]),
              "ln_b": col(a["conv_ln_b"][0]), "sconv_w": col(a["ssm_conv_w_2"][0].reshape(-1)),
              "sconv_b": col(a["ssm_conv_b_2"][0]), "wa_up": wa, "g_up": a["g_up"][0], "w_dt": wdt}
    cols = np.ascontiguousarray(np.concatenate([values[n] for n, _ in PCOLS], 1))
    rvals = {"q_gain": a["attn_q_norm_2"][0], "k_gain": a["attn_k_norm_2"][0],
             "dt_bias": a["ssm_dt_bias_2"][0], "a_log": a["ssm_a_log_2"][0], "d_skip": a["ssm_d_2"][0]}
    rws = np.concatenate([rvals[n] for n, _ in PROWS])[None, :]
    arrays = {"W": W, "cols": cols, "rows": rws, "post_gains": np.ascontiguousarray(g[1::2]), "consts": constants(), "x": np.ascontiguousarray(a["x"][0]),
              "mem": np.ascontiguousarray(a["mem"][0]),
              "pos": np.ascontiguousarray(a["positions_2"][0].reshape(TT, P).T.astype(np.int32))}

    nc = bacc.Bacc("TRN2", target_bir_lowering=False, num_devices=1)
    ins = [nc.dram_tensor(n, v.shape, mybir.dt.from_np(v.dtype), kind="ExternalInput").ap() for n, v in arrays.items()]
    out = nc.dram_tensor("out", (T, D), F32, kind="ExternalOutput").ap()
    build_program(nc, *ins, out)
    r = run_bass_kernel_spmd(nc, [arrays], core_ids=[0])
    return r.results[0]["out"].reshape(1, T, D)
```
